# Optimizing a Trainium2 kernel written in Bass

```python
import jax, jax.numpy as jnp
from jax import lax
import numpy as np

D_MODEL = 1024
BATCH = 1
SEQ = 256
DEPTH = 1

CHUNK = 64
MIX_WIDTH = 2 * D_MODEL
SSM_WIDTH = D_MODEL
SSM_HEAD_DIM = 64
SSM_HEADS = SSM_WIDTH // SSM_HEAD_DIM
SSM_GROUPS = 2
SSM_STATE = 128
CONV_WIDTH = 4
CONV_DIM = SSM_WIDTH + 2 * SSM_GROUPS * SSM_STATE
LSTM_WIDTH = MIX_WIDTH - SSM_WIDTH
LSTM_HEAD_DIM = 128
LSTM_HEADS = LSTM_WIDTH // LSTM_HEAD_DIM
N_EXPERTS = 32
TOP_K = 4
D_FF = D_MODEL
SWIGLU_LIMIT = 7.0
SWIGLU_ALPHA = 1.702
MOE_BLOCK = 256
RMS_EPS = 1e-6
IN_SIZES = (SSM_WIDTH, CONV_DIM, SSM_HEADS,
            LSTM_WIDTH, LSTM_WIDTH, LSTM_WIDTH, LSTM_WIDTH, LSTM_HEADS, LSTM_HEADS)
IN_PROJ_DIM = SSM_WIDTH + CONV_DIM + SSM_HEADS + 4 * LSTM_WIDTH + 2 * LSTM_HEADS

kernel_name = 'hybrid_ssd_mlstm_moe_block'

def _rms_norm(x, w):
    xf = x.astype(jnp.float32)
    y = xf * lax.rsqrt(jnp.mean(xf * xf, axis=-1, keepdims=True) + RMS_EPS)
    return (y * w.astype(jnp.float32)).astype(x.dtype)

def _segsum(a):
    t = a.shape[-1]
    cs = jnp.cumsum(a, axis=-1)
    diff = cs[..., :, None] - cs[..., None, :]
    mask = jnp.tril(jnp.ones((t, t), dtype=bool))
    return jnp.where(mask, diff, -jnp.inf)

def _causal_conv(u, w, b):
    ch = u.shape[-1]
    y = lax.conv_general_dilated(u, w[:, None, :], window_strides=(1,),
                                 padding=[(w.shape[0] - 1, 0)],
                                 dimension_numbers=('NWC', 'WIO', 'NWC'),
                                 feature_group_count=ch)
    return y + b

def _ssd(xs, dt, a_neg, bm, cm):
    b, s, h, p = xs.shape
    g, n = bm.shape[2], bm.shape[3]
    e, c, l = h // g, s // CHUNK, CHUNK
    xd = (xs * dt[..., None]).reshape(b, c, l, g, e, p)
    a = jnp.transpose((dt * a_neg).reshape(b, c, l, g, e), (0, 3, 4, 1, 2))
    bc = bm.reshape(b, c, l, g, n)
    cc = cm.reshape(b, c, l, g, n)
    a_cs = jnp.cumsum(a, axis=-1)
    decay_in = jnp.exp(_segsum(a))
    cb = jnp.einsum('bclgn,bcsgn->bgcls', cc, bc)
    y_diag = jnp.einsum('bgecls,bcsgep->bclgep', cb[:, :, None] * decay_in, xd)
    decay_to_end = jnp.exp(a_cs[..., -1:] - a_cs)
    states = jnp.einsum('bcsgn,bgecs,bcsgep->bcgepn', bc, decay_to_end, xd)
    states = jnp.concatenate([jnp.zeros_like(states[:, :1]), states], axis=1)
    chunk_decay = jnp.exp(_segsum(jnp.pad(a_cs[..., -1], ((0, 0), (0, 0), (0, 0), (1, 0)))))
    states = jnp.einsum('bgezc,bcgepn->bzgepn', chunk_decay, states)[:, :-1]
    y_off = jnp.einsum('bclgn,bcgepn,bgecl->bclgep', cc, states, jnp.exp(a_cs))
    return (y_diag + y_off).reshape(b, s, h, p)

def _mlstm(q, k, v, i_pre, f_pre):
    b, s, h, dh = q.shape
    c, l = s // CHUNK, CHUNK
    q = q.reshape(b, c, l, h, dh)
    k = k.reshape(b, c, l, h, dh) * (dh ** -0.5)
    v = v.reshape(b, c, l, h, dh)
    log_f = jnp.transpose(jax.nn.log_sigmoid(f_pre).reshape(b, c, l, h), (0, 3, 1, 2))
    log_i = jnp.transpose(i_pre.reshape(b, c, l, h), (0, 3, 1, 2))
    cum_f = jnp.cumsum(log_f, axis=-1)
    chunk_f = cum_f[..., -1]
    a_end = chunk_f[..., None] - cum_f + log_i
    m_loc = jnp.max(a_end, axis=-1)
    w_end = jnp.exp(a_end - m_loc[..., None])
    c_loc = jnp.einsum('bhcl,bclhk,bclhv->bhckv', w_end, k, v)
    n_loc = jnp.einsum('bhcl,bclhk->bhck', w_end, k)

    def step(carry, inp):
        c_st, n_st, m_st = carry
        f_c, m_c, c_c, n_c = inp
        m_new = jnp.maximum(f_c + m_st, m_c)
        s_old = jnp.exp(f_c + m_st - m_new)
        s_new = jnp.exp(m_c - m_new)
        c_next = s_old[..., None, None] * c_st + s_new[..., None, None] * c_c
        n_next = s_old[..., None] * n_st + s_new[..., None] * n_c
        return (c_next, n_next, m_new), (c_st, n_st, m_st)

    init = (jnp.zeros((b, h, dh, dh), q.dtype), jnp.zeros((b, h, dh), q.dtype),
            jnp.zeros((b, h), q.dtype))
    _, (c_prev, n_prev, m_prev) = lax.scan(
        step, init, (jnp.moveaxis(chunk_f, 2, 0), jnp.moveaxis(m_loc, 2, 0),
                     jnp.moveaxis(c_loc, 2, 0), jnp.moveaxis(n_loc, 2, 0)))
    c_prev = jnp.moveaxis(c_prev, 0, 2)
    n_prev = jnp.moveaxis(n_prev, 0, 2)
    m_prev = jnp.moveaxis(m_prev, 0, 2)
    causal = jnp.tril(jnp.ones((l, l), dtype=bool))
    log_d = jnp.where(causal, cum_f[..., :, None] - cum_f[..., None, :] + log_i[..., None, :],
                      -jnp.inf)
    log_inter = cum_f + m_prev[..., None]
    m_row = jnp.maximum(log_inter, jnp.max(log_d, axis=-1))
    sc = jnp.einsum('bclhk,bcjhk->bhclj', q, k) * jnp.exp(log_d - m_row[..., None])
    w_inter = jnp.exp(log_inter - m_row)
    num = (jnp.einsum('bhclj,bcjhv->bclhv', sc, v)
           + jnp.einsum('bclhk,bhckv->bclhv', q, c_prev) * jnp.transpose(w_inter, (0, 2, 3, 1))[..., None])
    den = jnp.sum(sc, axis=-1) + jnp.einsum('bclhk,bhck->bhcl', q, n_prev) * w_inter
    den = jnp.maximum(jnp.abs(den), jnp.exp(-m_row))
    hout = num / jnp.transpose(den, (0, 2, 3, 1))[..., None]
    return hout.reshape(b, s, h, dh)

def _moe(xn, w_router, b_router, w_gu, b_gu, w_dn, b_dn):
    bsz, s, d = xn.shape
    t = bsz * s
    xf = xn.reshape(t, d)
    logits = (xf @ w_router + b_router).astype(jnp.float32)
    top_val, top_idx = lax.top_k(logits, TOP_K)
    gates = jax.nn.softmax(top_val, axis=-1)
    n_assign = t * TOP_K
    n_blocks = -(-n_assign // MOE_BLOCK) + N_EXPERTS
    n_rows = n_blocks * MOE_BLOCK
    flat_e = top_idx.reshape(n_assign)
    flat_tok = jnp.arange(n_assign, dtype=jnp.int32) // TOP_K
    flat_gate = gates.reshape(n_assign)
    order = jnp.argsort(flat_e)
    sorted_e = flat_e[order]
    counts = jnp.bincount(flat_e, length=N_EXPERTS)
    starts = jnp.cumsum(counts) - counts
    padded = (counts + MOE_BLOCK - 1) // MOE_BLOCK * MOE_BLOCK
    padded_ends = jnp.cumsum(padded)
    padded_starts = padded_ends - padded
    dest = padded_starts[sorted_e] + jnp.arange(n_assign, dtype=jnp.int32) - starts[sorted_e]
    row_tok = jnp.zeros((n_rows,), jnp.int32).at[dest].set(flat_tok[order])
    row_gate = jnp.zeros((n_rows,), jnp.float32).at[dest].set(flat_gate[order])
    block_expert = jnp.minimum(
        jnp.searchsorted(padded_ends, jnp.arange(n_blocks, dtype=jnp.int32) * MOE_BLOCK, side='right'),
        N_EXPERTS - 1).astype(jnp.int32)

    def expert_block(args):
        tok, gate, e = args
        xb = xf[tok]
        hh = xb @ w_gu[e] + b_gu[e]
        g_h = jnp.minimum(hh[:, :D_FF], SWIGLU_LIMIT)
        u_h = jnp.clip(hh[:, D_FF:], -SWIGLU_LIMIT, SWIGLU_LIMIT)
        act = (u_h + 1.0) * (g_h * jax.nn.sigmoid(SWIGLU_ALPHA * g_h))
        out = act @ w_dn[e] + b_dn[e]
        return out * gate.astype(out.dtype)[:, None]

    outs = lax.map(expert_block, (row_tok.reshape(n_blocks, MOE_BLOCK),
                                  row_gate.reshape(n_blocks, MOE_BLOCK), block_expert))
    y = jax.ops.segment_sum(outs.reshape(n_rows, d), row_tok, num_segments=t)
    return y.reshape(bsz, s, d).astype(xn.dtype)

def setup_inputs(seed: int = 0) -> dict:
    key = jax.random.key(seed)
    ks = jax.random.split(key, 24)
    f32 = jnp.float32
    nrm = lambda k, shape, scale: jax.random.normal(k, shape, f32) * scale
    dt0 = jnp.exp(jax.random.uniform(ks[5], (DEPTH, SSM_HEADS), f32, np.log(1e-3), np.log(1e-1)))
    return {
        'x': jax.random.normal(ks[0], (BATCH, SEQ, D_MODEL), f32),
        'norm_mix_w': 1.0 + nrm(ks[1], (DEPTH, D_MODEL), 0.02),
        'w_in': nrm(ks[2], (DEPTH, D_MODEL, IN_PROJ_DIM), D_MODEL ** -0.5),
        'conv_w': nrm(ks[3], (DEPTH, CONV_WIDTH, CONV_DIM), CONV_WIDTH ** -0.5),
        'conv_b': nrm(ks[4], (DEPTH, CONV_DIM), 0.02),
        'dt_bias': dt0 + jnp.log(-jnp.expm1(-dt0)),
        'a_log': jnp.log(jax.random.uniform(ks[6], (DEPTH, SSM_HEADS), f32, 1.0, 16.0)),
        'd_skip': 1.0 + nrm(ks[7], (DEPTH, SSM_HEADS), 0.1),
        'ssm_norm_w': 1.0 + nrm(ks[8], (DEPTH, SSM_WIDTH), 0.02),
        'lstm_i_bias': nrm(ks[9], (DEPTH, LSTM_HEADS), 0.1),
        'lstm_f_bias': 3.0 + 3.0 * jax.random.uniform(ks[10], (DEPTH, LSTM_HEADS), f32),
        'lstm_norm_w': 1.0 + nrm(ks[11], (DEPTH, LSTM_WIDTH), 0.02),
        'w_out': nrm(ks[12], (DEPTH, MIX_WIDTH, D_MODEL), MIX_WIDTH ** -0.5),
        'norm_ffn_w': 1.0 + nrm(ks[13], (DEPTH, D_MODEL), 0.02),
        'w_router': nrm(ks[14], (DEPTH, D_MODEL, N_EXPERTS), D_MODEL ** -0.5),
        'b_router': nrm(ks[15], (DEPTH, N_EXPERTS), 0.01),
        'w_gate_up': nrm(ks[16], (DEPTH, N_EXPERTS, D_MODEL, 2 * D_FF), D_MODEL ** -0.5),
        'b_gate_up': nrm(ks[17], (DEPTH, N_EXPERTS, 2 * D_FF), 0.02),
        'w_down': nrm(ks[18], (DEPTH, N_EXPERTS, D_FF, D_MODEL), D_FF ** -0.5),
        'b_down': nrm(ks[19], (DEPTH, N_EXPERTS, D_MODEL), 0.02),
        'norm_final_w': 1.0 + nrm(ks[20], (D_MODEL,), 0.02),
    }

def reference(x, norm_mix_w, w_in, conv_w, conv_b, dt_bias, a_log, d_skip, ssm_norm_w,
              lstm_i_bias, lstm_f_bias, lstm_norm_w, w_out, norm_ffn_w, w_router, b_router,
              w_gate_up, b_gate_up, w_down, b_down, norm_final_w):
    f32 = jnp.float32
    b, s = x.shape[0], x.shape[1]
    splits = np.cumsum(IN_SIZES)[:-1].tolist()
    for layer in range(DEPTH):
        xn = _rms_norm(x, norm_mix_w[layer])
        proj = (xn @ w_in[layer]).astype(f32)
        z, xbc, dt_raw, q, k, v, o_pre, i_pre, f_pre = jnp.split(proj, splits, axis=-1)
        xbc = jax.nn.silu(_causal_conv(xbc, conv_w[layer].astype(f32), conv_b[layer].astype(f32)))
        xs, bm, cm = jnp.split(xbc, [SSM_WIDTH, SSM_WIDTH + SSM_GROUPS * SSM_STATE], axis=-1)
        xs = xs.reshape(b, s, SSM_HEADS, SSM_HEAD_DIM)
        bm = bm.reshape(b, s, SSM_GROUPS, SSM_STATE)
        cm = cm.reshape(b, s, SSM_GROUPS, SSM_STATE)
        dt = jax.nn.softplus(dt_raw + dt_bias[layer].astype(f32))
        a_neg = -jnp.exp(a_log[layer].astype(f32))
        y_ssm = _ssd(xs, dt, a_neg, bm, cm) + d_skip[layer].astype(f32)[:, None] * xs
        y_ssm = _rms_norm(y_ssm.reshape(b, s, SSM_WIDTH) * jax.nn.silu(z), ssm_norm_w[layer])
        h_l = _mlstm(q.reshape(b, s, LSTM_HEADS, LSTM_HEAD_DIM),
                     k.reshape(b, s, LSTM_HEADS, LSTM_HEAD_DIM),
                     v.reshape(b, s, LSTM_HEADS, LSTM_HEAD_DIM),
                     i_pre + lstm_i_bias[layer].astype(f32),
                     f_pre + lstm_f_bias[layer].astype(f32))
        h_l = _rms_norm(h_l, lstm_norm_w[layer].reshape(LSTM_HEADS, LSTM_HEAD_DIM))
        y_lstm = jax.nn.sigmoid(o_pre) * h_l.reshape(b, s, LSTM_WIDTH)
        mixed = jnp.concatenate([y_ssm, y_lstm], axis=-1).astype(x.dtype)
        x = x + mixed @ w_out[layer]
        x = x + _moe(_rms_norm(x, norm_ffn_w[layer]), w_router[layer], b_router[layer],
                     w_gate_up[layer], b_gate_up[layer], w_down[layer], b_down[layer])
    return _rms_norm(x, norm_final_w)


_drawn_inputs = setup_inputs


def setup_inputs(seed=0):
    import zlib

    import numpy as np

    out = dict(_drawn_inputs(seed))
    spreads = {}
    factors = {'lstm_i_bias': 200.0,
     'lstm_norm_w': 12.381,
     'b_gate_up': 6.328,
     'b_down': 7.316,
     'norm_final_w': 25.809,
     'ssm_norm_w': 3.097,
     'b_router': 8.851,
     'norm_ffn_w': 3.155}
    for name, (base, spread) in spreads.items():
        noise = np.random.default_rng([zlib.crc32(name.encode()), seed]).standard_normal(out[name].shape)
        drawn = base * np.exp(spread * noise) if base else spread * noise
        out[name] = __import__('jax').numpy.asarray(drawn.astype(out[name].dtype))
    for name, factor in factors.items():
        out[name] = (out[name] * factor).astype(out[name].dtype)
    return out
```

```python
import concourse.bass as bass
from concourse import mybir
from contextlib import ExitStack

P = 128
D = 1024
T = 256
TT = T // P
KT = D // P
H_SSM, HD_SSM = 16, 64
H_LSTM, HD_LSTM = 8, 128
W_SSM = H_SSM * HD_SSM
CONV_DIM = 1536
CONV_W = 4
NCH = CONV_DIM // P
XT_TILES = W_SSM // P
IN_DIM = 6688
COL_Z, COL_XBC, COL_DT = 0, 1024, 2560
COL_Q, COL_K, COL_V, COL_O, COL_I = 2576, 3600, 4624, 5648, 6672
NE = 32
TOPK = 4
FF = 1024
LIMIT, ALPHA = 7.0, 1.702
EPS = 1e-6
SL = 64
NBLK = T // SL
NV = NE * NBLK
MAXOVER = 16

SLOTS = 6
SLOTW = 4096
CW = SLOTW // KT
IN_COLS = ([COL_XBC + CW * i for i in range(3)] + [c + CW * i for c in (COL_Q, COL_K, COL_V, COL_Z, COL_O)
                                                   for i in range(2)])
N_IN = len(IN_COLS)
N_OUT = 4
N_MIX = N_IN + N_OUT
CPE = 6
RSQRT_D = 1.0 / D
QK_SCALE = float(HD_LSTM) ** -0.5
BIG = 1e30


def hybrid_block(nc, x_d, norm_mix_w, w_in, conv_w, conv_b, dt_bias, a_log, d_skip, ssm_norm_w,
                 lstm_i_bias, lstm_f_bias, lstm_norm_w, w_out, norm_ffn_w, w_router, b_router,
                 w_gate_up, b_gate_up, w_down, b_down, norm_final_w, out_d):
    f32, bf16, i32, u32 = mybir.dt.float32, mybir.dt.bfloat16, mybir.dt.int32, mybir.dt.uint32
    ALU, ACT, AX = mybir.AluOpType, mybir.ActivationFunctionType, mybir.AxisListType
    V, S, G, E = nc.vector, nc.scalar, nc.gpsimd, nc.tensor
    ctx = ExitStack()
    with ctx:
        def sb(name, shape, dt=f32):
            return ctx.enter_context(nc.sbuf_tensor(name, shape, dt))

        def sem(name):
            return ctx.enter_context(nc.semaphore(name))

        ring = sb("ring", [P, SLOTS, SLOTW])
        x = sb("x", [P, TT, D])
        xnT = sb("xnT", [P, KT, T])
        hn = xnT[:, :, :].rearrange("p a b -> p (a b)").rearrange("p (t d) -> p t d", t=TT)
        conv = sb("conv", [P, NCH, T])
        convf = conv[:, :, :].rearrange("p a b -> p (a b)")
        hl = convf[:, 0:TT * D].rearrange("p (t h d) -> p t h d", t=TT, h=H_LSTM)
        yssm = sb("yssm", [P, TT, D])
        xh = yssm
        hT = yssm[:, :, :].rearrange("p a b -> p (a b)").rearrange("p (j t) -> p j t", j=KT)
        xd = sb("xd", [P, TT, D])
        mixA = xd[:, :, :].rearrange("p a b -> p (a b)").rearrange("p (j t) -> p j t", j=KT)
        qT = sb("qT", [P, KT, T])
        mixB = qT
        wfin = qT[:, :, :].rearrange("p a b -> p (a b)")[:, 0:D]
        kT = sb("kT", [P, KT, T])
        og = kT[:, :, :].rearrange("p a b -> p (a b)").rearrange("p (t d) -> p t d", t=TT)
        VW = HD_LSTM + 1
        vz = sb("vz", [P, TT * H_LSTM * VW + TT * D])
        v1 = vz[:, 0:TT * H_LSTM * VW].rearrange("p (t h d) -> p t h d", t=TT, h=H_LSTM)
        z = vz[:, TT * H_LSTM * VW:].rearrange("p (t d) -> p t d", t=TT)
        biases = vz[:, 0:3 * FF]
        raw = sb("raw", [P, 3, CONV_W - 1 + T])
        csig = sb("csig", [P, 2, T])
        cbm = sb("cbm", [P, 2, 3 * P])
        dec = sb("dec", [P, 3, 3 * P])
        au = sb("au", [P, 2, 4, TT, P])
        auf = au[:, :, :, :, :].rearrange("p a b c d -> p (a b c d)")
        scr = auf.rearrange("p (t d) -> p t d", t=TT)
        small = sb("small", [P, KT, 32])
        wr = sb("wr", [P, KT, NE])
        nmw = sb("nmw", [P, KT])
        nfw = sb("nfw", [P, KT])
        NVEC = CONV_W * NCH + NCH + 8 + 8
        vecs = sb("vecs", [NVEC, P])
        vecT = sb("vecT", [P, NVEC])
        OFF_CB, OFF_SN, OFF_LN = CONV_W * NCH, CONV_W * NCH + NCH, CONV_W * NCH + NCH + 8
        dtb = sb("dtb", [P, H_SSM])
        alog = sb("alog", [P, H_SSM])
        dsk = sb("dsk", [P, H_SSM])
        br = sb("br", [P, NE])
        ifb = sb("ifb", [H_LSTM, 2])
        ident = sb("ident", [P, P])
        identb = sb("identb", [P, P], bf16)
        negm = sb("negm", [P, P], bf16)
        tri_le = sb("tri_le", [P, P])
        tri_gt = sb("tri_gt", [P, P])
        tri_lt = sb("tri_lt", [P, P])
        ones = sb("ones", [P, P])
        selh = sb("selh", [H_LSTM, H_LSTM, P])
        selall = sb("selall", [P, NBLK, NE])
        islot = sb("islot", [P, 2, SL])
        ie = sb("ie", [P, NE])
        ipart = sb("ipart", [P, 1])
        vmod = sb("vmod", [P, 1])
        thr = sb("thr", [P, 1])
        epst = sb("epst", [P, 1])
        st = sb("st", [P, 64])
        dsp = sb("dsp", [P, 7, 32])
        fsp = qT[:, :, :].rearrange("p a b -> p (a b)")[0:H_LSTM, 0:7 * T].rearrange("h (r t) -> h r t", r=7)
        dtt = sb("dtt", [P, TT, H_SSM])
        at = sb("at", [P, TT, H_SSM])
        r0 = sb("r0", [P, H_SSM])
        gates = kT[:, :, :].rearrange("p a b -> p (a b)")[0:H_LSTM, 0:7 * T].rearrange("h (r t) -> h r t", r=7)
        negG = sb("negG", [H_LSTM, T])
        agT = sb("agT", [P, 2, TT, H_LSTM])
        den = sb("den", [P, 2, TT, 2])
        XT = convf[:, 0:512]
        act = convf[:, 512:1024]
        gmin = convf[:, 1024:1536]
        sig = convf[:, 1536:2048]
        actT = convf[:, 2048:2560]
        outS = convf[:, 2560:3072]
        ucl = raw[:, :, :].rearrange("p a b -> p (a b)")[:, 0:512]
        gsg = csig[:, :, :].rearrange("p a b -> p (a b)")
        decf = dec[:, :, :].rearrange("p a b -> p (a b)")
        Pm = decf[:, 0:TT * SL].rearrange("p (t s) -> p t s", t=TT)
        Pg = decf[:, 128:128 + TT * 2 * SL].rearrange("p (t s) -> p t s", t=TT)
        PTg = decf[:, 384:384 + TT * P].rearrange("p (t s) -> p t s", t=TT)
        sel = decf[:, 640:640 + SL]
        posm, gall, mall = (auf[:, n * TT * NV:(n + 1) * TT * NV].rearrange("p (t v) -> p t v", t=TT) for n in range(3))
        lg = sb("lg", [P, TT, NE])
        top = sb("top", [P, TT, 8])
        tidx = sb("tidx", [P, TT, 8], u32)
        tidf = sb("tidf", [P, TT, 8])
        sm = sb("sm", [P, TT, 8])
        eq, eqg = (auf[:, 768 + n * TOPK * NE:768 + (n + 1) * TOPK * NE].rearrange("p (k e) -> p k e", k=TOPK)
                   for n in range(2))
        flag = sb("flag", [P, 4])
        oh = sb("oh", [P, MAXOVER])
        tabf = sb("tabf", [1, 2 * MAXOVER + 1])
        tab = sb("tab", [1, 2 * MAXOVER + 1], i32)

        B = [ctx.enter_context(nc.psum_tensor(f"bank{i}", [P, 512], f32)) for i in range(8)]
        ybank = [[B[0], B[1]], [B[2], B[3]]]
        hg, hu, outb, xb = B[4], B[5], B[6], B[7]

        s_x = [sem(f"x_loaded{t}") for t in range(TT)]
        s_small, s_nmw, s_vec, s_par = sem("small_loaded"), sem("norm_mix_loaded"), sem("vecs_loaded"), sem("params_loaded")
        s_bias, s_wfin, s_out = sem("biases_loaded"), sem("final_weight_loaded"), sem("output_stored")
        full = [sem(f"slot_full{i}") for i in range(SLOTS)]
        used = sem("chunks_used")
        c_pool, c_consts, c_raw0 = sem("pool_chain"), sem("consts_ready"), sem("pads_zero")
        s_ssq, s_rms, s_xh, s_xT, s_xnv, s_xna = (sem(n) for n in (
            "x_squares", "x_rms", "xh_ready", "xT_psum", "xnT_by_dve", "xnT_by_act"))
        s_vps, s_vecT = sem("vecs_psum"), sem("vecT_ready")
        s_sml, s_spin, s_spln, s_expa, s_at, s_gh, s_em, s_gtp, s_gte, s_au = (sem(n) for n in (
            "small_projected", "softplus_in", "softplus_ln", "exp_a_log", "a_ready", "gates_by_head",
            "exp_neg_m", "gates_psum", "gates_by_token", "au_ready"))
        s_pj, s_pe, s_cv, s_cs, s_cd = (sem(n) for n in (
            "proj_psum", "proj_evicted", "conv_sum", "conv_sigmoid", "conv_done"))
        s_xsp, s_xse, s_cbp, s_cbe, s_seg, s_dec, s_m, s_y, s_yev = (sem(n) for n in (
            "xs_psum", "xs_evicted", "cb_psum", "cb_evicted", "seg_psum", "ssd_decay", "ssd_weights",
            "ssd_y_psum", "ssd_y_evicted"))
        s_sp, s_gb, s_ld, s_sc, s_num, s_hl = (sem(n) for n in (
            "scores_psum", "maxima_psum", "lstm_decay", "lstm_weights", "num_psum", "hl_ready"))
        s_zs, s_yg, s_sq2, s_red, s_rm2, s_yn, s_hln, s_mxp, s_mxe, s_op, s_h = (sem(n) for n in (
            "z_sigmoid", "y_gated", "mixer_squares", "head_squares", "mixer_rms", "yssm_ready", "hlstm_ready",
            "mixed_psum", "mixed_evicted", "out_proj_psum", "h_ready"))
        s_sq3, s_rm3, s_hn, s_hTp, s_hTe, s_lgp, s_tp, s_se, s_M, s_pos, s_cnt, s_fl, s_pi, s_oh, s_tb, s_tab = (
            sem(n) for n in ("h_squares", "h_rms", "hn_ready", "hT_psum", "hT_ready", "logits_psum", "top_ready",
                             "softmax_exp", "selection_ready", "positions_psum", "counts_psum", "flags_ready",
                             "item_positions_psum", "item_onehot", "table_psum", "table_ready"))
        s_P, s_Pg, s_xg, s_XT, s_gu, s_g, s_u, s_sig, s_gs, s_act, s_pt, s_ptg, s_atp, s_aT, s_dnb, s_dn, s_os, s_sca = (
            sem(n) for n in ("P_ready", "Pg_sel_ready", "gathered_psum", "XT_ready", "gate_up_psum", "gate_clipped",
                             "up_clipped", "gate_sigmoid", "swish_ready", "act_ready", "PT_psum", "PT_ready",
                             "actT_psum", "actT_ready", "down_bias_done", "down_psum", "out_scaled", "scattered"))
        s_fsq, s_frm, s_fin = sem("final_squares"), sem("final_rms"), sem("final_ready")
        c_dve, c_act = sem("dve_chain"), sem("act_chain")

        def chain(engine, semaphore):
            count = [0]

            def link(ins):
                count[0] += 1
                ins.then_inc(semaphore, 1)
                engine.wait_ge(semaphore, count[0])
            return link

        def slot_of(g):
            return g % SLOTS

        def fills(g):
            return 16 * (g // SLOTS + 1)

        w_in_v = w_in[0].rearrange("(p j) n -> p j n", j=KT)
        w_out_v = w_out[0].rearrange("(j p) n -> p j n", p=P)
        wgu_v = w_gate_up[0].rearrange("e (p j) n -> e p (j n)", j=KT)
        wdn_v = w_down[0].rearrange("e (j p) n -> e p j n", p=P)

        block = ctx.enter_context(nc.Block())

        @block.sync
        def _(sp):
            for t in range(TT):
                sp.dma_start(x[:, t, :], x_d[0, t * P:(t + 1) * P, :]).then_inc(s_x[t], 16)
            sp.dma_start(small[:, :, 0:16], w_in_v[:, :, COL_DT:COL_DT + 16]).then_inc(s_small, 16)
            sp.dma_start(small[:, :, 16:32], w_in_v[:, :, COL_I:COL_I + 16]).then_inc(s_small, 16)

            def mixer_chunk_used(g):
                if g < 7:
                    sp.wait_ge(s_pj, 4 * (g + 1))
                elif g < N_IN:
                    sp.wait_ge(s_pj, 28 + 2 * (g - 6))
                elif g < N_MIX - 1:
                    sp.wait_ge(used, g - N_IN + 1)
                else:
                    sp.wait_ge(s_op, 1)

            for g in range(N_MIX):
                if g >= SLOTS:
                    mixer_chunk_used(g - SLOTS)
                if g < N_IN:
                    c = IN_COLS[g]
                    dst = ring[:, slot_of(g), :].rearrange("p (j n) -> p j n", j=KT)
                    sp.dma_start(dst, w_in_v[:, :, c:c + CW]).then_inc(full[slot_of(g)], 16)
                else:
                    k = g - N_IN
                    dst = ring[:, slot_of(g), :].rearrange("p (j n) -> p j n", j=4)
                    sp.dma_start(dst, w_out_v[:, 4 * k:4 * k + 4, :]).then_inc(full[slot_of(g)], 16)

            def load_expert(m, e, first=False):
                for c in range(CPE):
                    s = (N_MIX + c) % SLOTS
                    if first:
                        mixer_chunk_used(N_MIX + c - SLOTS)
                    elif c == 3:
                        sp.wait_ge(s_gu, m)
                    elif c == 5:
                        sp.wait_ge(s_dn, m)
                    else:
                        sp.wait_ge(used, 4 * m + (0, 1, 2, 0, 3)[c])
                    if c < 4:
                        src = wgu_v[bass.ds(e, 1), :, c * SLOTW:(c + 1) * SLOTW].rearrange("e p n -> (e p) n")
                        sp.dma_start(ring[:, s, :], src).then_inc(full[s], 16)
                    else:
                        src = wdn_v[bass.ds(e, 1), :, 4 * (c - 4):4 * (c - 4) + 4, :].rearrange("e p j n -> (e p) j n")
                        dst = ring[:, s, :].rearrange("p (j n) -> p j n", j=4)
                        sp.dma_start(dst, src).then_inc(full[s], 16)

            load_expert(0, 0, first=True)
            with sp.Fori(1, NE) as n:
                load_expert(n, n)
            sp.wait_ge(s_tab, 1)
            over = sp.value_load(tab[0:1, 2 * MAXOVER:2 * MAXOVER + 1], min_val=0, max_val=MAXOVER - 1)
            with sp.If(over > 0):
                with sp.Fori(0, over) as i:
                    e = sp.value_load(tab[0:1, bass.ds(i + MAXOVER, 1)], min_val=0, max_val=NE - 1)
                    load_expert(i + NE, e)
            sp.wait_ge(s_fin, 1)
            sp.dma_start(out_d[0, 0:P, :], hn[:, 0, :]).then_inc(s_out, 16)
            sp.wait_ge(s_fin, 2)
            sp.dma_start(out_d[0, P:T, :], hn[:, 1, :]).then_inc(s_out, 16)
            sp.wait_ge(s_out, 32)

        @block.gpsimd
        def _(pool):
            link = chain(pool, c_pool)
            for m, val in ((ident, 0.0), (identb, 0.0), (negm, 0.0), (tri_le, 1.0), (tri_gt, 1.0), (tri_lt, 1.0),
                           (selh, 0.0), (selall, 0.0)):
                last = G.memset(m[:], val)
            link(last)
            G.memset(ones[:, :], 1.0)
            G.memset(epst[:, :], EPS)

            def diagonal(m, op, fill, channel, pattern, base=0):
                return G.affine_select(out=m, in_=m, compare_op=op, fill=fill, base=base, pattern=pattern,
                                       channel_multiplier=channel)
            diagonal(ident[:, :], ALU.not_equal, 1.0, 1, [[-1, P]])
            diagonal(identb[:, :], ALU.not_equal, 1.0, 1, [[-1, P]])
            diagonal(negm[:, :], ALU.is_ge, -BIG, -1, [[1, P]])
            diagonal(tri_le[:, :], ALU.is_ge, 0.0, -1, [[1, P]])
            diagonal(tri_lt[:, :], ALU.is_gt, 0.0, -1, [[1, P]])
            diagonal(tri_gt[:, :], ALU.is_gt, 0.0, 1, [[-1, P]])
            diagonal(selh[:, :, :], ALU.not_equal, 1.0, 1, [[-1, H_LSTM], [0, P]])
            diagonal(selall[:, :, :], ALU.not_equal, 1.0, 1, [[0, NBLK], [-1, NE]])
            G.memset(raw[:, :, 0:CONV_W - 1], 0.0)
            G.iota(islot[:, :, :], pattern=[[0, 2], [1, SL]], base=0, channel_multiplier=0,
                   allow_small_or_imprecise_dtypes=True)
            G.iota(ie[:, :], pattern=[[1, NE]], base=0, channel_multiplier=0, allow_small_or_imprecise_dtypes=True)
            link(G.iota(ipart[:, :], pattern=[[0, 1]], base=0, channel_multiplier=1,
                        allow_small_or_imprecise_dtypes=True))
            for b in range(NBLK):
                rows = slice(b * NE, (b + 1) * NE)
                link(G.memset(thr[rows, :], float(b * SL) if b else BIG))
                link(G.iota(vmod[rows, :], pattern=[[0, 1]], base=0, channel_multiplier=1,
                            allow_small_or_imprecise_dtypes=True))
            G.memset(v1[:, :, :, HD_LSTM:VW], 1.0).then_inc(c_consts, 1)
            pool.wait_ge(s_at, 1)
            for g in range(4):
                if g >= 2:
                    pool.wait_ge(s_seg, 4 * (g - 1))
                for t in range(TT):
                    G.tensor_tensor(au[:, g % 2, :, t, :],
                                    tri_gt[:, :].unsqueeze(1).broadcast_to([P, 4, P]),
                                    at[:, t, 4 * g:4 * g + 4].unsqueeze(2).broadcast_to([P, 4, P]),
                                    ALU.mult).then_inc(s_au, 1)
            pool.wait_ge(s_yn, 1)
            pool.wait_ge(s_hl, H_LSTM)
            link(G.memset(biases, 0.0))
            pool.dma_start(biases[0:NE, 0:2 * FF], b_gate_up[0]).then_inc(s_bias, 16)
            pool.dma_start(biases[0:NE, 2 * FF:3 * FF], b_down[0]).then_inc(s_bias, 16)
            pool.wait_ge(s_op, 1)
            pool.dma_start(wfin, norm_final_w.unsqueeze(0).broadcast_to([P, D])).then_inc(s_wfin, 16)

        @block.scalar
        def _(ac):
            link = chain(ac, c_act)
            ac.dma_start(nmw[:, :], norm_mix_w[0].rearrange("(p j) -> p j", j=KT)).then_inc(s_nmw, 16)
            ac.dma_start(vecs[0:OFF_CB, :], conv_w[0].rearrange("w (c p) -> (w c) p", p=P)).then_inc(s_vec, 16)
            ac.dma_start(vecs[OFF_CB:OFF_SN, :], conv_b[0].rearrange("(c p) -> c p", p=P)).then_inc(s_vec, 16)
            ac.dma_start(vecs[OFF_SN:OFF_LN, :], ssm_norm_w[0].rearrange("(c p) -> c p", p=P)).then_inc(s_vec, 16)
            ac.dma_start(vecs[OFF_LN:NVEC, :], lstm_norm_w[0].rearrange("(c p) -> c p", p=P)).then_inc(s_vec, 16)
            ac.dma_start(dtb[:, :], dt_bias.broadcast_to([P, H_SSM])).then_inc(s_par, 16)
            ac.dma_start(alog[:, :], a_log.broadcast_to([P, H_SSM])).then_inc(s_par, 16)
            ac.dma_start(dsk[:, :], d_skip.broadcast_to([P, H_SSM])).then_inc(s_par, 16)
            ac.dma_start(ifb[:, 0:1], lstm_i_bias.rearrange("a h -> h a")).then_inc(s_par, 16)
            ac.dma_start(ifb[:, 1:2], lstm_f_bias.rearrange("a h -> h a")).then_inc(s_par, 16)
            ac.dma_start(nfw[:, :], norm_ffn_w[0].rearrange("(p j) -> p j", j=KT)).then_inc(s_par, 16)
            ac.dma_start(wr[:, :, :], w_router[0].rearrange("(p j) n -> p j n", j=KT)).then_inc(s_par, 16)
            ac.dma_start(br[:, :], b_router.broadcast_to([P, NE])).then_inc(s_par, 16)
            for t in range(TT):
                ac.wait_ge(s_x[t], 16)
                link(S.activation(scr[:, t, :], x[:, t, :], ACT.Square, accum_out=st[:, t:t + 1]))
            ac.wait_ge(c_consts, 1)
            S.activation(st[:, 2:4], st[:, 0:2], ACT.Sqrt, scale=RSQRT_D, bias=epst[:, :]).then_inc(s_rms, 1)
            ac.wait_ge(s_nmw, 16)
            for j in range(KT // 2, KT):
                ac.wait_ge(s_xT, j // 2 + 1)
                S.activation(xnT[:, j, :], B[j // 2][:, (j % 2) * T:(j % 2 + 1) * T], ACT.Copy,
                             scale=nmw[:, j:j + 1]).then_inc(s_xna, 1)
            ac.wait_ge(s_par, 128)
            S.activation(alog[:, :], alog[:, :], ACT.Exp).then_inc(s_expa, 1)
            for i, sp_t in enumerate((dsp, fsp)):
                ac.wait_ge(s_spin, i + 1)
                link(S.activation(sp_t[:, 2, :], sp_t[:, 1, :], ACT.Exp, scale=-1.0))
                S.activation(sp_t[:, 3, :], sp_t[:, 2, :], ACT.Ln, bias=1.0).then_inc(s_spln, 1)
            ac.wait_ge(s_gh, 1)
            S.activation(gates[:, 6, :], gates[:, 4, :], ACT.Exp, scale=-1.0).then_inc(s_em, 1)
            def conv_sigmoid(c):
                ac.wait_ge(s_cv, c + 1)
                if c >= 2:
                    ac.wait_ge(s_cd, c - 1)
                S.activation(csig[:, c % 2, :], conv[:, c, :], ACT.Sigmoid).then_inc(s_cs, 1)
            for c in range(NCH):
                ac.wait_ge(s_pj, c + 1)
                if c >= 3:
                    ac.wait_ge(s_cv, c - 2)
                S.activation(raw[:, c % 3, CONV_W - 1:], B[6 + c % 2][:, 0:T], ACT.Copy).then_inc(s_pe, 1)
                if c:
                    conv_sigmoid(c - 1)
            conv_sigmoid(NCH - 1)
            for h in range(2 * H_LSTM):
                i = NCH + h
                ac.wait_ge(s_pj, i + 1)
                dst = qT[:, h, :] if h < H_LSTM else kT[:, h - H_LSTM, :]
                S.activation(dst, B[6 + i % 2][:, 0:T], ACT.Copy).then_inc(s_pe, 1)
            ac.wait_ge(s_gte, 1)
            for h in range(H_SSM):
                ac.wait_ge(s_seg, h + 1)
                if h >= 3:
                    ac.wait_ge(s_y, h - 2)
                S.activation(dec[:, h % 3, 0:2 * P], B[h % 2][:, 0:2 * P], ACT.Exp)
                S.activation(dec[:, h % 3, 2 * P:3 * P], B[h % 2][:, 2 * P:3 * P], ACT.Exp,
                             bias=r0[:, h:h + 1]).then_inc(s_dec, 1)
            for n in range(8):
                i = NCH + 2 * H_LSTM + n
                half, t = (n % 4) // 2, n % 2
                ac.wait_ge(s_pj, i + 1)
                if n < 4:
                    S.activation(v1[:, t, 4 * half:4 * half + 4, 0:HD_LSTM],
                                 B[6 + i % 2][:, :].rearrange("p (h d) -> p h d", h=4), ACT.Copy).then_inc(s_pe, 1)
                else:
                    S.activation(z[:, t, half * 512:(half + 1) * 512], B[6 + i % 2][:, :], ACT.Copy).then_inc(s_pe, 1)
            for h in range(H_LSTM):
                ac.wait_ge(s_gb, h + 1)
                if h >= 3:
                    ac.wait_ge(s_num, h - 2)
                else:
                    ac.wait_ge(s_y, H_SSM)
                S.activation(dec[:, h % 3, 0:2 * P], B[2 + h % 2][:, 0:2 * P], ACT.Exp, bias=agT[:, 0, 0, h:h + 1])
                S.activation(dec[:, h % 3, 2 * P:3 * P], B[2 + h % 2][:, 2 * P:3 * P], ACT.Exp,
                             bias=agT[:, 0, 1, h:h + 1]).then_inc(s_ld, 1)
            ac.wait_ge(s_pe, NCH + 2 * H_LSTM + 8)
            for t in range(TT):
                S.activation(scr[:, t, :], z[:, t, :], ACT.Sigmoid).then_inc(s_zs, 1)
            ac.wait_ge(s_yg, 1)
            for t in range(TT):
                link(S.activation(scr[:, t, :], yssm[:, t, :], ACT.Square, accum_out=st[:, 4 + t:5 + t]))
            S.activation(st[:, 6:8], st[:, 4:6], ACT.Sqrt, scale=RSQRT_D, bias=epst[:, :]).then_inc(s_rm2, 1)
            ac.wait_ge(s_hl, H_LSTM)
            S.activation(auf, convf[:, 0:TT * D], ACT.Square).then_inc(s_sq2, 1)
            ac.wait_ge(s_red, 1)
            S.activation(st[:, 32:48], st[:, 16:32], ACT.Sqrt, scale=1.0 / HD_LSTM, bias=epst[:, :]).then_inc(s_rm2, 1)
            for n in range(4):
                i = NCH + 2 * H_LSTM + 8 + n
                ac.wait_ge(s_pj, i + 1)
                if n == 0:
                    ac.wait_ge(s_sc, H_LSTM)
                S.activation(og[:, n % 2, (n // 2) * 512:(n // 2 + 1) * 512], B[6 + i % 2][:, :],
                             ACT.Sigmoid).then_inc(s_pe, 1)
            for r in range(8):
                ac.wait_ge(s_mxp, r + 1)
                for jj in range(2):
                    c = 2 * r + jj
                    dst = mixA[:, c, :] if c < 8 else mixB[:, c - 8, :]
                    ins = S.activation(dst, B[4 + r % 2][:, jj * T:(jj + 1) * T], ACT.Copy,
                                       scale=vecT[:, OFF_SN + c:OFF_SN + c + 1])
                ins.then_inc(s_mxe, 1)
            for t in range(TT):
                ac.wait_ge(s_h, 2 * t + 2)
                link(S.activation(scr[:, t, :], x[:, t, :], ACT.Square, accum_out=st[:, 8 + t:9 + t]))
                S.activation(st[:, 10 + t:11 + t], st[:, 8 + t:9 + t], ACT.Sqrt, scale=RSQRT_D,
                             bias=epst[:, :]).then_inc(s_rm3, 1)
            for j in range(KT // 2, KT):
                ac.wait_ge(s_hTp, j // 2 + 1)
                S.activation(hT[:, j, :], B[4 + j // 2][:, (j % 2) * T:(j % 2 + 1) * T], ACT.Copy,
                             scale=nfw[:, j:j + 1]).then_inc(s_hTe, 1)
            for t in range(TT):
                ac.wait_ge(s_tp, t + 1)
                S.activation(sm[:, t, 0:4], top[:, t, 0:4], ACT.Exp, bias=sm[:, t, 4:5],
                             accum_out=sm[:, t, 5:6]).then_inc(s_se, 1)

            def expert(m):
                ac.wait_ge(s_g, m + 1)
                S.activation(sig, gmin, ACT.Sigmoid, scale=ALPHA).then_inc(s_sig, 1)
                ac.wait_ge(s_pt, m + 1)
                S.activation(PTg.rearrange("p t n -> p (t n)"), outb[:, 0:T], ACT.Copy).then_inc(s_ptg, 1)
                ac.wait_ge(s_atp, m + 1)
                S.activation(actT, hg[:, :], ACT.Copy).then_inc(s_aT, 1)
                ac.wait_ge(s_dn, m + 1)
                S.activation(outS, outb[:, :], ACT.Copy).then_inc(s_os, 1)

            with ac.Fori(0, NE) as n:
                expert(n)
            ac.wait_ge(s_tab, 1)
            over = ac.value_load(tab[0:1, 2 * MAXOVER:2 * MAXOVER + 1], min_val=0, max_val=MAXOVER - 1)
            with ac.If(over > 0):
                with ac.Fori(0, over) as i:
                    expert(i + NE)
            ac.wait_ge(s_sca, over + NE)
            ac.wait_ge(s_Pg, over + NE + 1)
            for t in range(TT):
                for hf in range(2):
                    ins = S.activation(scr[:, t, hf * 512:(hf + 1) * 512], ybank[t][hf][:, :], ACT.Square,
                                       accum_out=st[:, 48 + 2 * t + hf:49 + 2 * t + hf])
                ins.then_inc(s_fsq, 1)
            for t in range(TT):
                ac.wait_ge(s_frm, t + 1)
                S.activation(st[:, 54 + t:55 + t], st[:, 52 + t:53 + t], ACT.Sqrt, scale=RSQRT_D,
                             bias=epst[:, :]).then_inc(s_rm3, 1)

        @block.vector
        def _(ve):
            link = chain(ve, c_dve)
            ve.wait_ge(s_rms, 1)
            link(V.reciprocal(st[:, 12:14], st[:, 2:4]))
            for t in range(TT):
                V.tensor_scalar(xh[:, t, :], x[:, t, :], st[:, 12 + t:13 + t], None, ALU.mult).then_inc(s_xh, 1)
            ve.wait_ge(s_vps, 1)
            V.tensor_copy(vecT[:, :], B[4][:, 0:NVEC]).then_inc(s_vecT, 1)
            ve.wait_ge(s_nmw, 16)
            for j in range(KT // 2):
                ve.wait_ge(s_xT, j // 2 + 1)
                V.tensor_scalar(xnT[:, j, :], B[j // 2][:, (j % 2) * T:(j % 2 + 1) * T], nmw[:, j:j + 1], None,
                                ALU.mult).then_inc(s_xnv, 1)
            ve.wait_ge(s_sml, 1)
            ve.wait_ge(s_par, 128)
            dflat = B[5][:, 0:32].rearrange("p (t h) -> p t h", t=TT)
            d0 = dsp[:, 0, :].rearrange("p (t h) -> p t h", t=TT)
            link(V.tensor_tensor(d0, dflat, dtb[:, :].unsqueeze(1).broadcast_to([P, TT, H_SSM]), ALU.add))
            V.scalar_tensor_tensor(dsp[:, 1, :], dsp[:, 0, :], -1.0, dsp[:, 0, :], ALU.mult, ALU.max).then_inc(s_spin, 1)
            V.tensor_scalar(gates[:, 0, :], B[4][0:H_LSTM, 0:T], ifb[:, 0:1], None, ALU.add)
            link(V.tensor_scalar(fsp[:, 0, :], B[4][0:H_LSTM, T:2 * T], ifb[:, 1:2], -1.0, ALU.add, ALU.mult))
            V.scalar_tensor_tensor(fsp[:, 1, :], fsp[:, 0, :], -1.0, fsp[:, 0, :], ALU.mult, ALU.max).then_inc(s_spin, 1)
            for i, s5 in enumerate((dsp, fsp)):
                ve.wait_ge(s_spln, i + 1)
                link(V.tensor_scalar(s5[:, 4, :], s5[:, 2, :], 1.0, -1.0, ALU.add, ALU.add))
                link(V.tensor_scalar(s5[:, 5, :], s5[:, 4, :], 0.0, None, ALU.is_equal))
                V.tensor_tensor(s5[:, 3, :], s5[:, 3, :], s5[:, 5, :], ALU.add)
                link(V.tensor_tensor(s5[:, 4, :], s5[:, 4, :], s5[:, 5, :], ALU.add))
                link(V.reciprocal(s5[:, 6, :], s5[:, 4, :]))
                link(V.tensor_tensor(s5[:, 3, :], s5[:, 3, :], s5[:, 2, :], ALU.mult))
                link(V.tensor_tensor(s5[:, 3, :], s5[:, 3, :], s5[:, 6, :], ALU.mult))
                link(V.scalar_tensor_tensor(s5[:, 6, :], s5[:, 0, :], 0.0, s5[:, 3, :], ALU.max, ALU.add))
                if i == 0:
                    V.tensor_copy(dtt[:, :, :].rearrange("p t h -> p (t h)"), dsp[:, 6, :])
                    ve.wait_ge(s_expa, 1)
                    V.scalar_tensor_tensor(at[:, :, :], dsp[:, 6, :].rearrange("p (t h) -> p t h", t=TT), -1.0,
                                           alog[:, :].unsqueeze(1).broadcast_to([P, TT, H_SSM]),
                                           ALU.mult, ALU.mult).then_inc(s_at, 1)
            link(V.tensor_scalar(fsp[:, 6, :], fsp[:, 6, :], -1.0, None, ALU.mult))
            link(V.memset(fsp[:, 5, :], 1.0))
            link(V.tensor_tensor_scan(gates[:, 1, :], fsp[:, 5, :], fsp[:, 6, :], 0.0, ALU.mult, ALU.add))
            link(V.tensor_tensor(gates[:, 2, :], gates[:, 0, :], gates[:, 1, :], ALU.subtract))
            link(V.tensor_tensor_scan(gates[:, 3, :], gates[:, 2, :], gates[:, 2, :], 0.0, ALU.max, ALU.max))
            V.tensor_scalar(negG[:, :], gates[:, 3, :], -1.0, None, ALU.mult)
            V.tensor_tensor(gates[:, 4, :], gates[:, 1, :], gates[:, 3, :], ALU.add).then_inc(s_gh, 1)
            ve.wait_ge(s_vecT, 1)
            ve.wait_ge(c_consts, 1)

            def conv_finish(c):
                ve.wait_ge(s_cs, c + 1)
                V.tensor_tensor(conv[:, c, :], conv[:, c, :], csig[:, c % 2, :], ALU.mult).then_inc(s_cd, 1)
            for c in range(NCH):
                ve.wait_ge(s_pe, c + 1)

                def tap(w):
                    return raw[:, c % 3, w:w + T], vecT[:, w * NCH + c:w * NCH + c + 1]
                xi, wi = tap(0)
                link(V.tensor_scalar(conv[:, c, :], xi, wi, vecT[:, OFF_CB + c:OFF_CB + c + 1], ALU.mult, ALU.add))
                for w in range(1, CONV_W):
                    xi, wi = tap(w)
                    ins = V.scalar_tensor_tensor(conv[:, c, :], xi, wi, conv[:, c, :], ALU.mult, ALU.add)
                    if w < CONV_W - 1:
                        link(ins)
                ins.then_inc(s_cv, 1)
                if c:
                    conv_finish(c - 1)
            conv_finish(NCH - 1)
            ve.wait_ge(s_gtp, 1)
            V.tensor_copy(agT[:, :, :, :].rearrange("p a t h -> p (a t h)"), B[5][:, 80:112])
            V.tensor_copy(r0[:, :], B[5][:, 64:80]).then_inc(s_gte, 1)
            for b in range(4):
                t, half = b // 2, b % 2
                ve.wait_ge(s_xsp, b + 1)
                src = B[b][:, :].rearrange("p (h d) -> p h d", h=8)
                for dst, wgt in ((xd, dtt[:, t, 8 * half:8 * half + 8]), (yssm, dsk[:, 8 * half:8 * half + 8])):
                    ins = V.tensor_tensor(dst[:, t, half * 512:(half + 1) * 512].rearrange("p (h d) -> p h d", h=8),
                                          src, wgt.unsqueeze(2).broadcast_to([P, 8, HD_SSM]), ALU.mult)
                ins.then_inc(s_xse, 1)
            for g in range(2):
                ve.wait_ge(s_cbp, g + 1)
                V.tensor_tensor(cbm[:, g, 0:2 * P].rearrange("p (b n) -> p b n", b=2),
                                B[4 + g][:, 0:2 * P].rearrange("p (b n) -> p b n", b=2),
                                tri_le[:, :].unsqueeze(1).broadcast_to([P, 2, P]), ALU.mult)
                V.tensor_copy(cbm[:, g, 2 * P:3 * P], B[4 + g][:, 2 * P:3 * P]).then_inc(s_cbe, 1)
            ve.wait_ge(s_cbe, 2)
            for h in range(H_SSM):
                ve.wait_ge(s_dec, h + 1)
                V.tensor_tensor(dec[:, h % 3, :], dec[:, h % 3, :], cbm[:, h // 8, :], ALU.mult).then_inc(s_m, 1)
                if h % 8 == 7:
                    half = h // 8
                    ve.wait_ge(s_y, h + 1)
                    for t in range(TT):
                        part = yssm[:, t, half * 512:(half + 1) * 512]
                        V.tensor_tensor(part, B[2 + t][:, :], part, ALU.add).then_inc(s_yev, 1)
            def lstm_finish(h):
                ve.wait_ge(s_num, h + 1)
                nb = B[4 + h % 2][:, :].rearrange("p (t n) -> p t n", t=TT)
                dd = den[:, h % 2, :, :]
                link(V.tensor_copy(dd[:, :, 0:1], nb[:, :, HD_LSTM:HD_LSTM + 1]))
                link(V.scalar_tensor_tensor(dd[:, :, 1:2], dd[:, :, 0:1], -1.0, dd[:, :, 0:1], ALU.mult, ALU.max))
                link(V.tensor_tensor(dd[:, :, 0:1], dd[:, :, 1:2], agT[:, 1, :, h:h + 1], ALU.max))
                link(V.reciprocal(dd[:, :, 1:2], dd[:, :, 0:1]))
                for t in range(TT):
                    ins = V.tensor_scalar(hl[:, t, h, :], nb[:, t, 0:HD_LSTM], dd[:, t, 1:2], None, ALU.mult)
                ins.then_inc(s_hl, 1)
            for h in range(H_LSTM):
                ve.wait_ge(s_sp, h + 1)
                ve.wait_ge(s_ld, h + 1)
                V.scalar_tensor_tensor(dec[:, h % 3, :], B[h % 2][:, 0:3 * P], QK_SCALE, dec[:, h % 3, :],
                                       ALU.mult, ALU.mult).then_inc(s_sc, 1)
                if h:
                    lstm_finish(h - 1)
            lstm_finish(H_LSTM - 1)
            for t in range(TT):
                ve.wait_ge(s_zs, t + 1)
                link(V.tensor_tensor(z[:, t, :], z[:, t, :], scr[:, t, :], ALU.mult))
            ve.wait_ge(s_yev, 4)
            V.tensor_tensor(yssm[:, 0, :], yssm[:, 0, :], z[:, 0, :], ALU.mult)
            V.tensor_tensor(yssm[:, 1, :], yssm[:, 1, :], z[:, 1, :], ALU.mult).then_inc(s_yg, 1)
            ve.wait_ge(s_yg, 1)
            ve.wait_ge(s_rm2, 1)
            link(V.reciprocal(st[:, 14:16], st[:, 6:8]))
            for t in range(TT):
                ins = V.tensor_scalar(yssm[:, t, :], yssm[:, t, :], st[:, 14 + t:15 + t], None, ALU.mult)
            ins.then_inc(s_yn, 1)
            ve.wait_ge(s_sq2, 1)
            V.tensor_reduce(st[:, 16:32], auf.rearrange("p (g d) -> p g d", d=HD_LSTM), AX.X, ALU.add).then_inc(s_red, 1)
            ve.wait_ge(s_rm2, 2)
            link(V.reciprocal(st[:, 16:32], st[:, 32:48]))
            hlf = convf[:, 0:TT * D]
            link(V.tensor_tensor(hlf.rearrange("p (g d) -> p g d", d=HD_LSTM), hlf.rearrange("p (g d) -> p g d", d=HD_LSTM),
                                 st[:, 16:32].unsqueeze(2).broadcast_to([P, TT * H_LSTM, HD_LSTM]), ALU.mult))
            ve.wait_ge(s_pe, NCH + 2 * H_LSTM + 12)
            V.tensor_tensor(hlf, hlf, og.rearrange("p t d -> p (t d)"), ALU.mult).then_inc(s_hln, 1)
            ve.wait_ge(s_op, 1)
            for t in range(TT):
                for half in range(2):
                    part = x[:, t, half * 512:(half + 1) * 512]
                    V.tensor_tensor(part, B[2 * t + half][:, :], part, ALU.add).then_inc(s_h, 1)
            for t in range(TT):
                ve.wait_ge(s_rm3, t + 1)
                ve.wait_ge(s_h, 2 * t + 2)
                link(V.reciprocal(st[:, 56 + t:57 + t], st[:, 10 + t:11 + t]))
                V.tensor_scalar(hn[:, t, :], x[:, t, :], st[:, 56 + t:57 + t], None, ALU.mult).then_inc(s_hn, 1)
            for j in range(KT // 2):
                ve.wait_ge(s_hTp, j // 2 + 1)
                ins = V.tensor_scalar(hT[:, j, :], B[4 + j // 2][:, (j % 2) * T:(j % 2 + 1) * T], nfw[:, j:j + 1], None,
                                      ALU.mult)
            ins.then_inc(s_hTe, 1)
            ve.wait_ge(s_lgp, 1)
            link(V.tensor_tensor(lg[:, :, :], xb[:, 0:TT * NE].rearrange("p (t e) -> p t e", t=TT),
                                 br[:, :].unsqueeze(1).broadcast_to([P, TT, NE]), ALU.add))
            for t in range(TT):
                link(V.max(top[:, t, :], lg[:, t, :]))
                V.tensor_scalar(sm[:, t, 4:5], top[:, t, 0:1], -1.0, None, ALU.mult).then_inc(s_tp, 1)
            for t in range(TT):
                link(V.max_index(tidx[:, t, :], top[:, t, :], lg[:, t, :]))
                link(V.tensor_copy(tidf[:, t, :], tidx[:, t, :]))
                link(V.tensor_tensor(eq, ie[:, :].unsqueeze(1).broadcast_to([P, TOPK, NE]),
                                     tidf[:, t, 0:TOPK].unsqueeze(2).broadcast_to([P, TOPK, NE]), ALU.is_equal))
                link(V.tensor_reduce(mall[:, t, 0:NE], eq.rearrange("p k e -> p e k"), AX.X, ALU.add))
                ve.wait_ge(s_se, t + 1)
                link(V.reciprocal(sm[:, t, 6:7], sm[:, t, 5:6]))
                link(V.tensor_scalar(sm[:, t, 0:4], sm[:, t, 0:4], sm[:, t, 6:7], None, ALU.mult))
                link(V.tensor_tensor(eqg, eq, sm[:, t, 0:TOPK].unsqueeze(2).broadcast_to([P, TOPK, NE]),
                                     ALU.mult))
                link(V.tensor_reduce(gall[:, t, 0:NE], eqg.rearrange("p k e -> p e k"), AX.X, ALU.add))
            for b in range(1, NBLK):
                V.tensor_copy(gall[:, :, b * NE:(b + 1) * NE], gall[:, :, 0:NE])
                ins = V.tensor_copy(mall[:, :, b * NE:(b + 1) * NE], mall[:, :, 0:NE])
            ins.then_inc(s_M, 1)
            ve.wait_ge(s_pos, 1)
            link(V.scalar_tensor_tensor(posm[:, :, 0:NE], xb[:, 64:64 + TT * NE].rearrange("p (t e) -> p t e", t=TT), 1.0,
                                        mall[:, :, 0:NE], ALU.add, ALU.mult))
            for b in range(NBLK - 1, -1, -1):
                link(V.tensor_scalar(posm[:, :, b * NE:(b + 1) * NE], posm[:, :, 0:NE], -1.0 - b * SL, None, ALU.add))

            def pick(v):
                for t in range(TT):
                    ins = V.tensor_scalar(Pm[:, t, :], islot[:, 0, :], posm[:, t, bass.ds(v, 1)], None, ALU.is_equal)
                ins.then_inc(s_P, 1)

            def pick_gated(v):
                for t in range(TT):
                    V.tensor_scalar(Pg[:, t, :], islot[:, :, :].rearrange("p a s -> p (a s)"), posm[:, t, bass.ds(v, 1)],
                                    gall[:, t, bass.ds(v, 1)], ALU.is_equal, ALU.mult)
                V.tensor_copy(sel, selall[:, :, :].rearrange("p b e -> p (b e)")[:, bass.ds(v, 1)]
                              .broadcast_to([P, SL])).then_inc(s_Pg, 1)

            def gathered():
                V.tensor_tensor(XT.rearrange("p (j s) -> p j s", j=KT), xb[:, :].rearrange("p (j s) -> p j s", j=KT),
                                nfw[:, :].unsqueeze(2).broadcast_to([P, KT, SL]), ALU.mult).then_inc(s_XT, 1)

            def swiglu(m):
                ve.wait_ge(s_gu, m + 1)
                V.tensor_scalar(gmin, hg[:, :], LIMIT, None, ALU.min).then_inc(s_g, 1)
                V.tensor_scalar(ucl, hu[:, :], -LIMIT, LIMIT, ALU.max, ALU.min).then_inc(s_u, 1)
                ve.wait_ge(s_sig, m + 1)
                V.tensor_tensor(gsg, gmin, sig, ALU.mult).then_inc(s_gs, 1)
                ve.wait_ge(s_gs, m + 1)
                V.scalar_tensor_tensor(act, ucl, 1.0, gsg, ALU.add, ALU.mult).then_inc(s_act, 1)

            pick(0)
            pick_gated(0)
            ve.wait_ge(s_xg, 1)
            gathered()
            pick(1)
            ve.wait_ge(s_cnt, 1)
            V.tensor_tensor(flag[:, 0:1], outb[:, 0:1], thr[:, :], ALU.is_gt).then_inc(s_fl, 1)
            ve.wait_ge(s_pi, 1)
            link(V.tensor_copy(flag[:, 1:2], outb[:, 1:2]))
            V.tensor_scalar(oh[:, :], islot[:, 0, 0:MAXOVER], flag[:, 1:2], flag[:, 0:1], ALU.is_equal,
                            ALU.mult).then_inc(s_oh, 1)
            ve.wait_ge(s_tb, 1)
            link(V.tensor_copy(tabf[:, :], outb[0:1, 2:2 + 2 * MAXOVER + 1]))
            V.tensor_copy(tab[:, :], tabf[:, :]).then_inc(s_tab, 1)

            def main_item(n):
                swiglu(n)
                ve.wait_ge(s_xg, n + 2)
                gathered()
                pick(n + 2)
                ve.wait_ge(s_dnb, n + 1)
                pick_gated(n + 1)
            with ve.Fori(0, NE) as n:
                main_item(n)
            ve.wait_ge(s_tab, 1)
            over = ve.value_load(tab[0:1, 2 * MAXOVER:2 * MAXOVER + 1], min_val=0, max_val=MAXOVER - 1)
            with ve.If(over > 0):
                with ve.Fori(0, over) as i:
                    v = ve.value_load(tab[0:1, bass.ds(i, 1)], min_val=0, max_val=NV - 1)
                    ve.wait_ge(s_sca, i + NE)
                    pick(v)
                    pick_gated(v)
                    ve.wait_ge(s_xg, i + NE + 2)
                    gathered()
                    swiglu(i + NE)
            for t in range(TT):
                ve.wait_ge(s_fsq, t + 1)
                V.tensor_tensor(st[:, 52 + t:53 + t], st[:, 48 + 2 * t:49 + 2 * t], st[:, 49 + 2 * t:50 + 2 * t],
                                ALU.add).then_inc(s_frm, 1)
            ve.wait_ge(s_wfin, 16)
            for t in range(TT):
                ve.wait_ge(s_rm3, 3 + t)
                link(V.reciprocal(st[:, 58 + t:59 + t], st[:, 54 + t:55 + t]))
                for hf in range(2):
                    ins = V.scalar_tensor_tensor(hn[:, t, hf * 512:(hf + 1) * 512], ybank[t][hf][:, :],
                                                 st[:, 58 + t:59 + t], wfin[:, hf * 512:(hf + 1) * 512],
                                                 ALU.mult, ALU.mult)
                ins.then_inc(s_fin, 1)

        @block.tensor
        def _(pe):
            mm = E.matmul
            pe.wait_ge(c_consts, 1)
            pe.wait_ge(s_vec, 64)
            E.transpose(B[4][:, 0:NVEC], vecs[:, :], ident[0:NVEC, 0:NVEC]).then_inc(s_vps, 1)
            for t in range(TT):
                pe.wait_ge(s_xh, t + 1)
                for j in range(KT):
                    xv = xh[:, t, :].rearrange("p (q j) -> p q j", j=KT)[:, :, j]
                    ins = E.transpose(B[j // 2][:, (j % 2) * T + t * P:(j % 2) * T + (t + 1) * P], xv, ident[:, :])
                    if t == TT - 1 and j % 2:
                        ins.then_inc(s_xT, 1)
            pe.wait_ge(s_xnv, 4)
            pe.wait_ge(s_xna, 4)
            pe.wait_ge(s_small, 32)
            for t in range(TT):
                for j in range(KT):
                    mm(B[5][:, t * 16:(t + 1) * 16], xnT[:, j, t * P:(t + 1) * P], small[:, j, 0:16],
                       start=j == 0, stop=j == KT - 1)
            pe.wait_ge(s_vecT, 1)
            for k in range(2):
                for j in range(KT):
                    ins = mm(B[4][0:H_LSTM, k * T:(k + 1) * T], small[:, j, 16 + 8 * k:24 + 8 * k], xnT[:, j, :],
                             start=j == 0, stop=j == KT - 1)
            ins.then_inc(s_sml, 1)

            def by_channel(i, g, q):
                bank = B[6 + i % 2]
                if q == 0:
                    pe.wait_ge(full[slot_of(g)], fills(g))
                if i >= 2:
                    pe.wait_ge(s_pe, i - 1)
                for j in range(KT):
                    ins = mm(bank[:, 0:T], ring[:, slot_of(g), j * CW + q * P:j * CW + (q + 1) * P], xnT[:, j, :],
                             start=j == 0, stop=j == KT - 1)
                ins.then_inc(s_pj, 1)

            def by_token(i, g, t):
                bank = B[6 + i % 2]
                if t == 0:
                    pe.wait_ge(full[slot_of(g)], fills(g))
                pe.wait_ge(s_pe, i - 1)
                for j in range(KT):
                    ins = mm(bank[:, :], xnT[:, j, t * P:(t + 1) * P], ring[:, slot_of(g), j * CW:(j + 1) * CW],
                             start=j == 0, stop=j == KT - 1)
                ins.then_inc(s_pj, 1)

            for i in range(NCH):
                by_channel(i, i // 4, i % 4)
            pe.wait_ge(s_at, 1)
            pe.wait_ge(s_em, 1)
            mm(B[5][:, 64:80], tri_gt[:, :], at[:, 0, :], start=True, stop=True)
            for a, row in ((0, 2), (1, 6)):
                for t in range(TT):
                    ins = E.transpose(B[5][:, 80 + 16 * a + 8 * t:88 + 16 * a + 8 * t],
                                      gates[:, row, t * P:(t + 1) * P], ident[0:H_LSTM, 0:H_LSTM])
            ins.then_inc(s_gtp, 1)
            for i in range(NCH, NCH + 2 * H_LSTM):
                by_channel(i, i // 4, i % 4)
            pe.wait_ge(s_cd, XT_TILES)
            for t in range(TT):
                for c in range(XT_TILES):
                    ins = E.transpose(B[2 * t + c // 4][:, (c % 4) * P:(c % 4 + 1) * P], conv[:, c, t * P:(t + 1) * P],
                                      ident[:, :])
                    if c % 4 == 3:
                        ins.then_inc(s_xsp, 1)
            pe.wait_ge(s_cd, NCH)
            pe.wait_ge(s_gte, 1)
            for g in range(2):
                bT, cT = conv[:, XT_TILES + g, :], conv[:, XT_TILES + 2 + g, :]
                mm(B[4 + g][:, 0:P], bT[:, 0:P], cT[:, 0:P], start=True, stop=True)
                mm(B[4 + g][:, 2 * P:3 * P], bT[:, 0:P], cT[:, P:T], start=True, stop=True)
                mm(B[4 + g][:, P:2 * P], bT[:, P:T], cT[:, P:T], start=True, stop=True).then_inc(s_cbp, 1)
            pe.wait_ge(s_xse, 4)

            def seg(h):
                pe.wait_ge(s_au, 2 * (h // 4) + 2)
                if h >= 2:
                    pe.wait_ge(s_dec, h - 1)
                bank, a = B[h % 2], au[:, (h // 4) % 2, h % 4, :, :]
                mm(bank[:, 0:P], a[:, 0, :], tri_le[:, :], start=True, stop=True)
                mm(bank[:, P:2 * P], a[:, 1, :], tri_le[:, :], start=True, stop=True)
                mm(bank[:, 2 * P:3 * P], at[:, 1, h:h + 1].broadcast_to([P, P]), tri_le[:, :],
                   start=True, stop=True).then_inc(s_seg, 1)

            seg(0)
            for h in range(H_SSM):
                if h + 1 < H_SSM:
                    seg(h + 1)
                pe.wait_ge(s_m, h + 1)
                if h == 8:
                    pe.wait_ge(s_yev, 2)
                w, c = dec[:, h % 3, :], (h % 8) * HD_SSM
                xd0, xd1 = (xd[:, t, h * HD_SSM:(h + 1) * HD_SSM] for t in range(TT))
                mm(B[2][:, c:c + HD_SSM], w[:, 0:P], xd0, start=True, stop=True)
                mm(B[3][:, c:c + HD_SSM], w[:, 2 * P:3 * P], xd0, start=True, stop=False)
                mm(B[3][:, c:c + HD_SSM], w[:, P:2 * P], xd1, start=False, stop=True).then_inc(s_y, 1)
            i = NCH + 2 * H_LSTM
            for g in range(7, 11):
                for t in range(TT):
                    by_token(i, g, t)
                    i += 1
            pe.wait_ge(s_yev, 4)

            def scores(h):
                if h < 2:
                    pe.wait_ge(s_dec, H_SSM)
                else:
                    pe.wait_ge(s_sc, h - 1)
                q = qT[:, h, :]
                mm(B[h % 2][:, 0:T], kT[:, h, 0:P], q, start=True, stop=True)
                mm(B[h % 2][:, T:T + P], kT[:, h, P:T], q[:, P:T], start=True, stop=True).then_inc(s_sp, 1)
                if h >= 2:
                    pe.wait_ge(s_ld, h - 1)
                gb = B[2 + h % 2]
                mm(gb[:, 0:T], selh[:, h, :], negG[:, :], start=True, stop=False)
                mm(gb[:, 0:P], identb[:, :], negm[:, :], start=False, stop=True)
                mm(gb[:, T:T + P], selh[:, h, :], negG[:, P:T], start=True, stop=False)
                mm(gb[:, T:T + P], identb[:, :], negm[:, :], start=False, stop=True).then_inc(s_gb, 1)

            scores(0)
            for h in range(H_LSTM):
                if h + 1 < H_LSTM:
                    scores(h + 1)
                pe.wait_ge(s_sc, h + 1)
                if h < 2:
                    pe.wait_ge(s_cbe, 2)
                else:
                    pe.wait_ge(s_hl, h - 1)
                w, nb = dec[:, h % 3, :], B[4 + h % 2]
                mm(nb[:, 0:VW], w[:, 0:P], v1[:, 0, h, :], start=True, stop=True)
                mm(nb[:, T:T + VW], w[:, P:2 * P], v1[:, 0, h, :], start=True, stop=False)
                mm(nb[:, T:T + VW], w[:, 2 * P:3 * P], v1[:, 1, h, :], start=False, stop=True).then_inc(s_num, 1)
            for g in range(11, N_IN):
                for t in range(TT):
                    by_token(i, g, t)
                    i += 1
            for part in range(2):
                pe.wait_ge((s_yn, s_hln)[part], 1)
                for r in range(4 * part, 4 * part + 4):
                    if r < 2:
                        pe.wait_ge(s_hl, H_LSTM)
                    else:
                        pe.wait_ge(s_mxe, r - 1)
                    for jj in range(2):
                        c = 2 * r + jj
                        for t in range(TT):
                            src = yssm[:, t, c * P:(c + 1) * P] if c < 8 else hl[:, t, c - 8, :]
                            ins = E.transpose(B[4 + r % 2][:, jj * T + t * P:jj * T + (t + 1) * P], src, ident[:, :])
                    ins.then_inc(s_mxp, 1)
                for c in range(8 * part, 8 * part + 8):
                    g = N_IN + c // 4
                    if c % 4 == 0:
                        pe.wait_ge(full[slot_of(g)], fills(g))
                    pe.wait_ge(s_mxe, c // 2 + 1)
                    src = mixA[:, c, :] if c < 8 else mixB[:, c - 8, :]
                    for t in range(TT):
                        for half in range(2):
                            o = (c % 4) * D + half * 512
                            ins = mm(B[2 * t + half][:, :], src[:, t * P:(t + 1) * P], ring[:, slot_of(g), o:o + 512],
                                     start=c == 0, stop=c == 15)
                    if c % 4 == 3:
                        ins.then_inc(used if c < 15 else s_op, 1)
            pe.wait_ge(s_pe, NCH + 2 * H_LSTM + 12)
            pe.wait_ge(s_mxe, 8)
            for t in range(TT):
                pe.wait_ge(s_hn, t + 1)
                for j in range(KT):
                    xv = hn[:, t, :].rearrange("p (q j) -> p q j", j=KT)[:, :, j]
                    ins = E.transpose(B[4 + j // 2][:, (j % 2) * T + t * P:(j % 2) * T + (t + 1) * P], xv, ident[:, :])
                    if t == TT - 1 and j % 2:
                        ins.then_inc(s_hTp, 1)
            pe.wait_ge(s_h, 4)
            for t in range(TT):
                for half in range(2):
                    mm(ybank[t][half][:, :], ident[:, :], x[:, t, half * 512:(half + 1) * 512], start=True, stop=False)
            pe.wait_ge(s_hTe, 5)
            for t in range(TT):
                for j in range(KT):
                    ins = mm(xb[:, t * NE:(t + 1) * NE], hT[:, j, t * P:(t + 1) * P], wr[:, j, :],
                             start=j == 0, stop=j == KT - 1)
            ins.then_inc(s_lgp, 1)
            pe.wait_ge(s_M, 1)
            mm(xb[:, 64:96], tri_lt[:, :], mall[:, 0, 0:NE], start=True, stop=True)
            mm(xb[:, 96:128], ones[:, :], mall[:, 0, 0:NE], start=True, stop=False)
            mm(xb[:, 96:128], tri_lt[:, :], mall[:, 1, 0:NE], start=False, stop=True).then_inc(s_pos, 1)
            for t in range(TT):
                ins = mm(outb[:, 0:1], mall[:, t, :], ones[:, 0:1], start=t == 0, stop=t == TT - 1)
            ins.then_inc(s_cnt, 1)

            def gather(p):
                pe.wait_ge(s_P, p)
                for j in range(KT):
                    for t in range(TT):
                        hv = hn[:, t, :].rearrange("p (q j) -> p q j", j=KT)[:, :, j]
                        ins = mm(xb[:, j * SL:(j + 1) * SL], hv, Pm[:, t, :], start=t == 0, stop=t == TT - 1)
                ins.then_inc(s_xg, 1)

            def column_tiles(bank, lhsT, rhs, start, stop):
                for hf in range(2):
                    ins = mm(bank[hf * SL:(hf + 1) * SL, :], lhsT[hf], rhs[hf], start=start, stop=stop)
                return ins

            def gate_up(m, ready):
                pe.wait_ge(s_XT, ready)
                pe.wait_ge(s_Pg, ready)
                for bank, o in ((hg, 0), (hu, FF)):
                    column_tiles(bank, [sel] * 2, [biases[:, o:o + 512], biases[:, o + 512:o + 1024]], True, False)
                for j in range(KT):
                    s = (N_MIX + j // 2) % SLOTS
                    if j % 2 == 0:
                        pe.wait_ge(full[s], 16 * m + 16 * ((N_MIX + j // 2) // SLOTS + 1))
                    lhsT = XT[:, j * SL:(j + 1) * SL]
                    for bank, o in ((hg, 0), (hu, FF)):
                        o += (j % 2) * 2 * FF
                        ins = column_tiles(bank, [lhsT] * 2, [ring[:, s, o:o + 512], ring[:, s, o + 512:o + 1024]],
                                           False, j == KT - 1)
                    if j % 2:
                        ins.then_inc(used if j < KT - 1 else s_gu, 1)

            def transpose_gates():
                for t in range(TT):
                    ins = E.transpose(outb[:, t * P:(t + 1) * P], Pg[:, t, :], ident[:, :])
                ins.then_inc(s_pt, 1)

            def down(m):
                pe.wait_ge(s_act, m + 1)
                for q in range(4):
                    ins = E.transpose(hg[:, q * P:(q + 1) * P], act[:, q * P:(q + 1) * P], ident[:, :])
                ins.then_inc(s_atp, 1)
                pe.wait_ge(s_ptg, m + 1)
                column_tiles(outb, [sel] * 2, [biases[:, 2 * FF:2 * FF + 512], biases[:, 2 * FF + 512:3 * FF]],
                             True, False).then_inc(s_dnb, 1)
                pe.wait_ge(s_aT, m + 1)
                for f in range(8):
                    s = (N_MIX + 4 + f // 4) % SLOTS
                    if f % 4 == 0:
                        pe.wait_ge(full[s], 16 * m + 16 * ((N_MIX + 4 + f // 4) // SLOTS + 1))
                    q, half = f % 4, f // 4
                    lhsT = actT[:, q * P + half * SL:q * P + (half + 1) * SL]
                    o = q * D
                    ins = column_tiles(outb, [lhsT] * 2, [ring[:, s, o:o + 512], ring[:, s, o + 512:o + 1024]],
                                       False, f == 7)
                    if f % 4 == 3:
                        ins.then_inc(used if f < 7 else s_dn, 1)

            def scatter(m, last=False, again=False):
                pe.wait_ge(s_os, m + 1)
                for t in range(TT):
                    for hf in range(2):
                        rows = slice(hf * SL, (hf + 1) * SL)
                        ins = mm(ybank[t][hf][:, :], PTg[rows, t, :], outS[rows, :], start=False, stop=last,
                                 skip_group_check=again)
                ins.then_inc(s_sca, 1)

            gather(1)
            pe.wait_ge(s_bias, 32)

            def main_item(m, first=False):
                gate_up(m, m + 1)
                if first:
                    pe.wait_ge(s_fl, 1)
                    mm(outb[:, 1:2], tri_lt[:, :], flag[:, 0:1], start=True, stop=True).then_inc(s_pi, 1)
                    pe.wait_ge(s_oh, 1)
                    mm(outb[0:1, 2:2 + MAXOVER], ipart[:, :], oh[:, :], start=True, stop=True)
                    mm(outb[0:1, 2 + MAXOVER:2 + 2 * MAXOVER], vmod[:, :], oh[:, :], start=True, stop=True)
                    mm(outb[0:1, 2 + 2 * MAXOVER:3 + 2 * MAXOVER], flag[:, 0:1], ones[:, 0:1], start=True,
                       stop=True).then_inc(s_tb, 1)
                    pe.wait_ge(s_tab, 1)
                else:
                    scatter(m - 1)
                transpose_gates()
                gather(m + 2)
                down(m)

            main_item(0, first=True)
            with pe.Fori(1, NE) as n:
                main_item(n)
            scatter(NE - 1, last=True)
            over = pe.value_load(tab[0:1, 2 * MAXOVER:2 * MAXOVER + 1], min_val=0, max_val=MAXOVER - 1)
            with pe.If(over > 0):
                with pe.Fori(0, over) as i:
                    gather(i + NE + 3)
                    gate_up(i + NE, i + NE + 2)
                    transpose_gates()
                    down(i + NE)
                    scatter(i + NE, last=True, again=True)


_INS = ['x', 'norm_mix_w', 'w_in', 'conv_w', 'conv_b', 'dt_bias', 'a_log', 'd_skip', 'ssm_norm_w', 'lstm_i_bias',
        'lstm_f_bias', 'lstm_norm_w', 'w_out', 'norm_ffn_w', 'w_router', 'b_router', 'w_gate_up', 'b_gate_up',
        'w_down', 'b_down', 'norm_final_w']


def kernel(**inputs):
    import numpy as _np
    import concourse.bacc as _bacc
    from concourse import mybir as _mybir
    from concourse.bass_utils import run_bass_kernel_spmd as _run

    nc = _bacc.Bacc("TRN2", target_bir_lowering=False, num_devices=1)
    arrays, args = {}, []
    for name in _INS:
        a = _np.ascontiguousarray(inputs[name])
        arrays[f"in_{name}_dram"] = a
        args.append(nc.dram_tensor(f"in_{name}_dram", a.shape, _mybir.dt.from_np(a.dtype), kind="ExternalInput").ap())
    args.append(nc.dram_tensor("out_0_dram", (1, T, D), _mybir.dt.float32, kind="ExternalOutput").ap())
    hybrid_block(nc, *args)
    r = _run(nc, [arrays], core_ids=[0])
    return r.results[0]["out_0_dram"]
```

```python
import concourse.bass as bass
from concourse import mybir
from contextlib import ExitStack

P = 128
D = 1024
T = 256
TT = T // P
KT = D // P
H_SSM, HD_SSM = 16, 64
H_LSTM, HD_LSTM = 8, 128
W_SSM = H_SSM * HD_SSM
CONV_DIM = 1536
CONV_W = 4
NCH = CONV_DIM // P
XT_TILES = W_SSM // P
IN_DIM = 6688
COL_Z, COL_XBC, COL_DT = 0, 1024, 2560
COL_Q, COL_K, COL_V, COL_O, COL_I = 2576, 3600, 4624, 5648, 6672
NE = 32
TOPK = 4
FF = 1024
LIMIT, ALPHA = 7.0, 1.702
EPS = 1e-6
SL = 64
NBLK = T // SL
NV = NE * NBLK
MAXOVER = 16

SLOTS = 6
MSLOTS = 4
EXP_SLOTS = (4, 5, 1, 2, 3, 0)
SLOTW = 4096
CW = SLOTW // KT
UW = CW // 2
NHB = 3
IN_COLS = ([COL_XBC + CW * i for i in range(3)] + [c + CW * i for c in (COL_Q, COL_K, COL_V, COL_Z, COL_O)
                                                   for i in range(2)])
NQK = NCH + 2 * H_LSTM
N_IN = len(IN_COLS)
N4 = NCH + 4
I_TR = 8
I_GT, I_XS, I_CB = NCH + 8, NCH + 9, NCH + 11
N_OUT = 4
N_MIX = N_IN + N_OUT
CPE = 6
RSQRT_D = 1.0 / D
QK_SCALE = float(HD_LSTM) ** -0.5
BIG = 1e30


def hybrid_block(nc, x_d, norm_mix_w, w_in, conv_w, conv_b, dt_bias, a_log, d_skip, ssm_norm_w,
                 lstm_i_bias, lstm_f_bias, lstm_norm_w, w_out, norm_ffn_w, w_router, b_router,
                 w_gate_up, b_gate_up, w_down, b_down, norm_final_w, out_d):
    f32, f32r, bf16, i32, u32 = (mybir.dt.float32, mybir.dt.float32r, mybir.dt.bfloat16, mybir.dt.int32,
                                 mybir.dt.uint32)
    ALU, ACT, AX = mybir.AluOpType, mybir.ActivationFunctionType, mybir.AxisListType
    V, S, G, E = nc.vector, nc.scalar, nc.gpsimd, nc.tensor
    ctx = ExitStack()
    with ctx:
        def sb(name, shape, dt=f32):
            return ctx.enter_context(nc.sbuf_tensor(name, shape, dt))

        def sem(name):
            return ctx.enter_context(nc.semaphore(name))

        with (nc.sbuf_tensor("ringr", [P, SLOTS, SLOTW], f32r) as ringr,
              nc.sbuf_tensor("smallr", [P, KT, 32], f32r) as small_lo,
              nc.sbuf_tensor("xl", [P, KT, T], f32r) as xl):
            pass
        ring = sb("ring", [P, SLOTS, SLOTW])
        small = sb("small", [P, KT, 32])
        fin = sb("fin", [P, TT, D])
        small_hi = sb("small_hi", [P, KT, 32], f32r)
        w_hi = [ringr[:, MSLOTS + b // 2, (b % 2) * KT * UW:(b % 2 + 1) * KT * UW].rearrange("p (j n) -> p j n", j=KT)
                for b in range(NHB)]
        xh = ringr[:, SLOTS - 1, KT * UW:].rearrange("p (j t) -> p j t", j=KT)
        x = sb("x", [P, TT, D])
        conv = sb("conv", [P, NCH, T])
        convf = conv[:, :, :].rearrange("p a b -> p (a b)")
        hl = convf[:, 0:TT * D].rearrange("p (t h d) -> p t h d", t=TT, h=H_LSTM)
        nmr = convf[0:1, D:2 * D]
        yssm = sb("yssm", [P, TT, D])
        hT = yssm[:, :, :].rearrange("p a b -> p (a b)").rearrange("p (j t) -> p j t", j=KT)
        xd = sb("xd", [P, TT, D])
        og = xd
        qT = sb("qT", [P, KT, T])
        mixB = qT
        wfin = qT[:, :, :].rearrange("p a b -> p (a b)")[:, 0:D]
        kT = sb("kT", [P, KT, T])
        mixA = kT
        VW = HD_LSTM + 1
        vz = sb("vz", [P, TT * H_LSTM * VW + TT * D])
        v1 = vz[:, 0:TT * H_LSTM * VW].rearrange("p (t h d) -> p t h d", t=TT, h=H_LSTM)
        z = vz[:, TT * H_LSTM * VW:].rearrange("p (t d) -> p t d", t=TT)
        biases = vz[:, 0:3 * FF]
        raw = sb("raw", [P, 3, CONV_W - 1 + T])
        csig = sb("csig", [P, 2, T])
        cbm = sb("cbm", [P, 2, 3 * P])
        dec = sb("dec", [P, 3, 3 * P])
        au = sb("au", [P, 2, 4, TT, P])
        auf = au[:, :, :, :, :].rearrange("p a b c d -> p (a b c d)")
        scr = auf.rearrange("p (t d) -> p t d", t=TT)
        ifs = sb("ifs", [P, TT, 2 * H_LSTM])
        wr = sb("wr", [P, KT, NE])
        NVEC = CONV_W * NCH + NCH + 3 * KT
        vecs = sb("vecs", [NVEC, P])
        vecT = sb("vecT", [P, NVEC])
        OFF_CB = CONV_W * NCH
        OFF_SN, OFF_LN, OFF_FN = (OFF_CB + NCH + KT * i for i in range(3))
        nfw = vecT[:, OFF_FN:OFF_FN + KT]
        dtb = sb("dtb", [P, H_SSM])
        alog = sb("alog", [P, H_SSM])
        dsk = sb("dsk", [P, H_SSM])
        br = sb("br", [P, NE])
        ifb = sb("ifb", [H_LSTM, 2])
        ident = sb("ident", [P, P])
        identb = sb("identb", [P, P], bf16)
        negm = sb("negm", [P, P], bf16)
        tri_le = sb("tri_le", [P, P])
        tri_gt = sb("tri_gt", [P, P])
        tri_lt = sb("tri_lt", [P, P])
        ones = sb("ones", [P, P])
        selall = sb("selall", [P, NBLK, NE])
        islot = sb("islot", [P, 2, SL])
        ie = sb("ie", [P, NE])
        iover = ie[:, 0:MAXOVER]
        ipart = sb("ipart", [P, 1])
        vmod = sb("vmod", [P, 1])
        thr = sb("thr", [P, 1])
        epst = sb("epst", [P, 1])
        st = sb("st", [P, 32])
        XS, YS, HS, FS = 0, 6, 12, 18
        junk = csig[:, :, :].rearrange("p a (b d) -> p a b d", b=2)
        ls = sb("ls", [P, 6, TT, H_LSTM])
        dsp = sb("dsp", [P, 7, 32])
        fsp = vz[0:H_LSTM, TT * H_LSTM * VW:TT * H_LSTM * VW + 7 * T].rearrange("h (r t) -> h r t", r=7)
        dtt = sb("dtt", [P, TT, H_SSM])
        at = sb("at", [P, TT, H_SSM])
        r0 = sb("r0", [P, H_SSM])
        gates = xd[:, :, :].rearrange("p a b -> p (a b)")[0:H_LSTM, 0:7 * T].rearrange("h (r t) -> h r t", r=7)
        negG = sb("negG", [H_LSTM, T])
        agT = sb("agT", [P, 2, TT, H_LSTM])
        XT = convf[:, 0:512]
        act = convf[:, 512:1024]
        gmin = convf[:, 1024:1536]
        sig = convf[:, 1536:2048]
        actT = convf[:, 2048:2560]
        outS = convf[:, 2560:3072]
        ucl = raw[:, :, :].rearrange("p a b -> p (a b)")[:, 0:512]
        gsg = csig[:, :, :].rearrange("p a b -> p (a b)")
        decf = dec[:, :, :].rearrange("p a b -> p (a b)")
        Pm = decf[:, 0:TT * SL].rearrange("p (t s) -> p t s", t=TT)
        Pg = decf[:, 128:128 + TT * 2 * SL].rearrange("p (t s) -> p t s", t=TT)
        PTg = decf[:, 384:384 + TT * P].rearrange("p (t s) -> p t s", t=TT)
        sel = decf[:, 640:640 + SL]
        posm, gall, mall = (auf[:, n * TT * NV:(n + 1) * TT * NV].rearrange("p (t v) -> p t v", t=TT) for n in range(3))
        lg = sb("lg", [P, TT, NE])
        top = sb("top", [P, TT, 8])
        tidx = sb("tidx", [P, TT, 8], u32)
        tidf = sb("tidf", [P, TT, 8])
        sm = sb("sm", [P, TT, 8])
        eq = auf[:, 768:1024].rearrange("p (t k e) -> p t k e", t=TT, k=TOPK)
        eqg = auf[:, 1024:1152].rearrange("p (k e) -> p k e", k=TOPK)
        flag = sb("flag", [P, 4])
        oh = sb("oh", [P, MAXOVER])
        tabf = sb("tabf", [1, 2 * MAXOVER + 1])
        tab = sb("tab", [1, 2 * MAXOVER + 1], i32)

        B = [ctx.enter_context(nc.psum_tensor(f"bank{i}", [P, 512], f32)) for i in range(8)]
        ybank = [[B[0], B[1]], [B[2], B[3]]]
        hg, hu, outb, xb = B[4], B[5], B[6], B[7]

        s_x = [sem(f"x_loaded{t}") for t in range(TT)]
        s_first = sem("first_unit_loaded")
        s_nm, s_small, s_vec, s_par = sem("norm_mix_loaded"), sem("small_loaded"), sem("vecs_loaded"), sem("params_loaded")
        s_bias, s_wfin, s_out = sem("biases_loaded"), sem("final_weight_loaded"), sem("output_stored")
        full = [sem(f"slot_full{i}") for i in range(SLOTS)]
        used = sem("chunks_used")
        c_pool, c_eps, c_id, c_ones, c_consts = sem("pool_chain"), sem("eps_ready"), sem("ident_ready"), sem("ones_ready"), sem("consts_ready")
        s_rms, s_rx, s_xs, s_xT, s_xh, s_xl, s_smh, s_sml2, s_wh, s_wl = (sem(n) for n in (
            "x_rms", "x_rstd", "x_scaled", "xT_psum", "xT_high", "xT_low", "small_high", "small_low",
            "w_in_high", "w_in_low"))
        s_nmp, s_vps, s_vecT = sem("norm_mix_psum"), sem("vecs_psum"), sem("vecT_ready")
        s_sml, s_ifs, s_ift, s_dt, s_spin, s_spln, s_expa, s_at, s_gh, s_em, s_gtp, s_gte, s_au = (sem(n) for n in (
            "small_projected", "if_by_token", "if_by_head", "dt_biased", "softplus_in", "softplus_ln", "exp_a_log", "a_ready", "gates_by_head",
            "exp_neg_m", "gates_psum", "gates_by_token", "au_ready"))
        s_pj, s_pe, s_pa, s_raw, s_cv, s_cs, s_cd = (sem(n) for n in (
            "proj_psum", "channels_evicted", "tokens_evicted", "first_tap_ready", "conv_sum", "conv_sigmoid",
            "conv_done"))
        s_xsp, s_xse, s_cbp, s_cbe, s_seg, s_dec, s_m, s_y, s_yev = (sem(n) for n in (
            "xs_psum", "xs_evicted", "cb_psum", "cb_evicted", "seg_psum", "ssd_decay", "ssd_weights",
            "ssd_y_psum", "ssd_y_evicted"))
        s_sp, s_gb, s_ld, s_sc, s_num, s_hl = (sem(n) for n in (
            "scores_psum", "maxima_psum", "lstm_decay", "lstm_weights", "num_psum", "hl_ready"))
        s_zs, s_yg, s_yr, s_nsq, s_osg, s_lr, s_lm, s_hln, s_mxp, s_mxe, s_opa, s_ha, s_op, s_h = (sem(n) for n in (
            "z_sigmoid", "y_gated", "y_rms", "num_squares", "o_sigmoid", "head_variance", "head_rms", "hlstm_ready",
            "mixed_psum", "mixed_evicted", "out_proj_ssm_psum", "h_ssm_added", "out_proj_psum", "h_ready"))
        s_rm3, s_fr, s_lge, s_hTp, s_hTv, s_hTa, s_lgp, s_tp, s_se, s_M, s_pos, s_cnt, s_fl, s_pi, s_oh, s_tb, s_tab, s_tabs = (
            sem(n) for n in ("h_rms", "final_rms", "logits_evicted", "hT_psum", "hT_by_dve", "hT_by_act", "logits_psum", "top_ready",
                             "softmax_exp", "selection_ready", "positions_psum", "counts_psum", "flags_ready",
                             "item_positions_psum", "item_onehot", "table_psum", "table_ready", "block_tables"))
        s_P, s_Pg, s_xg, s_XT, s_gu, s_g, s_u, s_sig, s_gs, s_act, s_pt, s_ptg, s_atp, s_aT, s_dnb, s_dn, s_os, s_sca = (
            sem(n) for n in ("P_ready", "Pg_sel_ready", "gathered_psum", "XT_ready", "gate_up_psum", "gate_clipped",
                             "up_clipped", "gate_sigmoid", "swish_ready", "act_ready", "PT_psum", "PT_ready",
                             "actT_psum", "actT_ready", "down_bias_done", "down_psum", "out_scaled", "scattered"))
        s_fsq, s_frm, s_fin = sem("final_squares"), sem("final_sums"), sem("final_ready")
        c_dve, c_act = sem("dve_chain"), sem("act_chain")

        def chain(engine, semaphore):
            count = [0]

            def link(ins):
                count[0] += 1
                ins.then_inc(semaphore, 1)
                engine.wait_ge(semaphore, count[0])
            return link

        def slot_of(g):
            return g % MSLOTS

        def fills(g):
            return 16 * (g // MSLOTS + 1)

        def expert_fills(c, m):
            s = EXP_SLOTS[c]
            return 16 * m + 16 * (1 + sum(slot_of(g) == s for g in range(N_MIX)))

        def channel_bank(i):
            return B[(6, 7, 0, 1)[i % 4]] if i < N4 else B[6 + i % 2]

        def unit(tensor, u):
            chunk = tensor[:, slot_of(u // 2), :].rearrange("p (j n) -> p j n", j=KT)
            return chunk[:, :, (u % 2) * UW:(u % 2 + 1) * UW]

        w_in_v = w_in[0].rearrange("(j p) n -> p j n", p=P)
        w_out_v = w_out[0].rearrange("(j p) n -> p j n", p=P)
        wgu_v = w_gate_up[0].rearrange("e (j p) n -> e p j n", p=P)
        wdn_v = w_down[0].rearrange("e (j p) n -> e p j n", p=P)

        block = ctx.enter_context(nc.Block())

        @block.sync
        def _(sp):
            sp.dma_start(nmr, norm_mix_w).then_inc(s_nm, 16)
            for t in range(TT):
                sp.dma_start(x[:, t, :], x_d[0, t * P:(t + 1) * P, :]).then_inc(s_x[t], 16)
            def mixer_chunk_used(g):
                if g < 7:
                    sp.wait_ge(s_pj, 4 * (g + 1))
                elif g < N_IN:
                    sp.wait_ge(s_pj, 28 + 2 * (g - 6))
                else:
                    sp.wait_ge(*((used, 1), (s_opa, 1), (used, 2), (s_op, 2))[g - N_IN])

            for g in range(N_MIX):
                if g >= MSLOTS:
                    mixer_chunk_used(g - MSLOTS)
                if g < N_IN:
                    c = IN_COLS[g]
                    dst = ring[:, slot_of(g), :].rearrange("p (j n) -> p j n", j=KT)
                    if g:
                        sp.dma_start(dst, w_in_v[:, :, c:c + CW]).then_inc(full[slot_of(g)], 16)
                    else:
                        sp.dma_start(dst[:, :, 0:UW], w_in_v[:, :, c:c + UW]).then_inc(s_first, 16)
                        sp.dma_start(dst[:, :, UW:], w_in_v[:, :, c + UW:c + CW]).then_inc(full[0], 16)
                        sp.dma_start(small[:, :, 0:16], w_in_v[:, :, COL_DT:COL_DT + 16]).then_inc(s_small, 16)
                        sp.dma_start(small[:, :, 16:32], w_in_v[:, :, COL_I:COL_I + 16]).then_inc(s_small, 16)
                        sp.dma_start(vecs[0:OFF_CB, :], conv_w[0].rearrange("w (c p) -> (w c) p", p=P)).then_inc(s_vec, 16)
                        for off, rows, v in ((OFF_CB, NCH, conv_b), (OFF_SN, KT, ssm_norm_w), (OFF_LN, KT, lstm_norm_w),
                                             (OFF_FN, KT, norm_ffn_w)):
                            sp.dma_start(vecs[off:off + rows, :], v[0].rearrange("(c p) -> c p", p=P)).then_inc(s_vec, 16)
                    if g == 1:
                        sp.dma_start(dtb[:, :], dt_bias.broadcast_to([P, H_SSM])).then_inc(s_par, 16)
                        sp.dma_start(alog[:, :], a_log.broadcast_to([P, H_SSM])).then_inc(s_par, 16)
                        sp.dma_start(dsk[:, :], d_skip.broadcast_to([P, H_SSM])).then_inc(s_par, 16)
                        sp.dma_start(ifb[:, 0:1], lstm_i_bias.rearrange("a h -> h a")).then_inc(s_par, 16)
                        sp.dma_start(ifb[:, 1:2], lstm_f_bias.rearrange("a h -> h a")).then_inc(s_par, 16)
                        sp.dma_start(wr[:, :, :], w_router[0].rearrange("(j p) n -> p j n", p=P)).then_inc(s_par, 16)
                        sp.dma_start(br[:, :], b_router.broadcast_to([P, NE])).then_inc(s_par, 16)
                else:
                    k = g - N_IN
                    dst = ring[:, slot_of(g), :].rearrange("p (j n) -> p j n", j=4)
                    sp.dma_start(dst, w_out_v[:, 4 * k:4 * k + 4, :]).then_inc(full[slot_of(g)], 16)

            def load_expert(m, e, first=False):
                for c, s in enumerate(EXP_SLOTS):
                    if first:
                        mixer_chunk_used(N_IN - 1 if c < 2 else N_IN + c - 2)
                    elif c == 3:
                        sp.wait_ge(s_gu, m)
                    elif c == 5:
                        sp.wait_ge(s_dn, m)
                    else:
                        sp.wait_ge(used, 4 * m + (-1, 0, 1, 0, 2)[c])
                    if c < 4:
                        src = wgu_v[bass.ds(e, 1), :, 2 * c:2 * c + 2, :].rearrange("e p j n -> (e p) j n")
                        dst = ring[:, s, :].rearrange("p (j n) -> p j n", j=2)
                        sp.dma_start(dst, src).then_inc(full[s], 16)
                    else:
                        src = wdn_v[bass.ds(e, 1), :, 4 * (c - 4):4 * (c - 4) + 4, :].rearrange("e p j n -> (e p) j n")
                        dst = ring[:, s, :].rearrange("p (j n) -> p j n", j=4)
                        sp.dma_start(dst, src).then_inc(full[s], 16)

            load_expert(0, 0, first=True)
            with sp.Fori(1, NE) as n:
                load_expert(n, n)
            sp.wait_ge(s_tab, 1)
            over = sp.value_load(tab[0:1, 2 * MAXOVER:2 * MAXOVER + 1], min_val=0, max_val=MAXOVER - 1)
            with sp.If(over > 0):
                with sp.Fori(0, over) as i:
                    e = sp.value_load(tab[0:1, bass.ds(i + MAXOVER, 1)], min_val=0, max_val=NE - 1)
                    load_expert(i + NE, e)
            sp.wait_ge(s_fin, 1)
            sp.dma_start(out_d[0, 0:P, :], fin[:, 0, :]).then_inc(s_out, 16)
            sp.wait_ge(s_fin, 2)
            sp.dma_start(out_d[0, P:T, :], fin[:, 1, :]).then_inc(s_out, 16)
            sp.wait_ge(s_out, 32)

        @block.gpsimd
        def _(pool):
            link = chain(pool, c_pool)
            G.memset(epst[:, :], EPS).then_inc(c_eps, 1)
            G.memset(ones[:, :], 1.0).then_inc(c_ones, 1)
            link(G.memset(ident[:, :], 0.0))
            G.affine_select(out=ident[:, :], in_=ident[:, :], compare_op=ALU.not_equal, fill=1.0, base=0,
                            pattern=[[-1, P]], channel_multiplier=1).then_inc(c_id, 1)
            for m, val in ((identb, 0.0), (negm, 0.0), (tri_le, 1.0), (tri_gt, 1.0), (tri_lt, 1.0), (selall, 0.0)):
                last = G.memset(m[:], val)
            link(last)

            def diagonal(m, op, fill, channel, pattern, base=0):
                return G.affine_select(out=m, in_=m, compare_op=op, fill=fill, base=base, pattern=pattern,
                                       channel_multiplier=channel)
            diagonal(identb[:, :], ALU.not_equal, 1.0, 1, [[-1, P]])
            diagonal(negm[:, :], ALU.is_ge, -BIG, -1, [[1, P]])
            diagonal(tri_le[:, :], ALU.is_ge, 0.0, -1, [[1, P]])
            diagonal(tri_lt[:, :], ALU.is_gt, 0.0, -1, [[1, P]])
            diagonal(tri_gt[:, :], ALU.is_gt, 0.0, 1, [[-1, P]])
            diagonal(selall[:, :, :], ALU.not_equal, 1.0, 1, [[0, NBLK], [-1, NE]])
            G.memset(raw[:, :, 0:CONV_W - 1], 0.0)
            G.iota(islot[:, :, :], pattern=[[0, 2], [1, SL]], base=1, channel_multiplier=0,
                   allow_small_or_imprecise_dtypes=True)
            G.iota(ie[:, :], pattern=[[1, NE]], base=0, channel_multiplier=0, allow_small_or_imprecise_dtypes=True)
            link(G.iota(ipart[:, :], pattern=[[0, 1]], base=0, channel_multiplier=1,
                        allow_small_or_imprecise_dtypes=True))
            for b in range(NBLK):
                rows = slice(b * NE, (b + 1) * NE)
                link(G.memset(thr[rows, :], float(b * SL) if b else BIG))
                link(G.iota(vmod[rows, :], pattern=[[0, 1]], base=0, channel_multiplier=1,
                            allow_small_or_imprecise_dtypes=True))
            G.memset(v1[:, :, :, HD_LSTM:VW], 1.0).then_inc(c_consts, 1)
            pool.wait_ge(s_at, 1)
            for g in range(4):
                if g >= 2:
                    pool.wait_ge(s_seg, 4 * (g - 1))
                for t in range(TT):
                    G.tensor_tensor(au[:, g % 2, :, t, :],
                                    tri_gt[:, :].unsqueeze(1).broadcast_to([P, 4, P]),
                                    at[:, t, 4 * g:4 * g + 4].unsqueeze(2).broadcast_to([P, 4, P]),
                                    ALU.mult).then_inc(s_au, 1)
            pool.wait_ge(s_yg, 1)
            pool.wait_ge(s_num, H_LSTM)
            link(G.memset(biases, 0.0))
            pool.dma_start(biases[0:NE, 0:2 * FF], b_gate_up[0]).then_inc(s_bias, 16)
            pool.dma_start(biases[0:NE, 2 * FF:3 * FF], b_down[0]).then_inc(s_bias, 16)
            pool.wait_ge(s_op, 2)
            pool.dma_start(wfin, norm_final_w.unsqueeze(0).broadcast_to([P, D])).then_inc(s_wfin, 16)

        @block.scalar
        def _(ac):
            link = chain(ac, c_act)

            def rms(dst, src):
                return S.activation(dst, src, ACT.Sqrt, scale=RSQRT_D, bias=epst[:, :])
            ac.wait_ge(c_eps, 1)
            S.activation(st[:, 31:32], epst[:, :], ACT.Sqrt)
            for t in range(TT):
                ac.wait_ge(s_x[t], 16)
                link(S.activation(convf[:, 0:D], x[:, t, :], ACT.Square, accum_out=st[:, XS + t:XS + t + 1]))
                rms(st[:, XS + 2 + t:XS + 3 + t], st[:, XS + t:XS + t + 1]).then_inc(s_rms, 1)
            def w_high(u):
                if u:
                    ac.wait_ge(full[slot_of(u // 2)], fills(u // 2))
                else:
                    ac.wait_ge(s_first, 16)
                if u >= NHB:
                    v = u - NHB
                    ac.wait_ge(s_pj, 2 * (v + 1) if 2 * v < NQK else NQK + v - NQK // 2 + 1)
                S.activation(w_hi[u % NHB], unit(ring, u), ACT.Copy).then_inc(s_wh, 1)
            for t in range(TT):
                for b in range(2):
                    ac.wait_ge(s_xT, 2 * t + b + 1)
                    S.activation(xh[:, 4 * b:4 * b + 4, t * P:(t + 1) * P],
                                 B[2 * t + b][:, :].rearrange("p (j t) -> p j t", j=4), ACT.Copy).then_inc(s_xh, 1)
                if t == 0:
                    w_high(0)

            ac.wait_ge(s_small, 32)
            S.activation(small_hi[:, :, :], small[:, :, :], ACT.Copy).then_inc(s_smh, 1)
            w_high(1)

            def conv_sigmoid(c):
                ac.wait_ge(s_cv, c + 1)
                if c >= 2:
                    ac.wait_ge(s_cd, c - 1)
                S.activation(csig[:, c % 2, :], conv[:, c, :], ACT.Sigmoid).then_inc(s_cs, 1)
            ac.wait_ge(s_vecT, 1)
            ac.wait_ge(c_consts, 1)
            for i in range(NQK):
                if i % 2 == 0:
                    w_high(i // 2 + 2)
                ac.wait_ge(s_pj, i + 1)
                bank = channel_bank(i)[:, 0:T]
                if i < NCH:
                    if i >= 3:
                        ac.wait_ge(s_cv, i - 2)
                    S.activation(raw[:, i % 3, CONV_W - 1:], bank, ACT.Copy).then_inc(s_pe, 1)
                    if i:
                        conv_sigmoid(i - 1)
                    ac.wait_ge(s_pe, i + 1)
                    S.activation(conv[:, i, :], raw[:, i % 3, 0:T], ACT.Identity, scale=vecT[:, i:i + 1],
                                 bias=vecT[:, OFF_CB + i:OFF_CB + i + 1]).then_inc(s_raw, 1)
                else:
                    h = i - NCH
                    dst = qT[:, h, :] if h < H_LSTM else kT[:, h - H_LSTM, :]
                    S.activation(dst, bank, ACT.Copy).then_inc(s_pe, 1)
                if i == NCH:
                    conv_sigmoid(NCH - 1)
                if i == NCH + 1:
                    ac.wait_ge(s_par, 112)
                    S.activation(alog[:, :], alog[:, :], ACT.Exp).then_inc(s_expa, 1)
                if i in (NCH + 1, NCH + 2):
                    sp_t = (dsp, fsp)[i - NCH - 1]
                    ac.wait_ge(s_spin, i - NCH)
                    link(S.activation(sp_t[:, 2, :], sp_t[:, 1, :], ACT.Exp, scale=-1.0))
                    S.activation(sp_t[:, 3, :], sp_t[:, 2, :], ACT.Ln, bias=1.0).then_inc(s_spln, 1)
                if i == NCH + 6:
                    ac.wait_ge(s_gh, 1)
                    S.activation(gates[:, 6, :], gates[:, 4, :], ACT.Exp, scale=-1.0).then_inc(s_em, 1)
            ac.wait_ge(s_gte, 1)

            def by_token_tile(n):
                quarter, bank = n % 4, B[6 + n % 2]
                if n + 2 < N_IN * 2 - NQK // 2:
                    w_high(NQK // 2 + n + 2)
                ac.wait_ge(s_pj, NQK + n + 1)
                if n < 4:
                    for t in range(TT):
                        ins = S.activation(v1[:, t, 2 * quarter:2 * quarter + 2, 0:HD_LSTM],
                                           bank[:, t * UW:(t + 1) * UW].rearrange("p (h d) -> p h d", h=2), ACT.Copy)
                    ins.then_inc(s_pa, 1)
                else:
                    S.activation((z, og)[n // 4 - 1][:, :, quarter * UW:(quarter + 1) * UW],
                                 bank[:, :].rearrange("p (t n) -> p t n", t=TT), ACT.Copy).then_inc(s_pa, 1)

            for h in range(H_SSM):
                ac.wait_ge(s_seg, h + 1)
                if h >= 3:
                    ac.wait_ge(s_y, h - 2)
                S.activation(dec[:, h % 3, 0:2 * P], B[h % 2][:, 0:2 * P], ACT.Exp)
                S.activation(dec[:, h % 3, 2 * P:3 * P], B[h % 2][:, 2 * P:3 * P], ACT.Exp,
                             bias=r0[:, h:h + 1]).then_inc(s_dec, 1)
                if h % 2:
                    by_token_tile(h // 2)
            ac.wait_ge(s_pa, 8)
            ac.wait_ge(s_seg, H_SSM)
            for t in range(TT):
                S.activation(scr[:, t, :], z[:, t, :], ACT.Sigmoid).then_inc(s_zs, 1)
            ac.wait_ge(s_y, H_SSM)
            for h in range(H_LSTM):
                ac.wait_ge(s_gb, h + 1)
                if h >= 3:
                    ac.wait_ge(s_num, h - 2)
                S.activation(dec[:, h % 3, 0:2 * P], B[2 + h % 2][:, 0:2 * P], ACT.Exp, bias=agT[:, 0, 0, h:h + 1])
                S.activation(dec[:, h % 3, 2 * P:3 * P], B[2 + h % 2][:, 2 * P:3 * P], ACT.Exp,
                             bias=agT[:, 0, 1, h:h + 1]).then_inc(s_ld, 1)
                if h % 2:
                    by_token_tile(8 + h // 2)
                    for hh in (h - 1, h):
                        ac.wait_ge(s_hl, hh + 1)
                        if hh >= 2:
                            ac.wait_ge(s_nsq, hh - 1)
                        for t in range(TT):
                            ins = S.activation(junk[:, hh % 2, t, :], hl[:, t, hh, :], ACT.Square,
                                               accum_out=ls[:, 1, t, hh:hh + 1])
                        ins.then_inc(s_nsq, 1)
                if h == 3:
                    ac.wait_ge(s_yg, 1)
                    for t in range(TT):
                        S.activation(scr[:, t, :], yssm[:, t, :], ACT.Square, accum_out=st[:, YS + t:YS + t + 1])

            def mixed(r):
                ac.wait_ge(s_mxp, r + 1)
                for jj in range(2):
                    c = 2 * r + jj
                    dst = mixA[:, c, :] if c < 8 else mixB[:, c - 8, :]
                    ins = S.activation(dst, B[4 + r % 2][:, jj * T:(jj + 1) * T], ACT.Copy,
                                       scale=vecT[:, OFF_SN + c:OFF_SN + c + 1])
                ins.then_inc(s_mxe, 1)
            mixed(0)
            mixed(1)
            ac.wait_ge(s_pa, 12)
            for t in range(TT):
                ins = S.activation(og[:, t, :], og[:, t, :], ACT.Sigmoid)
            ins.then_inc(s_osg, 1)
            mixed(2)
            mixed(3)
            rms(st[:, YS + 2:YS + 4], st[:, YS:YS + 2]).then_inc(s_yr, 1)
            ac.wait_ge(s_lr, 1)
            S.activation(ls[:, 3, :, :], ls[:, 5, :, :], ACT.Sqrt, scale=1.0 / HD_LSTM, bias=epst[:, :]).then_inc(s_lm, 1)
            for r in range(4, 8):
                mixed(r)
            for t in range(TT):
                ac.wait_ge(s_h, t + 1)
                link(S.activation(scr[:, t, :], x[:, t, :], ACT.Square, accum_out=st[:, HS + t:HS + t + 1]))
                rms(st[:, HS + 2 + t:HS + 3 + t], st[:, HS + t:HS + t + 1]).then_inc(s_rm3, 1)
                ac.wait_ge(s_hTp, 2 * t + 2)
                for j in range(4, KT):
                    S.activation(hT[:, j, t * P:(t + 1) * P], B[5 + 2 * t][:, (j - 4) * P:(j - 3) * P], ACT.Copy,
                                 scale=nfw[:, j:j + 1]).then_inc(s_hTa, 1)
            for t in range(TT):
                ac.wait_ge(s_tp, t + 1)
                S.activation(sm[:, t, 0:4], top[:, t, 0:4], ACT.Exp, bias=sm[:, t, 4:5],
                             accum_out=sm[:, t, 5:6]).then_inc(s_se, 1)

            def expert(m):
                ac.wait_ge(s_g, m + 1)
                S.activation(sig, gmin, ACT.Sigmoid, scale=ALPHA).then_inc(s_sig, 1)
                ac.wait_ge(s_pt, m + 1)
                S.activation(PTg.rearrange("p t n -> p (t n)"), outb[:, 0:T], ACT.Copy).then_inc(s_ptg, 1)
                ac.wait_ge(s_atp, m + 1)
                S.activation(actT, hg[:, :], ACT.Copy).then_inc(s_aT, 1)
                ac.wait_ge(s_dn, m + 1)
                S.activation(outS, outb[:, :], ACT.Copy).then_inc(s_os, 1)

            with ac.Fori(0, NE) as n:
                expert(n)
            ac.wait_ge(s_tab, 1)
            over = ac.value_load(tab[0:1, 2 * MAXOVER:2 * MAXOVER + 1], min_val=0, max_val=MAXOVER - 1)
            with ac.If(over > 0):
                with ac.Fori(0, over) as i:
                    expert(i + NE)
            ac.wait_ge(s_sca, over + NE)
            ac.wait_ge(s_Pg, over + NE + 1)
            for t in range(TT):
                for hf in range(2):
                    ins = S.activation(scr[:, t, hf * 512:(hf + 1) * 512], ybank[t][hf][:, :], ACT.Square,
                                       accum_out=st[:, FS + 2 * t + hf:FS + 1 + 2 * t + hf])
                ins.then_inc(s_fsq, 1)
            ac.wait_ge(s_frm, 1)
            rms(st[:, FS + 6:FS + 8], st[:, FS + 4:FS + 6]).then_inc(s_fr, 1)

        @block.vector
        def _(ve):
            link = chain(ve, c_dve)

            def transposed(dst, bank, t, wgt, done):
                V.tensor_tensor(dst[:, 0:4, t * P:(t + 1) * P], bank[:, :].rearrange("p (j t) -> p j t", j=4),
                                wgt[:, 0:4].unsqueeze(2).broadcast_to([P, 4, P]), ALU.mult).then_inc(done, 1)
            for t in range(TT):
                ve.wait_ge(s_rms, t + 1)
                V.reciprocal(st[:, XS + 4 + t:XS + 5 + t], st[:, XS + 2 + t:XS + 3 + t]).then_inc(s_rx, 1)
                ve.wait_ge(s_rx, t + 1)
                ve.wait_ge(s_nmp, 1)
                for half in range(2):
                    cols = slice(half * 512, (half + 1) * 512)
                    V.scalar_tensor_tensor(scr[:, t, cols], x[:, t, cols], st[:, XS + 4 + t:XS + 5 + t],
                                           B[4 + half][:, :], ALU.mult, ALU.mult).then_inc(s_xs, 1)
            def xT_low(t):
                rows = slice(t * P, (t + 1) * P)
                for b in range(2):
                    ve.wait_ge(s_xh, 2 * t + b + 1)
                    js = slice(4 * b, 4 * b + 4)
                    V.tensor_tensor(xl[:, js, rows], B[2 * t + b][:, :].rearrange("p (j t) -> p j t", j=4),
                                    xh[:, js, rows], ALU.subtract).then_inc(s_xl, 1)

            def w_low(u):
                ve.wait_ge(s_wh, u + 1)
                V.tensor_tensor(unit(ringr, u), unit(ring, u), w_hi[u % NHB], ALU.subtract).then_inc(s_wl, 1)
            xT_low(0)
            xT_low(1)
            w_low(0)
            ve.wait_ge(s_vps, 1)
            V.tensor_copy(vecT[:, :], B[4][:, 0:NVEC]).then_inc(s_vecT, 1)
            ve.wait_ge(s_vecT, 1)
            ve.wait_ge(s_smh, 1)
            V.tensor_tensor(small_lo[:, :, :], small[:, :, :], small_hi[:, :, :], ALU.subtract).then_inc(s_sml2, 1)
            w_low(1)

            def if_by_token():
                ve.wait_ge(s_sml, 1)
                V.tensor_copy(ifs[:, :, :], B[5][:, 0:64].rearrange("p (t n) -> p t n", t=TT)[:, :, H_SSM:]).then_inc(s_ifs, 1)

            def softplus_inputs():
                ve.wait_ge(s_par, 112)
                V.tensor_tensor(dsp[:, 0, :].rearrange("p (t h) -> p t h", t=TT),
                                B[5][:, 0:64].rearrange("p (t n) -> p t n", t=TT)[:, :, 0:H_SSM],
                                dtb[:, :].unsqueeze(1).broadcast_to([P, TT, H_SSM]), ALU.add).then_inc(s_dt, 1)
                ve.wait_ge(s_dt, 1)
                V.scalar_tensor_tensor(dsp[:, 1, :], dsp[:, 0, :], -1.0, dsp[:, 0, :], ALU.mult,
                                       ALU.max).then_inc(s_spin, 1)
                ve.wait_ge(s_ift, 1)
                V.tensor_scalar(gates[:, 0, :], B[4][0:H_LSTM, 0:T], ifb[:, 0:1], None, ALU.add)
                link(V.tensor_scalar(fsp[:, 0, :], B[4][0:H_LSTM, T:2 * T], ifb[:, 1:2], -1.0, ALU.add, ALU.mult))
                V.scalar_tensor_tensor(fsp[:, 1, :], fsp[:, 0, :], -1.0, fsp[:, 0, :], ALU.mult,
                                       ALU.max).then_inc(s_spin, 1)

            def softplus(i):
                s5 = (dsp, fsp)[i]
                ve.wait_ge(s_spln, i + 1)
                link(V.tensor_scalar(s5[:, 4, :], s5[:, 2, :], 1.0, -1.0, ALU.add, ALU.add))
                link(V.tensor_scalar(s5[:, 5, :], s5[:, 4, :], 0.0, None, ALU.is_equal))
                V.tensor_tensor(s5[:, 3, :], s5[:, 3, :], s5[:, 5, :], ALU.add)
                link(V.tensor_tensor(s5[:, 4, :], s5[:, 4, :], s5[:, 5, :], ALU.add))
                link(V.reciprocal(s5[:, 6, :], s5[:, 4, :]))
                link(V.tensor_tensor(s5[:, 3, :], s5[:, 3, :], s5[:, 2, :], ALU.mult))
                link(V.tensor_tensor(s5[:, 3, :], s5[:, 3, :], s5[:, 6, :], ALU.mult))
                link(V.scalar_tensor_tensor(s5[:, 6, :], s5[:, 0, :], 0.0, s5[:, 3, :], ALU.max, ALU.add))

            def ssd_gates():
                V.tensor_copy(dtt[:, :, :].rearrange("p t h -> p (t h)"), dsp[:, 6, :])
                ve.wait_ge(s_expa, 1)
                V.scalar_tensor_tensor(at[:, :, :], dsp[:, 6, :].rearrange("p (t h) -> p t h", t=TT), -1.0,
                                       alog[:, :].unsqueeze(1).broadcast_to([P, TT, H_SSM]),
                                       ALU.mult, ALU.mult).then_inc(s_at, 1)

            def lstm_gates():
                V.memset(fsp[:, 5, :], -1.0)
                link(V.memset(fsp[:, 4, :], 1.0))
                link(V.tensor_tensor(fsp[:, 6, :], fsp[:, 6, :], fsp[:, 5, :], ALU.mult))
                link(V.tensor_tensor_scan(gates[:, 1, :], fsp[:, 4, :], fsp[:, 6, :], 0.0, ALU.mult, ALU.add))
                link(V.tensor_tensor(gates[:, 2, :], gates[:, 0, :], gates[:, 1, :], ALU.subtract))
                link(V.tensor_tensor_scan(gates[:, 3, :], gates[:, 2, :], gates[:, 2, :], 0.0, ALU.max, ALU.max))
                V.tensor_scalar(negG[:, :], gates[:, 3, :], -1.0, None, ALU.mult)
                V.tensor_tensor(gates[:, 4, :], gates[:, 1, :], gates[:, 3, :], ALU.add).then_inc(s_gh, 1)

            def conv_finish(c):
                ve.wait_ge(s_cs, c + 1)
                V.tensor_tensor(conv[:, c, :], conv[:, c, :], csig[:, c % 2, :], ALU.mult).then_inc(s_cd, 1)
            for c in range(NCH):
                if c % 2 == 0:
                    w_low(c // 2 + 2)
                ve.wait_ge(s_raw, c + 1)
                for w in range(1, CONV_W):
                    ins = V.scalar_tensor_tensor(conv[:, c, :], raw[:, c % 3, w:w + T],
                                                 vecT[:, w * NCH + c:w * NCH + c + 1], conv[:, c, :], ALU.mult, ALU.add)
                    if w < CONV_W - 1:
                        link(ins)
                ins.then_inc(s_cv, 1)
                if c:
                    conv_finish(c - 1)
                if c == I_TR - 2:
                    if_by_token()

            def gates_by_token():
                ve.wait_ge(s_gtp, 1)
                V.tensor_copy(agT[:, :, :, :].rearrange("p a t h -> p (a t h)"), B[5][:, 80:112])
                V.tensor_copy(r0[:, :], B[5][:, 64:80]).then_inc(s_gte, 1)

            def xs_by_token(b):
                t, half = b // 2, b % 2
                ve.wait_ge(s_xsp, b + 1)
                src = B[b][:, :].rearrange("p (h d) -> p h d", h=8)
                for dst, wgt in ((xd, dtt[:, t, 8 * half:8 * half + 8]), (yssm, dsk[:, 8 * half:8 * half + 8])):
                    ins = V.tensor_tensor(dst[:, t, half * 512:(half + 1) * 512].rearrange("p (h d) -> p h d", h=8),
                                          src, wgt.unsqueeze(2).broadcast_to([P, 8, HD_SSM]), ALU.mult)
                ins.then_inc(s_xse, 1)

            def cb_masked(g):
                ve.wait_ge(s_cbp, g + 1)
                V.tensor_tensor(cbm[:, g, 0:2 * P].rearrange("p (b n) -> p b n", b=2),
                                B[4 + g][:, 0:2 * P].rearrange("p (b n) -> p b n", b=2),
                                tri_le[:, :].unsqueeze(1).broadcast_to([P, 2, P]), ALU.mult)
                V.tensor_copy(cbm[:, g, 2 * P:3 * P], B[4 + g][:, 2 * P:3 * P]).then_inc(s_cbe, 1)

            for i in range(NCH, NQK):
                if i % 2 == 0:
                    w_low(i // 2 + 2)
                if i == NCH:
                    conv_finish(NCH - 1)
                    softplus_inputs()
                if i == NCH + 2:
                    softplus(0)
                    ssd_gates()
                if i == NCH + 3:
                    softplus(1)
                if i == NCH + 4:
                    lstm_gates()
                if i == I_GT:
                    gates_by_token()
                if i == I_XS:
                    for b in range(4):
                        xs_by_token(b)
                if i == I_CB:
                    cb_masked(0)
                    cb_masked(1)
            ve.wait_ge(s_cbe, 2)
            ve.wait_ge(s_xse, 4)
            for h in range(H_SSM):
                ve.wait_ge(s_dec, h + 1)
                V.tensor_tensor(dec[:, h % 3, :], dec[:, h % 3, :], cbm[:, h // 8, :], ALU.mult).then_inc(s_m, 1)
                if h % 2:
                    w_low(NQK // 2 + h // 2 + 2)
                if h % 8 == 7:
                    half = h // 8
                    ve.wait_ge(s_y, h + 1)
                    for t in range(TT):
                        part = yssm[:, t, half * 512:(half + 1) * 512]
                        V.tensor_tensor(part, B[2 + t][:, :], part, ALU.add).then_inc(s_yev, 1)

            def weights(h):
                ve.wait_ge(s_sp, h + 1)
                ve.wait_ge(s_ld, h + 1)
                V.scalar_tensor_tensor(dec[:, h % 3, :], B[h % 2][:, 0:3 * P], QK_SCALE, dec[:, h % 3, :],
                                       ALU.mult, ALU.mult).then_inc(s_sc, 1)
            for h in range(0, H_LSTM, 2):
                weights(h)
                weights(h + 1)
                if NQK // 2 + 8 + h // 2 + 2 < 2 * N_IN:
                    w_low(NQK // 2 + 8 + h // 2 + 2)
                if h == 0:
                    for t in range(TT):
                        ve.wait_ge(s_zs, t + 1)
                        link(V.tensor_tensor(z[:, t, :], z[:, t, :], scr[:, t, :], ALU.mult))
                    ve.wait_ge(s_yev, 4)
                    V.tensor_tensor(yssm[:, 0, :], yssm[:, 0, :], z[:, 0, :], ALU.mult)
                    V.tensor_tensor(yssm[:, 1, :], yssm[:, 1, :], z[:, 1, :], ALU.mult).then_inc(s_yg, 1)
                for hh in (h, h + 1):
                    ve.wait_ge(s_num, hh + 1)
                    nb = B[4 + hh % 2][:, :].rearrange("p (t n) -> p t n", t=TT)
                    V.tensor_copy(hl[:, :, hh, :], nb[:, :, 0:HD_LSTM])
                    V.tensor_copy(ls[:, 0, :, hh:hh + 1], nb[:, :, HD_LSTM:HD_LSTM + 1]).then_inc(s_hl, 1)
            ve.wait_ge(s_hl, H_LSTM)
            ve.wait_ge(s_nsq, H_LSTM)
            link(V.scalar_tensor_tensor(ls[:, 5, :, :], ls[:, 0, :, :], -1.0, ls[:, 0, :, :], ALU.mult, ALU.max))
            link(V.tensor_tensor(ls[:, 5, :, :], ls[:, 5, :, :], agT[:, 1, :, :], ALU.max))
            link(V.reciprocal(ls[:, 2, :, :], ls[:, 5, :, :]))
            link(V.tensor_tensor(ls[:, 4, :, :], ls[:, 2, :, :], ls[:, 1, :, :], ALU.mult))
            V.tensor_tensor(ls[:, 5, :, :], ls[:, 4, :, :], ls[:, 2, :, :], ALU.mult).then_inc(s_lr, 1)
            ve.wait_ge(s_lm, 1)
            link(V.reciprocal(ls[:, 4, :, :], ls[:, 3, :, :]))
            link(V.tensor_tensor(ls[:, 4, :, :], ls[:, 4, :, :], ls[:, 2, :, :], ALU.mult))
            ve.wait_ge(s_osg, 1)
            for t in range(TT):
                for h in range(H_LSTM):
                    ins = V.scalar_tensor_tensor(hl[:, t, h, :], hl[:, t, h, :], ls[:, 4, t, h:h + 1],
                                                 og[:, t, h * HD_LSTM:(h + 1) * HD_LSTM], ALU.mult, ALU.mult)
            ins.then_inc(s_hln, 1)
            ve.wait_ge(s_yr, 1)
            link(V.reciprocal(st[:, YS + 4:YS + 6], st[:, YS + 2:YS + 4]))
            ve.wait_ge(s_opa, 1)
            for t in range(TT):
                for half in range(2):
                    part = x[:, t, half * 512:(half + 1) * 512]
                    ins = V.scalar_tensor_tensor(part, B[2 * t + half][:, :], st[:, YS + 4 + t:YS + 5 + t], part,
                                                 ALU.mult, ALU.add)
                ins.then_inc(s_ha, 1)

            def choose(t):
                ve.wait_ge(s_op, t + 1)
                ve.wait_ge(s_ha, t + 1)
                for half in range(2):
                    part = x[:, t, half * 512:(half + 1) * 512]
                    ins = V.tensor_tensor(part, B[2 * t + half][:, :], part, ALU.add)
                ins.then_inc(s_h, 1)
                ve.wait_ge(s_hTp, 2 * t + 1)
                transposed(hT, B[4 + 2 * t], t, nfw, s_hTv)
                ve.wait_ge(s_rm3, t + 1)
                link(V.reciprocal(st[:, HS + 4 + t:HS + 5 + t], st[:, HS + 2 + t:HS + 3 + t]))
                ve.wait_ge(s_lgp, t + 1)
                V.scalar_tensor_tensor(lg[:, t, :], B[2 * t][:, 0:NE], st[:, HS + 4 + t:HS + 5 + t], br[:, :],
                                       ALU.mult, ALU.add).then_inc(s_lge, 1)
                ve.wait_ge(s_lge, t + 1)
                link(V.max(top[:, t, :], lg[:, t, :]))
                link(V.max_index(tidx[:, t, :], top[:, t, :], lg[:, t, :]))
                link(V.tensor_copy(tidf[:, t, :], tidx[:, t, :]))
                link(V.tensor_tensor(eq[:, t, :, :], ie[:, :].unsqueeze(1).broadcast_to([P, TOPK, NE]),
                                     tidf[:, t, 0:TOPK].unsqueeze(2).broadcast_to([P, TOPK, NE]), ALU.is_equal))
                V.tensor_reduce(mall[:, t, 0:NE], eq[:, t, :, :].rearrange("p k e -> p e k"), AX.X,
                                ALU.add).then_inc(s_M, 1)
                V.tensor_scalar(sm[:, t, 4:5], top[:, t, 0:1], -1.0, None, ALU.mult).then_inc(s_tp, 1)

            def position_tables():
                ve.wait_ge(s_pos, 1)
                link(V.scalar_tensor_tensor(posm[:, :, 0:NE], xb[:, 64:64 + TT * NE].rearrange("p (t e) -> p t e", t=TT),
                                            1.0, mall[:, :, 0:NE], ALU.add, ALU.mult))

            def block_tables():
                for b in range(NBLK - 1, 0, -1):
                    V.tensor_scalar(posm[:, :, b * NE:(b + 1) * NE], posm[:, :, 0:NE], -1.0 * b * SL, None, ALU.add)
                    V.tensor_copy(mall[:, :, b * NE:(b + 1) * NE], mall[:, :, 0:NE])
                for t in range(TT):
                    ve.wait_ge(s_se, t + 1)
                    link(V.reciprocal(sm[:, t, 6:7], sm[:, t, 5:6]))
                    link(V.tensor_scalar(sm[:, t, 0:4], sm[:, t, 0:4], sm[:, t, 6:7], None, ALU.mult))
                    link(V.tensor_tensor(eqg, eq[:, t, :, :], sm[:, t, 0:TOPK].unsqueeze(2).broadcast_to([P, TOPK, NE]),
                                         ALU.mult))
                    link(V.tensor_reduce(gall[:, t, 0:NE], eqg.rearrange("p k e -> p e k"), AX.X, ALU.add))
                for b in range(1, NBLK):
                    ins = V.tensor_copy(gall[:, :, b * NE:(b + 1) * NE], gall[:, :, 0:NE])
                ins.then_inc(s_tabs, 1)
                ve.wait_ge(s_tabs, 1)

            choose(0)
            choose(1)
            position_tables()

            def pick(v):
                for t in range(TT):
                    ins = V.tensor_scalar(Pm[:, t, :], islot[:, 0, :], posm[:, t, bass.ds(v, 1)],
                                          st[:, HS + 4 + t:HS + 5 + t], ALU.is_equal, ALU.mult)
                ins.then_inc(s_P, 1)

            def pick_gated(v):
                for t in range(TT):
                    V.tensor_scalar(Pg[:, t, :], islot[:, :, :].rearrange("p a s -> p (a s)"), posm[:, t, bass.ds(v, 1)],
                                    gall[:, t, bass.ds(v, 1)], ALU.is_equal, ALU.mult)
                V.tensor_copy(sel, selall[:, :, :].rearrange("p b e -> p (b e)")[:, bass.ds(v, 1)]
                              .broadcast_to([P, SL])).then_inc(s_Pg, 1)

            def gathered():
                V.tensor_tensor(XT.rearrange("p (j s) -> p j s", j=KT), xb[:, :].rearrange("p (j s) -> p j s", j=KT),
                                nfw[:, :].unsqueeze(2).broadcast_to([P, KT, SL]), ALU.mult).then_inc(s_XT, 1)

            def swiglu(m):
                ve.wait_ge(s_gu, m + 1)
                V.tensor_scalar(gmin, hg[:, :], LIMIT, None, ALU.min).then_inc(s_g, 1)
                V.tensor_scalar(ucl, hu[:, :], -LIMIT, LIMIT, ALU.max, ALU.min).then_inc(s_u, 1)
                ve.wait_ge(s_sig, m + 1)
                V.tensor_tensor(gsg, gmin, sig, ALU.mult).then_inc(s_gs, 1)
                ve.wait_ge(s_gs, m + 1)
                V.scalar_tensor_tensor(act, ucl, 1.0, gsg, ALU.add, ALU.mult).then_inc(s_act, 1)

            pick(0)
            block_tables()
            pick_gated(0)
            ve.wait_ge(s_xg, 1)
            gathered()
            pick(1)
            ve.wait_ge(s_cnt, 1)
            V.tensor_tensor(flag[:, 0:1], outb[:, 0:1], thr[:, :], ALU.is_gt).then_inc(s_fl, 1)
            ve.wait_ge(s_pi, 1)
            link(V.tensor_copy(flag[:, 1:2], outb[:, 1:2]))
            V.tensor_scalar(oh[:, :], iover[:, :], flag[:, 1:2], flag[:, 0:1], ALU.is_equal,
                            ALU.mult).then_inc(s_oh, 1)
            ve.wait_ge(s_tb, 1)
            link(V.tensor_copy(tabf[:, :], outb[0:1, 2:2 + 2 * MAXOVER + 1]))
            V.tensor_copy(tab[:, :], tabf[:, :]).then_inc(s_tab, 1)

            def main_item(n):
                swiglu(n)
                ve.wait_ge(s_xg, n + 2)
                gathered()
                pick(n + 2)
                ve.wait_ge(s_dnb, n + 1)
                pick_gated(n + 1)
            with ve.Fori(0, NE) as n:
                main_item(n)
            ve.wait_ge(s_tab, 1)
            over = ve.value_load(tab[0:1, 2 * MAXOVER:2 * MAXOVER + 1], min_val=0, max_val=MAXOVER - 1)
            with ve.If(over > 0):
                with ve.Fori(0, over) as i:
                    v = ve.value_load(tab[0:1, bass.ds(i, 1)], min_val=0, max_val=NV - 1)
                    ve.wait_ge(s_sca, i + NE)
                    ve.wait_ge(s_P, i + NE + 2)
                    ve.wait_ge(s_Pg, i + NE + 1)
                    pick(v)
                    pick_gated(v)
                    ve.wait_ge(s_xg, i + NE + 2)
                    gathered()
                    swiglu(i + NE)
            ve.wait_ge(s_fsq, 2)
            V.tensor_tensor(st[:, FS + 4:FS + 6], st[:, FS:FS + 4:2], st[:, FS + 1:FS + 4:2], ALU.add).then_inc(s_frm, 1)
            ve.wait_ge(s_wfin, 16)
            ve.wait_ge(s_fr, 1)
            link(V.reciprocal(st[:, FS + 8:FS + 10], st[:, FS + 6:FS + 8]))
            for t in range(TT):
                for hf in range(2):
                    ins = V.scalar_tensor_tensor(fin[:, t, hf * 512:(hf + 1) * 512], ybank[t][hf][:, :],
                                                 st[:, FS + 8 + t:FS + 9 + t], wfin[:, hf * 512:(hf + 1) * 512],
                                                 ALU.mult, ALU.mult)
                ins.then_inc(s_fin, 1)

        @block.tensor
        def _(pe):
            mm = E.matmul
            pe.wait_ge(c_ones, 1)
            pe.wait_ge(s_nm, 16)
            for half in range(2):
                ins = mm(B[4 + half][:, :], ones[0:1, :], nmr[:, half * 512:(half + 1) * 512], start=True, stop=True)
            ins.then_inc(s_nmp, 1)
            pe.wait_ge(c_id, 1)

            def transpose_x(src, t, banks, done):
                for j in range(KT):
                    if src is scr and j % 4 == 0:
                        pe.wait_ge(s_xs, 2 * t + j // 4 + 1)
                    ins = E.transpose(banks[2 * t + j // 4][:, (j % 4) * P:(j % 4 + 1) * P],
                                      src[:, t, j * P:(j + 1) * P], ident[:, :])
                    if j % 4 == 3:
                        ins.then_inc(done, 1)
            for t in range(TT):
                transpose_x(scr, t, B[0:4], s_xT)
            pe.wait_ge(s_vec, 80)
            E.transpose(B[4][:, 0:NVEC], vecs[:, :], ident[0:NVEC, 0:NVEC]).then_inc(s_vps, 1)
            pe.wait_ge(s_xl, 4)

            def split_product(out, lhs_hi, lhs_lo, rhs_hi, rhs_lo, start, stop):
                mm(out, lhs_hi, rhs_hi, start=start, stop=False)
                mm(out, lhs_hi, rhs_lo, start=False, stop=False)
                return mm(out, lhs_lo, rhs_hi, start=False, stop=stop)

            def small_projections():
                pe.wait_ge(s_sml2, 1)
                for t in range(TT):
                    rows = slice(t * P, (t + 1) * P)
                    for j in range(KT):
                        ins = split_product(B[5][:, t * 32:(t + 1) * 32], xh[:, j, rows], xl[:, j, rows],
                                            small_hi[:, j, :], small_lo[:, j, :], j == 0, j == KT - 1)
                ins.then_inc(s_sml, 1)

            def if_by_head():
                pe.wait_ge(s_ifs, 1)
                pe.wait_ge(s_vecT, 1)
                for k in range(2):
                    for t in range(TT):
                        ins = E.transpose(B[4][0:H_LSTM, k * T + t * P:k * T + (t + 1) * P],
                                          ifs[:, t, k * H_LSTM:(k + 1) * H_LSTM], ident[:, :])
                ins.then_inc(s_ift, 1)

            def bank_free(i):
                if i < N4:
                    if i >= 4:
                        pe.wait_ge(s_pe, i - 3)
                elif NQK <= i - 2:
                    pe.wait_ge(s_pa, i - 1 - NQK)
                elif i >= 2:
                    pe.wait_ge(s_pe, i - 1)

            def by_channel(i):
                u = i // 2
                pe.wait_ge(s_wl, u + 1)
                bank_free(i)
                cols = slice((i % 2) * P, (i % 2 + 1) * P)
                for j in range(KT):
                    ins = split_product(channel_bank(i)[:, 0:T], w_hi[u % NHB][:, j, cols], unit(ringr, u)[:, j, cols],
                                        xh[:, j, :], xl[:, j, :], j == 0, j == KT - 1)
                ins.then_inc(s_pj, 1)

            def by_token(n):
                i, u = NQK + n, NQK // 2 + n
                pe.wait_ge(s_wl, u + 1)
                bank_free(i)
                for t in range(TT):
                    rows = slice(t * P, (t + 1) * P)
                    for j in range(KT):
                        ins = split_product(B[6 + i % 2][:, t * UW:(t + 1) * UW], xh[:, j, rows], xl[:, j, rows],
                                            w_hi[u % NHB][:, j, :], unit(ringr, u)[:, j, :], j == 0, j == KT - 1)
                ins.then_inc(s_pj, 1)

            for i in range(NCH):
                by_channel(i)
                if i == 2:
                    small_projections()
                if i == I_TR:
                    if_by_head()

            def gates_by_token():
                pe.wait_ge(s_at, 1)
                pe.wait_ge(s_em, 1)
                pe.wait_ge(c_consts, 1)
                mm(B[5][:, 64:80], tri_gt[:, :], at[:, 0, :], start=True, stop=True)
                for a, row in ((0, 2), (1, 6)):
                    for t in range(TT):
                        ins = E.transpose(B[5][:, 80 + 16 * a + 8 * t:88 + 16 * a + 8 * t],
                                          gates[:, row, t * P:(t + 1) * P], ident[0:H_LSTM, 0:H_LSTM])
                ins.then_inc(s_gtp, 1)

            def xs_by_token():
                pe.wait_ge(s_cd, XT_TILES)
                for t in range(TT):
                    for c in range(XT_TILES):
                        ins = E.transpose(B[2 * t + c // 4][:, (c % 4) * P:(c % 4 + 1) * P],
                                          conv[:, c, t * P:(t + 1) * P], ident[:, :])
                        if c % 4 == 3:
                            ins.then_inc(s_xsp, 1)

            def c_dot_b():
                pe.wait_ge(s_cd, NCH)
                pe.wait_ge(s_gte, 1)
                for g in range(2):
                    bT, cT = conv[:, XT_TILES + g, :], conv[:, XT_TILES + 2 + g, :]
                    mm(B[4 + g][:, 0:P], bT[:, 0:P], cT[:, 0:P], start=True, stop=True)
                    mm(B[4 + g][:, 2 * P:3 * P], bT[:, 0:P], cT[:, P:T], start=True, stop=True)
                    mm(B[4 + g][:, P:2 * P], bT[:, P:T], cT[:, P:T], start=True, stop=True).then_inc(s_cbp, 1)
            for i in range(NCH, NQK):
                if i == I_GT:
                    gates_by_token()
                if i == I_XS:
                    xs_by_token()
                if i == I_CB:
                    c_dot_b()
                by_channel(i)
            pe.wait_ge(s_xse, 4)

            def seg(h):
                pe.wait_ge(s_au, 2 * (h // 4) + 2)
                if h >= 2:
                    pe.wait_ge(s_dec, h - 1)
                bank, a = B[h % 2], au[:, (h // 4) % 2, h % 4, :, :]
                mm(bank[:, 0:P], a[:, 0, :], tri_le[:, :], start=True, stop=True)
                mm(bank[:, P:2 * P], a[:, 1, :], tri_le[:, :], start=True, stop=True)
                mm(bank[:, 2 * P:3 * P], at[:, 1, h:h + 1].broadcast_to([P, P]), tri_le[:, :],
                   start=True, stop=True).then_inc(s_seg, 1)

            def ssd_product(h):
                pe.wait_ge(s_m, h + 1)
                if h == 8:
                    pe.wait_ge(s_yev, 2)
                w, c = dec[:, h % 3, :], (h % 8) * HD_SSM
                xd0, xd1 = (xd[:, t, h * HD_SSM:(h + 1) * HD_SSM] for t in range(TT))
                mm(B[2][:, c:c + HD_SSM], w[:, 0:P], xd0, start=True, stop=True)
                mm(B[3][:, c:c + HD_SSM], w[:, 2 * P:3 * P], xd0, start=True, stop=False)
                mm(B[3][:, c:c + HD_SSM], w[:, P:2 * P], xd1, start=False, stop=True).then_inc(s_y, 1)

            for n in range(H_SSM // 2):
                seg(2 * n)
                seg(2 * n + 1)
                by_token(n)
                ssd_product(2 * n)
                ssd_product(2 * n + 1)
            pe.wait_ge(s_yev, 4)

            def scores(h):
                if h < 2:
                    pe.wait_ge(s_dec, H_SSM)
                else:
                    pe.wait_ge(s_sc, h - 1)
                q = qT[:, h, :]
                mm(B[h % 2][:, 0:T], kT[:, h, 0:P], q, start=True, stop=True)
                mm(B[h % 2][:, T:T + P], kT[:, h, P:T], q[:, P:T], start=True, stop=True).then_inc(s_sp, 1)
                if h >= 2:
                    pe.wait_ge(s_ld, h - 1)
                gb = B[2 + h % 2]
                selh = ident[0:H_LSTM, h:h + 1].broadcast_to([H_LSTM, P])
                mm(gb[:, 0:T], selh, negG[:, :], start=True, stop=False)
                mm(gb[:, 0:P], identb[:, :], negm[:, :], start=False, stop=True)
                mm(gb[:, T:T + P], selh, negG[:, P:T], start=True, stop=False)
                mm(gb[:, T:T + P], identb[:, :], negm[:, :], start=False, stop=True).then_inc(s_gb, 1)

            def lstm_product(h):
                pe.wait_ge(s_sc, h + 1)
                if h < 2:
                    pe.wait_ge(s_pa, 4)
                else:
                    pe.wait_ge(s_hl, h - 1)
                w, nb = dec[:, h % 3, :], B[4 + h % 2]
                mm(nb[:, 0:VW], w[:, 0:P], v1[:, 0, h, :], start=True, stop=True)
                mm(nb[:, T:T + VW], w[:, P:2 * P], v1[:, 0, h, :], start=True, stop=False)
                mm(nb[:, T:T + VW], w[:, 2 * P:3 * P], v1[:, 1, h, :], start=False, stop=True).then_inc(s_num, 1)

            for n in range(H_LSTM // 2):
                scores(2 * n)
                scores(2 * n + 1)
                by_token(8 + n)
                lstm_product(2 * n)
                lstm_product(2 * n + 1)
            def router_logits(t):
                pe.wait_ge(s_hTv, t + 1)
                pe.wait_ge(s_hTa, 4 * t + 4)
                for j in range(KT):
                    ins = mm(B[2 * t][:, 0:NE], hT[:, j, t * P:(t + 1) * P], wr[:, j, :],
                             start=j == 0, stop=j == KT - 1)
                ins.then_inc(s_lgp, 1)

            def mix_transposes(r):
                if r < 2:
                    pe.wait_ge(s_hl, H_LSTM)
                else:
                    pe.wait_ge(s_mxe, r - 1)
                for jj in range(2):
                    c = 2 * r + jj
                    for t in range(TT):
                        src = yssm[:, t, c * P:(c + 1) * P] if c < 8 else hl[:, t, c - 8, :]
                        ins = E.transpose(B[4 + r % 2][:, jj * T + t * P:jj * T + (t + 1) * P], src, ident[:, :])
                ins.then_inc(s_mxp, 1)

            def out_product(c, t):
                g = N_IN + c // 4
                if c % 4 == 0 and t == 0:
                    pe.wait_ge(full[slot_of(g)], fills(g))
                src = mixA[:, c, :] if c < 8 else mixB[:, c - 8, :]
                for half in range(2):
                    o = (c % 4) * D + half * 512
                    ins = mm(B[2 * t + half][:, :], src[:, t * P:(t + 1) * P], ring[:, slot_of(g), o:o + 512],
                             start=c % 8 == 0, stop=c % 8 == 7)
                return ins
            pe.wait_ge(s_yg, 1)
            for c in range(8):
                if c % 2 == 0:
                    mix_transposes(c // 2)
                    pe.wait_ge(s_mxe, c // 2 + 1)
                if c == 0:
                    pe.wait_ge(s_sc, H_LSTM)
                for t in range(TT):
                    ins = out_product(c, t)
                if c % 4 == 3:
                    ins.then_inc((used, s_opa)[c // 4], 1)
            pe.wait_ge(s_hln, 1)
            for r in range(4, 8):
                mix_transposes(r)
            for t in range(TT):
                pe.wait_ge(s_ha, t + 1)
                for c in range(8, 16):
                    if t == 0 and c % 2 == 0:
                        pe.wait_ge(s_mxe, c // 2 + 1)
                    ins = out_product(c, t)
                    if t == TT - 1 and c == 11:
                        ins.then_inc(used, 1)
                    if t == TT - 1 and c == 12:
                        pe.wait_ge(s_h, 1)
                        transpose_x(x, 0, B[4:8], s_hTp)
                    if t == TT - 1 and c == 14:
                        router_logits(0)
                ins.then_inc(s_op, 1)
            pe.wait_ge(s_h, 2)
            pe.wait_ge(s_pa, 12)
            transpose_x(x, 1, B[4:8], s_hTp)
            router_logits(1)
            for t in range(TT):
                pe.wait_ge(s_lge, t + 1)
                for half in range(2):
                    mm(ybank[t][half][:, :], ident[:, :], x[:, t, half * 512:(half + 1) * 512], start=True, stop=False)
            pe.wait_ge(s_M, 2)
            mm(xb[:, 64:96], tri_lt[:, :], mall[:, 0, 0:NE], start=True, stop=True)
            mm(xb[:, 96:128], ones[:, :], mall[:, 0, 0:NE], start=True, stop=False)
            mm(xb[:, 96:128], tri_lt[:, :], mall[:, 1, 0:NE], start=False, stop=True).then_inc(s_pos, 1)

            def gather(p):
                pe.wait_ge(s_P, p)
                for j in range(KT):
                    for t in range(TT):
                        ins = mm(xb[:, j * SL:(j + 1) * SL], x[:, t, j * P:(j + 1) * P], Pm[:, t, :], start=t == 0, stop=t == TT - 1)
                ins.then_inc(s_xg, 1)

            def column_tiles(bank, lhsT, rhs, start, stop):
                for hf in range(2):
                    ins = mm(bank[hf * SL:(hf + 1) * SL, :], lhsT[hf], rhs[hf], start=start, stop=stop)
                return ins

            def gate_up(m, ready):
                pe.wait_ge(s_XT, ready)
                pe.wait_ge(s_Pg, ready)
                for bank, o in ((hg, 0), (hu, FF)):
                    column_tiles(bank, [sel] * 2, [biases[:, o:o + 512], biases[:, o + 512:o + 1024]], True, False)
                for j in range(KT):
                    s = EXP_SLOTS[j // 2]
                    if j % 2 == 0:
                        pe.wait_ge(full[s], expert_fills(j // 2, m))
                    lhsT = XT[:, j * SL:(j + 1) * SL]
                    for bank, o in ((hg, 0), (hu, FF)):
                        o += (j % 2) * 2 * FF
                        ins = column_tiles(bank, [lhsT] * 2, [ring[:, s, o:o + 512], ring[:, s, o + 512:o + 1024]],
                                           False, j == KT - 1)
                    if j % 2:
                        ins.then_inc(used if j < KT - 1 else s_gu, 1)

            def transpose_gates():
                for t in range(TT):
                    ins = E.transpose(outb[:, t * P:(t + 1) * P], Pg[:, t, :], ident[:, :])
                ins.then_inc(s_pt, 1)

            def down(m):
                pe.wait_ge(s_act, m + 1)
                for q in range(4):
                    ins = E.transpose(hg[:, q * P:(q + 1) * P], act[:, q * P:(q + 1) * P], ident[:, :])
                ins.then_inc(s_atp, 1)
                pe.wait_ge(s_ptg, m + 1)
                column_tiles(outb, [sel] * 2, [biases[:, 2 * FF:2 * FF + 512], biases[:, 2 * FF + 512:3 * FF]],
                             True, False).then_inc(s_dnb, 1)
                pe.wait_ge(s_aT, m + 1)
                for f in range(8):
                    s = EXP_SLOTS[4 + f // 4]
                    if f % 4 == 0:
                        pe.wait_ge(full[s], expert_fills(4 + f // 4, m))
                    q, half = f % 4, f // 4
                    lhsT = actT[:, q * P + half * SL:q * P + (half + 1) * SL]
                    o = q * D
                    ins = column_tiles(outb, [lhsT] * 2, [ring[:, s, o:o + 512], ring[:, s, o + 512:o + 1024]],
                                       False, f == 7)
                    if f % 4 == 3:
                        ins.then_inc(used if f < 7 else s_dn, 1)

            def scatter(m, last=False, again=False):
                pe.wait_ge(s_os, m + 1)
                for t in range(TT):
                    for hf in range(2):
                        rows = slice(hf * SL, (hf + 1) * SL)
                        ins = mm(ybank[t][hf][:, :], PTg[rows, t, :], outS[rows, :], start=False, stop=last,
                                 skip_group_check=again)
                ins.then_inc(s_sca, 1)

            gather(1)
            pe.wait_ge(s_bias, 32)

            def main_item(m, first=False):
                gate_up(m, m + 1)
                if first:
                    for t in range(TT):
                        ins = mm(outb[:, 0:1], mall[:, t, :], ones[:, 0:1], start=t == 0, stop=t == TT - 1)
                    ins.then_inc(s_cnt, 1)
                    pe.wait_ge(s_fl, 1)
                    mm(outb[:, 1:2], tri_lt[:, :], flag[:, 0:1], start=True, stop=True).then_inc(s_pi, 1)
                    pe.wait_ge(s_oh, 1)
                    mm(outb[0:1, 2:2 + MAXOVER], ipart[:, :], oh[:, :], start=True, stop=True)
                    mm(outb[0:1, 2 + MAXOVER:2 + 2 * MAXOVER], vmod[:, :], oh[:, :], start=True, stop=True)
                    mm(outb[0:1, 2 + 2 * MAXOVER:3 + 2 * MAXOVER], flag[:, 0:1], ones[:, 0:1], start=True,
                       stop=True).then_inc(s_tb, 1)
                    pe.wait_ge(s_tab, 1)
                else:
                    scatter(m - 1)
                transpose_gates()
                gather(m + 2)
                down(m)

            main_item(0, first=True)
            with pe.Fori(1, NE) as n:
                main_item(n)
            scatter(NE - 1, last=True)
            over = pe.value_load(tab[0:1, 2 * MAXOVER:2 * MAXOVER + 1], min_val=0, max_val=MAXOVER - 1)
            with pe.If(over > 0):
                with pe.Fori(0, over) as i:
                    gather(i + NE + 3)
                    gate_up(i + NE, i + NE + 2)
                    transpose_gates()
                    down(i + NE)
                    scatter(i + NE, last=True, again=True)


_INS = ['x', 'norm_mix_w', 'w_in', 'conv_w', 'conv_b', 'dt_bias', 'a_log', 'd_skip', 'ssm_norm_w', 'lstm_i_bias',
        'lstm_f_bias', 'lstm_norm_w', 'w_out', 'norm_ffn_w', 'w_router', 'b_router', 'w_gate_up', 'b_gate_up',
        'w_down', 'b_down', 'norm_final_w']


def kernel(**inputs):
    import numpy as _np
    import concourse.bacc as _bacc
    from concourse import mybir as _mybir
    from concourse.bass_utils import run_bass_kernel_spmd as _run

    nc = _bacc.Bacc("TRN2", target_bir_lowering=False, num_devices=1)
    arrays, args = {}, []
    for name in _INS:
        a = _np.ascontiguousarray(inputs[name])
        arrays[f"in_{name}_dram"] = a
        args.append(nc.dram_tensor(f"in_{name}_dram", a.shape, _mybir.dt.from_np(a.dtype), kind="ExternalInput").ap())
    args.append(nc.dram_tensor("out_0_dram", (1, T, D), _mybir.dt.float32, kind="ExternalOutput").ap())
    hybrid_block(nc, *args)
    r = _run(nc, [arrays], core_ids=[0])
    return r.results[0]["out_0_dram"]
```

```python
import concourse.bass as bass
from concourse import mybir
from contextlib import ExitStack

P = 128
D = 1024
T = 256
TT = T // P
KT = D // P
H_SSM, HD_SSM = 16, 64
H_LSTM, HD_LSTM = 8, 128
W_SSM = H_SSM * HD_SSM
CONV_DIM = 1536
CONV_W = 4
NCH = CONV_DIM // P
XT_TILES = W_SSM // P
IN_DIM = 6688
COL_Z, COL_XBC, COL_DT = 0, 1024, 2560
COL_Q, COL_K, COL_V, COL_O, COL_I = 2576, 3600, 4624, 5648, 6672
NE = 32
TOPK = 4
FF = 1024
LIMIT, ALPHA = 7.0, 1.702
EPS = 1e-6
SL = 64
NBLK = T // SL
NV = NE * NBLK
MAXOVER = 16

SLOTS = 6
MSLOTS = 4
EXP_SLOTS = (1, 2, 3, 4, 0, 5)
NA = 2
FIRST, SECOND = 0, 1
SLOTW = 4096
CW = SLOTW // KT
UW = CW // 2
NHB = 3
IN_COLS = ([COL_XBC + CW * i for i in range(3)] + [c + CW * i for c in (COL_Q, COL_K, COL_V, COL_Z, COL_O)
                                                   for i in range(2)])
NQK = NCH + 2 * H_LSTM
N_IN = len(IN_COLS)
N4 = NCH + 8
I_TR, I_GT, I_XS, I_CB = NCH + 7, NCH + 12, NCH + 13, NCH + 15
NS = H_SSM + 2 * H_LSTM
N_OUT = 4
POOL_IN_UNITS = (4, 6)
UO = 2 * N_OUT
POOL_UNITS = (5, 7)
N_MIX = N_IN + N_OUT
CPE = 6
RSQRT_D = 1.0 / D
QK_SCALE = float(HD_LSTM) ** -0.5
BIG = 1e30


def hybrid_block(nc, x_d, norm_mix_w, w_in, conv_w, conv_b, dt_bias, a_log, d_skip, ssm_norm_w,
                 lstm_i_bias, lstm_f_bias, lstm_norm_w, w_out, norm_ffn_w, w_router, b_router,
                 w_gate_up, b_gate_up, w_down, b_down, norm_final_w, out_d):
    f32, f32r, bf16, i32, u32 = (mybir.dt.float32, mybir.dt.float32r, mybir.dt.bfloat16, mybir.dt.int32,
                                 mybir.dt.uint32)
    ALU, ACT, AX = mybir.AluOpType, mybir.ActivationFunctionType, mybir.AxisListType
    V, S, G, E = nc.vector, nc.scalar, nc.gpsimd, nc.tensor
    ctx = ExitStack()
    with ctx:
        def sb(name, shape, dt=f32):
            return ctx.enter_context(nc.sbuf_tensor(name, shape, dt))

        def sem(name):
            return ctx.enter_context(nc.semaphore(name))

        with (nc.sbuf_tensor("ringr", [P, SLOTS, SLOTW], f32r) as ringr,
              nc.sbuf_tensor("smallr", [P, KT, 32], f32r) as small_lo,
              nc.sbuf_tensor("xl", [P, KT, T], f32r) as xl,
              nc.sbuf_tensor("negG_lo", [H_LSTM, T], f32r) as negG_lo,
              nc.sbuf_tensor("mix_hi", [P, KT, T], f32r) as mix_hi,
              nc.sbuf_tensor("mix_lo", [P, KT, T], f32r) as mix_lo):
            pass
        ring = sb("ring", [P, SLOTS, SLOTW])
        small = sb("small", [P, KT, 32])
        fin = sb("fin", [P, TT, D])
        hT = fin[:, :, :].rearrange("p a b -> p (a b)").rearrange("p (j t) -> p j t", j=KT)
        negG = sb("negG", [H_LSTM, T])
        qk = sb("qk", [P, 2 * KT * T])
        qT, kT = (qk[:, n * KT * T:(n + 1) * KT * T].rearrange("p (j t) -> p j t", j=KT) for n in range(2))
        small_hi = sb("small_hi", [P, KT, 32], f32r)
        negG_hi = sb("negG_hi", [H_LSTM, T], f32r)
        identr = sb("identr", [H_LSTM, H_LSTM], f32r)
        halves = [ringr[:, MSLOTS + b // 2, (b % 2) * KT * UW:(b % 2 + 1) * KT * UW] for b in range(4)]
        w_hi = [halves[b].rearrange("p (j n) -> p j n", j=KT) for b in (1, 2, 0)]
        xh = halves[3].rearrange("p (j t) -> p j t", j=KT)
        x = sb("x", [P, TT, D])
        conv = sb("conv", [P, NCH, T])
        convf = conv[:, :, :].rearrange("p a b -> p (a b)")
        hl = convf[:, 0:TT * D].rearrange("p (t h d) -> p t h d", t=TT, h=H_LSTM)
        nmr = convf[0:1, D:2 * D]
        xy = sb("xy", [P, 2 * TT * D])
        xd, yssm = (xy[:, n * TT * D:(n + 1) * TT * D].rearrange("p (t d) -> p t d", t=TT) for n in range(2))
        og = xd
        VW = HD_LSTM + 1
        vz = sb("vz", [P, TT * H_LSTM * VW + TT * D])
        v1 = vz[:, 0:TT * H_LSTM * VW].rearrange("p (t h d) -> p t h d", t=TT, h=H_LSTM)
        z = vz[:, TT * H_LSTM * VW:].rearrange("p (t d) -> p t d", t=TT)
        biases = vz[:, 0:3 * FF]
        wfin = vz[:, 3 * FF:3 * FF + D]
        annex = [xy, qk]
        raw = sb("raw", [P, 3, CONV_W - 1 + T])
        csig = sb("csig", [P, 2, T])
        cbm = sb("cbm", [P, 2, 3 * P])
        dec = sb("dec", [P, 3, 3 * P])
        au = sb("au", [P, 2, 4, TT, P])
        auf = au[:, :, :, :, :].rearrange("p a b c d -> p (a b c d)")
        scr = auf.rearrange("p (t d) -> p t d", t=TT)
        wr = sb("wr", [P, KT, NE])
        NVEC = CONV_W * NCH + NCH + 3 * KT
        vecs = sb("vecs", [NVEC, P])
        vecT = sb("vecT", [P, NVEC])
        OFF_CB = CONV_W * NCH
        OFF_SN, OFF_LN, OFF_FN = (OFF_CB + NCH + KT * i for i in range(3))
        nfw = vecT[:, OFF_FN:OFF_FN + KT]
        smb = sb("smb", [P, NS])
        alog = sb("alog", [P, H_SSM])
        dsk = sb("dsk", [P, H_SSM])
        br = sb("br", [P, NE])
        ident = sb("ident", [P, P])
        identb = sb("identb", [P, P], bf16)
        negm = sb("negm", [P, P], bf16)
        tri_le = sb("tri_le", [P, P])
        tri_gt = sb("tri_gt", [P, P])
        tri_lt = sb("tri_lt", [P, P])
        ones = sb("ones", [P, P])
        selall = sb("selall", [P, NBLK, NE])
        islot = sb("islot", [P, 2, SL])
        ie = sb("ie", [P, NE])
        iover = ie[:, 0:MAXOVER]
        ipart = sb("ipart", [P, 1])
        vmod = sb("vmod", [P, 1])
        thr = sb("thr", [P, 1])
        epst = sb("epst", [P, 1])
        st = sb("st", [P, 32])
        XS, YS, HS, FS = 0, 6, 12, 18
        junk = csig[:, :, :].rearrange("p a (b d) -> p a b d", b=2)
        ls = sb("ls", [P, 6, TT, H_LSTM])
        dsp = sb("dsp", [P, 7, TT * NS])
        dtt = sb("dtt", [P, TT, H_SSM])
        at = sb("at", [P, TT, H_SSM])
        r0 = sb("r0", [P, H_SSM])
        smT = xy[0:NS, 7 * T:8 * T]
        gates = xy[0:H_LSTM, 0:7 * T].rearrange("h (r t) -> h r t", r=7)
        agT = sb("agT", [P, 2, TT, H_LSTM])
        XT = convf[:, 0:512]
        act = convf[:, 512:1024]
        gmin = convf[:, 1024:1536]
        sig = convf[:, 1536:2048]
        actT = convf[:, 2048:2560]
        outS = convf[:, 2560:3072]
        ucl = raw[:, :, :].rearrange("p a b -> p (a b)")[:, 0:512]
        gsg = csig[:, :, :].rearrange("p a b -> p (a b)")
        decf = dec[:, :, :].rearrange("p a b -> p (a b)")
        Pm = decf[:, 0:TT * SL].rearrange("p (t s) -> p t s", t=TT)
        Pg = decf[:, 128:128 + TT * 2 * SL].rearrange("p (t s) -> p t s", t=TT)
        PTg = decf[:, 384:384 + TT * P].rearrange("p (t s) -> p t s", t=TT)
        sel = decf[:, 640:640 + SL]
        posm, gall, mall = (auf[:, n * TT * NV:(n + 1) * TT * NV].rearrange("p (t v) -> p t v", t=TT) for n in range(3))
        lg = sb("lg", [P, TT, NE])
        top = sb("top", [P, TT, 8])
        tidx = sb("tidx", [P, TT, 8], u32)
        tidf = sb("tidf", [P, TT, 8])
        sm = sb("sm", [P, TT, 8])
        eq = auf[:, 768:1024].rearrange("p (t k e) -> p t k e", t=TT, k=TOPK)
        eqg = auf[:, 1024:1152].rearrange("p (k e) -> p k e", k=TOPK)
        flag = sb("flag", [P, 4])
        oh = sb("oh", [P, MAXOVER])
        tabf = sb("tabf", [1, 2 * MAXOVER + 1])
        tab = sb("tab", [1, 2 * MAXOVER + 1], i32)

        B = [ctx.enter_context(nc.psum_tensor(f"bank{i}", [P, 512], f32)) for i in range(8)]
        ybank = [[B[2], B[3]], [B[0], B[1]]]
        hg, hu, outb, xb = B[4], B[5], B[6], B[7]
        hT_banks = [B[2:4], B[4:6]]

        s_x = [sem(f"x_loaded{t}") for t in range(TT)]
        s_first = sem("first_unit_loaded")
        s_nm, s_small, s_vec, s_par = sem("norm_mix_loaded"), sem("small_loaded"), sem("vecs_loaded"), sem("params_loaded")
        s_bias, s_wfin, s_out = sem("biases_loaded"), sem("final_weight_loaded"), sem("output_stored")
        full = [sem(f"slot_full{i}") for i in range(SLOTS)]
        s_piece = [sem(f"last_chunk_piece{q}") for q in range(3)]
        s_annex = [sem(f"annex_full{c}") for c in range(NA)]
        used = sem("chunks_used")
        c_pool, c_eps, c_id, c_ones, c_consts = sem("pool_chain"), sem("eps_ready"), sem("ident_ready"), sem("ones_ready"), sem("consts_ready")
        s_rms, s_rx, s_xs, s_xT, s_xh, s_xl, s_smh, s_sml2, s_wh, s_wl, s_wlp = (sem(n) for n in (
            "x_rms", "x_rstd", "x_scaled", "xT_psum", "xT_high", "xT_low", "small_high", "small_low",
            "w_in_high", "w_in_low", "w_in_low_by_pool"))
        s_nmp, s_vps, s_vecT = sem("norm_mix_psum"), sem("vecs_psum"), sem("vecT_ready")
        s_smp, s_smc, s_sml, s_ift, s_dt, s_spin, s_spln, s_spd, s_expa, s_at, s_gh, s_em, s_ngh, s_ngl, s_gtp, s_gte, s_au = (sem(n) for n in (
            "small_projected", "small_evicted", "small_by_token", "if_by_head", "small_biased", "softplus_in", "softplus_ln", "softplus_done", "exp_a_log", "a_ready", "gates_by_head",
            "exp_neg_m", "neg_G_high", "neg_G_low", "gates_psum", "gates_by_token", "au_ready"))
        s_pj, s_pe, s_pa, s_raw, s_cv, s_cs, s_cd = (sem(n) for n in (
            "proj_psum", "channels_evicted", "tokens_evicted", "first_tap_ready", "conv_sum", "conv_sigmoid",
            "conv_done"))
        s_xsp, s_xse, s_cbp, s_cbe, s_seg, s_dec, s_m, s_y, s_yev = (sem(n) for n in (
            "xs_psum", "xs_evicted", "cb_psum", "cb_evicted", "seg_psum", "ssd_decay", "ssd_weights",
            "ssd_y_psum", "ssd_y_evicted"))
        s_sp, s_gb, s_ld, s_sc, s_num, s_hl = (sem(n) for n in (
            "scores_psum", "maxima_psum", "lstm_decay", "lstm_weights", "num_psum", "hl_ready"))
        s_zs, s_yg, s_yr, s_nsq, s_osg, s_lr, s_lm, s_hln, s_mxp, s_mxh, s_mxe, s_woh, s_wol, s_wop, s_ou, s_ha, s_op, s_h = (sem(n) for n in (
            "z_sigmoid", "y_gated", "y_rms", "num_squares", "o_sigmoid", "head_variance", "head_rms", "hlstm_ready",
            "mixed_psum", "mixed_high", "mixed_low", "w_out_high", "w_out_low", "w_out_low_by_pool", "w_out_units_used", "h_ssm_added", "out_proj_psum", "h_ready"))
        s_rm3, s_fr, s_lge, s_hTp, s_hTv, s_hTa, s_lgp, s_tp, s_se, s_M, s_pos, s_cnt, s_fl, s_pi, s_oh, s_tb, s_tab, s_tabs = (
            sem(n) for n in ("h_rms", "final_rms", "logits_evicted", "hT_psum", "hT_by_dve", "hT_by_act", "logits_psum", "top_ready",
                             "softmax_exp", "selection_ready", "positions_psum", "counts_psum", "flags_ready",
                             "item_positions_psum", "item_onehot", "table_psum", "table_ready", "block_tables"))
        s_P, s_Pg, s_xg, s_XT, s_gu, s_g, s_sig, s_gs, s_act, s_pt, s_ptg, s_atp, s_aT, s_dnb, s_dn, s_os, s_sca0, s_sca = (
            sem(n) for n in ("P_ready", "Pg_sel_ready", "gathered_psum", "XT_ready", "gate_up_psum", "gate_clipped",
                             "gate_sigmoid", "swish_ready", "act_ready", "PT_psum", "PT_ready",
                             "actT_psum", "actT_ready", "down_bias_done", "down_psum", "out_scaled", "scattered_tile_0", "scattered"))
        s_fsq, s_frm, s_fin = sem("final_squares"), sem("final_sums"), sem("final_ready")
        c_dve, c_act = sem("dve_chain"), sem("act_chain")

        def chain(engine, semaphore):
            count = [0]

            def link(ins):
                count[0] += 1
                ins.then_inc(semaphore, 1)
                engine.wait_ge(semaphore, count[0])
            return link

        def slot_of(g):
            return g % MSLOTS

        def fills(g):
            return 16 * (g // MSLOTS + 1)

        def is_item(m, n):
            return isinstance(m, int) and m == n

        def expert_slot(m, c):
            return EXP_SLOTS[c if is_item(m, FIRST) else (c - NA) % SLOTS]

        def expert_fills(m, c):
            s = expert_slot(m, c)
            before = sum(slot_of(g) == s for g in range(N_MIX))
            return 16 * (before + 1) if is_item(m, FIRST) else 16 * m + 16 * (before + (c >= NA))

        def in_annex(m, c):
            return is_item(m, SECOND) and c < NA

        def expert_chunk(m, c):
            return annex[c] if in_annex(m, c) else ring[:, expert_slot(m, c), :]

        def channel_bank(i):
            return B[(6, 7, 0, 1)[i % 4]] if i < N4 else B[6 + i % 2]

        def unit(tensor, u):
            chunk = tensor[:, slot_of(u // 2), :].rearrange("p (j n) -> p j n", j=KT)
            return chunk[:, :, (u % 2) * UW:(u % 2 + 1) * UW]

        tile_cols = (slice(0, P), slice(P, 2 * P))

        def out_unit(tensor, u):
            return tensor[:, slot_of(N_IN + u // 2), (u % 2) * 2 * D:(u % 2 + 1) * 2 * D]

        w_in_v = w_in[0].rearrange("(j p) n -> p j n", p=P)
        w_out_v = w_out[0].rearrange("(j p) n -> p j n", p=P)
        wgu_v = w_gate_up[0].rearrange("e (j p) n -> e p j n", p=P)
        wdn_v = w_down[0].rearrange("e (j p) n -> e p j n", p=P)

        block = ctx.enter_context(nc.Block())

        @block.sync
        def _(sp):
            sp.dma_start(nmr, norm_mix_w).then_inc(s_nm, 16)
            for t in range(TT):
                sp.dma_start(x[:, t, :], x_d[0, t * P:(t + 1) * P, :]).then_inc(s_x[t], 16)
            def mixer_chunk_used(g):
                if g < 7:
                    sp.wait_ge(s_pj, 4 * (g + 1))
                elif g < N_IN:
                    sp.wait_ge(s_pj, 28 + 2 * (g - 6))
                else:
                    sp.wait_ge(*((s_ou, 2), (s_ou, 4), (s_ou, 5), (s_op, 2))[g - N_IN])

            for g in range(N_MIX):
                if g >= MSLOTS:
                    mixer_chunk_used(g - MSLOTS)
                if g < N_IN:
                    c = IN_COLS[g]
                    dst = ring[:, slot_of(g), :].rearrange("p (j n) -> p j n", j=KT)
                    if g:
                        sp.dma_start(dst, w_in_v[:, :, c:c + CW]).then_inc(full[slot_of(g)], 16)
                    else:
                        sp.dma_start(dst[:, :, 0:UW], w_in_v[:, :, c:c + UW]).then_inc(s_first, 16)
                        sp.dma_start(dst[:, :, UW:], w_in_v[:, :, c + UW:c + CW]).then_inc(full[0], 16)
                        sp.dma_start(small[:, :, 0:16], w_in_v[:, :, COL_DT:COL_DT + 16]).then_inc(s_small, 16)
                        sp.dma_start(small[:, :, 16:32], w_in_v[:, :, COL_I:COL_I + 16]).then_inc(s_small, 16)
                        sp.dma_start(vecs[0:OFF_CB, :], conv_w[0].rearrange("w (c p) -> (w c) p", p=P)).then_inc(s_vec, 16)
                        for off, rows, v in ((OFF_CB, NCH, conv_b), (OFF_SN, KT, ssm_norm_w), (OFF_LN, KT, lstm_norm_w),
                                             (OFF_FN, KT, norm_ffn_w)):
                            sp.dma_start(vecs[off:off + rows, :], v[0].rearrange("(c p) -> c p", p=P)).then_inc(s_vec, 16)
                    if g == 1:
                        for o, v, n in ((0, dt_bias, H_SSM), (H_SSM, lstm_i_bias, H_LSTM),
                                        (H_SSM + H_LSTM, lstm_f_bias, H_LSTM)):
                            sp.dma_start(smb[:, o:o + n], v.broadcast_to([P, n])).then_inc(s_par, 16)
                        sp.dma_start(alog[:, :], a_log.broadcast_to([P, H_SSM])).then_inc(s_par, 16)
                        sp.dma_start(dsk[:, :], d_skip.broadcast_to([P, H_SSM])).then_inc(s_par, 16)
                        sp.dma_start(wr[:, :, :], w_router[0].rearrange("(j p) n -> p j n", p=P)).then_inc(s_par, 16)
                        sp.dma_start(br[:, :], b_router.broadcast_to([P, NE])).then_inc(s_par, 16)
                else:
                    k = g - N_IN
                    dst = ring[:, slot_of(g), :].rearrange("p (j n) -> p j n", j=4)
                    sp.dma_start(dst, w_out_v[:, 4 * k:4 * k + 4, :]).then_inc(full[slot_of(g)], 16)

            def slot_released(m, c):
                if is_item(m, FIRST):
                    mixer_chunk_used(N_IN + (0, 1, 2, 2, 3, 3)[c])
                elif is_item(m, SECOND) and c == 0:
                    sp.wait_ge(s_hln, 4)
                    sp.wait_ge(s_mxp, 4)
                elif is_item(m, SECOND) and c == 1:
                    sp.wait_ge(s_op, 2)
                else:
                    if is_item(m, SECOND):
                        n, c = m, c - NA
                    elif is_item(m, 2) and c < NA:
                        n, c = 1, c + 4
                    else:
                        n = m
                    if c == 3:
                        sp.wait_ge(s_gu, n)
                    elif c == 5:
                        sp.wait_ge(s_dn, n)
                    else:
                        sp.wait_ge(used, 4 * n + (-3, -2, -1, 0, 0)[c])

            def load_last_chunk():
                m, c = NE - 1, CPE - 1
                slot_released(m, c)
                for q in range(4):
                    done = s_piece[q] if q < 3 else full[expert_slot(m, c)]
                    sp.dma_start(expert_chunk(m, c)[:, q * D:(q + 1) * D],
                                 w_down[0, m, (4 + q) * P:(5 + q) * P, :]).then_inc(done, 16)

            def load_chunk(m, e, c):
                slot_released(m, c)
                if c < 4:
                    src = wgu_v[bass.ds(e, 1), :, 2 * c:2 * c + 2, :].rearrange("e p j n -> (e p) j n")
                else:
                    src = wdn_v[bass.ds(e, 1), :, 4 * (c - 4):4 * (c - 4) + 4, :].rearrange("e p j n -> (e p) j n")
                dst = expert_chunk(m, c).rearrange("p (j n) -> p j n", j=2 if c < 4 else 4)
                sp.dma_start(dst, src).then_inc(s_annex[c] if in_annex(m, c) else full[expert_slot(m, c)], 16)

            for m, c in ((0, 0), (0, 1), (1, 0), (0, 2), (0, 3), (0, 4), (0, 5), (1, 1), (1, 2), (1, 3), (1, 4), (1, 5)):
                load_chunk(m, m, c)
            for c in range(CPE):
                load_chunk(2, 2, c)
            with sp.Fori(3, NE - 1) as n:
                for c in range(CPE):
                    load_chunk(n, n, c)
            for c in range(CPE - 1):
                load_chunk(NE - 1, NE - 1, c)
            load_last_chunk()
            sp.wait_ge(s_tab, 1)
            over = sp.value_load(tab[0:1, 2 * MAXOVER:2 * MAXOVER + 1], min_val=0, max_val=MAXOVER - 1)
            with sp.If(over > 0):
                with sp.Fori(0, over) as i:
                    e = sp.value_load(tab[0:1, bass.ds(i + MAXOVER, 1)], min_val=0, max_val=NE - 1)
                    for c in range(CPE):
                        load_chunk(i + NE, e, c)
            for t in range(TT):
                for half in range(2):
                    sp.wait_ge(s_fin, 2 * t + half + 1)
                    cols = slice(half * 512, (half + 1) * 512)
                    sp.dma_start(out_d[0, t * P:(t + 1) * P, cols], fin[:, t, cols]).then_inc(s_out, 16)
            sp.wait_ge(s_out, 16 * 2 * TT)

        @block.gpsimd
        def _(pool):
            link = chain(pool, c_pool)
            G.memset(epst[:, :], EPS).then_inc(c_eps, 1)
            G.memset(ones[:, :], 1.0).then_inc(c_ones, 1)
            link(G.memset(ident[:, :], 0.0))
            G.affine_select(out=ident[:, :], in_=ident[:, :], compare_op=ALU.not_equal, fill=1.0, base=0,
                            pattern=[[-1, P]], channel_multiplier=1).then_inc(c_id, 1)
            for m, val in ((identb, 0.0), (negm, 0.0), (tri_le, 1.0), (tri_gt, 1.0), (tri_lt, 1.0), (selall, 0.0)):
                last = G.memset(m[:], val)
            link(last)

            def diagonal(m, op, fill, channel, pattern, base=0):
                return G.affine_select(out=m, in_=m, compare_op=op, fill=fill, base=base, pattern=pattern,
                                       channel_multiplier=channel)
            diagonal(identb[:, :], ALU.not_equal, 1.0, 1, [[-1, P]])
            diagonal(negm[:, :], ALU.is_ge, -BIG, -1, [[1, P]])
            diagonal(tri_le[:, :], ALU.is_ge, 0.0, -1, [[1, P]])
            diagonal(tri_lt[:, :], ALU.is_gt, 0.0, -1, [[1, P]])
            diagonal(tri_gt[:, :], ALU.is_gt, 0.0, 1, [[-1, P]])
            diagonal(selall[:, :, :], ALU.not_equal, 1.0, 1, [[0, NBLK], [-1, NE]])
            G.memset(raw[:, :, 0:CONV_W - 1], 0.0)
            G.iota(islot[:, :, :], pattern=[[0, 2], [1, SL]], base=1, channel_multiplier=0,
                   allow_small_or_imprecise_dtypes=True)
            G.iota(ie[:, :], pattern=[[1, NE]], base=0, channel_multiplier=0, allow_small_or_imprecise_dtypes=True)
            link(G.iota(ipart[:, :], pattern=[[0, 1]], base=0, channel_multiplier=1,
                        allow_small_or_imprecise_dtypes=True))
            for b in range(NBLK):
                rows = slice(b * NE, (b + 1) * NE)
                link(G.memset(thr[rows, :], float(b * SL) if b else BIG))
                link(G.iota(vmod[rows, :], pattern=[[0, 1]], base=0, channel_multiplier=1,
                            allow_small_or_imprecise_dtypes=True))
            G.memset(gates[:, 5, :], 1.0)
            G.memset(v1[:, :, :, HD_LSTM:VW], 1.0).then_inc(c_consts, 1)
            for u in POOL_IN_UNITS:
                pool.wait_ge(s_wh, u + 2)
                G.tensor_tensor(unit(ringr, u), unit(ring, u), w_hi[u % NHB], ALU.subtract).then_inc(s_wlp, 1)
            pool.wait_ge(s_at, 1)
            for g in range(4):
                if g >= 2:
                    pool.wait_ge(s_seg, 4 * (g - 1))
                for t in range(TT):
                    G.tensor_tensor(au[:, g % 2, :, t, :],
                                    tri_gt[:, :].unsqueeze(1).broadcast_to([P, 4, P]),
                                    at[:, t, 4 * g:4 * g + 4].unsqueeze(2).broadcast_to([P, 4, P]),
                                    ALU.mult).then_inc(s_au, 1)
            pool.wait_ge(s_yg, 1)
            pool.wait_ge(s_num, H_LSTM)
            link(G.memset(biases, 0.0))
            pool.dma_start(biases[0:NE, 0:2 * FF], b_gate_up[0]).then_inc(s_bias, 16)
            pool.dma_start(biases[0:NE, 2 * FF:3 * FF], b_down[0]).then_inc(s_bias, 16)
            pool.dma_start(wfin, norm_final_w.unsqueeze(0).broadcast_to([P, D])).then_inc(s_wfin, 16)
            for u in POOL_UNITS:
                pool.wait_ge(s_woh, u + 1)
                G.tensor_tensor(out_unit(ringr, u), out_unit(ring, u), halves[u % 4], ALU.subtract).then_inc(s_wop, 1)

        @block.scalar
        def _(ac):
            link = chain(ac, c_act)

            def rms(dst, src):
                return S.activation(dst, src, ACT.Sqrt, scale=RSQRT_D, bias=epst[:, :])
            ac.wait_ge(c_eps, 1)
            S.activation(st[:, 31:32], epst[:, :], ACT.Sqrt)
            for t in range(TT):
                ac.wait_ge(s_x[t], 16)
                link(S.activation(convf[:, 0:D], x[:, t, :], ACT.Square, accum_out=st[:, XS + t:XS + t + 1]))
                rms(st[:, XS + 2 + t:XS + 3 + t], st[:, XS + t:XS + t + 1]).then_inc(s_rms, 1)
            def w_high(u):
                ac.wait_ge(full[slot_of(u // 2)], fills(u // 2))
                if u >= NHB:
                    v = u - NHB
                    ac.wait_ge(s_pj, 2 * (v + 1) if 2 * v < NQK else NQK + v - NQK // 2 + 1)
                S.activation(w_hi[u % NHB], unit(ring, u), ACT.Copy).then_inc(s_wh, 1)
            for t in range(TT):
                for b in range(2):
                    ac.wait_ge(s_xT, 2 * t + b + 1)
                    S.activation(xh[:, 4 * b:4 * b + 4, t * P:(t + 1) * P],
                                 B[2 * t + b][:, :].rearrange("p (j t) -> p j t", j=4), ACT.Copy).then_inc(s_xh, 1)
                if t == 0:
                    ac.wait_ge(s_first, 16)
                cols = tile_cols[t]
                S.activation(w_hi[0][:, :, cols], unit(ring, 0)[:, :, cols], ACT.Copy).then_inc(s_wh, 1)

            ac.wait_ge(s_small, 32)
            S.activation(small_hi[:, :, :], small[:, :, :], ACT.Copy).then_inc(s_smh, 1)
            w_high(1)

            def conv_sigmoid(c):
                ac.wait_ge(s_cv, c + 1)
                if c >= 2:
                    ac.wait_ge(s_cd, c - 1)
                S.activation(csig[:, c % 2, :], conv[:, c, :], ACT.Sigmoid).then_inc(s_cs, 1)
            ac.wait_ge(s_vecT, 1)
            ac.wait_ge(c_consts, 1)
            for i in range(NQK):
                if i % 2 == 0:
                    w_high(i // 2 + 2)
                ac.wait_ge(s_pj, i + 1)
                bank = channel_bank(i)[:, 0:T]
                if i < NCH:
                    if i >= 3:
                        ac.wait_ge(s_cv, i - 2)
                    S.activation(raw[:, i % 3, CONV_W - 1:], bank, ACT.Copy).then_inc(s_pe, 1)
                    if i:
                        conv_sigmoid(i - 1)
                    ac.wait_ge(s_pe, i + 1)
                    S.activation(conv[:, i, :], raw[:, i % 3, 0:T], ACT.Identity, scale=vecT[:, i:i + 1],
                                 bias=vecT[:, OFF_CB + i:OFF_CB + i + 1]).then_inc(s_raw, 1)
                else:
                    h = i - NCH
                    dst = qT[:, h, :] if h < H_LSTM else kT[:, h - H_LSTM, :]
                    S.activation(dst, bank, ACT.Copy).then_inc(s_pe, 1)
                if i == NCH:
                    conv_sigmoid(NCH - 1)
                if i == NCH + 1:
                    ac.wait_ge(s_par, 112)
                    S.activation(alog[:, :], alog[:, :], ACT.Exp).then_inc(s_expa, 1)
                if i == NCH + 1:
                    ac.wait_ge(s_spin, 1)
                    link(S.activation(dsp[:, 2, :], dsp[:, 1, :], ACT.Exp, scale=-1.0))
                    S.activation(dsp[:, 3, :], dsp[:, 2, :], ACT.Ln, bias=1.0).then_inc(s_spln, 1)
                if i == NCH + 10:
                    ac.wait_ge(s_gh, 1)
                    S.activation(gates[:, 6, :], gates[:, 4, :], ACT.Exp, scale=-1.0).then_inc(s_em, 1)
                    S.activation(identr[:, :], ident[0:H_LSTM, 0:H_LSTM], ACT.Copy)
                    S.activation(negG_hi[:, :], negG[:, :], ACT.Copy).then_inc(s_ngh, 1)
            ac.wait_ge(s_gte, 1)

            def by_token_tile(n):
                quarter, bank = n % 4, B[6 + n % 2]
                if n + 2 < N_IN * 2 - NQK // 2:
                    w_high(NQK // 2 + n + 2)
                ac.wait_ge(s_pj, NQK + n + 1)
                if n < 4:
                    for t in range(TT):
                        ins = S.activation(v1[:, t, 2 * quarter:2 * quarter + 2, 0:HD_LSTM],
                                           bank[:, t * UW:(t + 1) * UW].rearrange("p (h d) -> p h d", h=2), ACT.Copy)
                    ins.then_inc(s_pa, 1)
                else:
                    S.activation((z, og)[n // 4 - 1][:, :, quarter * UW:(quarter + 1) * UW],
                                 bank[:, :].rearrange("p (t n) -> p t n", t=TT), ACT.Copy).then_inc(s_pa, 1)

            for h in range(H_SSM):
                ac.wait_ge(s_seg, h + 1)
                if h >= 3:
                    ac.wait_ge(s_y, h - 2)
                S.activation(dec[:, h % 3, 0:2 * P], B[h % 2][:, 0:2 * P], ACT.Exp)
                S.activation(dec[:, h % 3, 2 * P:3 * P], B[h % 2][:, 2 * P:3 * P], ACT.Exp,
                             bias=r0[:, h:h + 1]).then_inc(s_dec, 1)
                if h % 2:
                    by_token_tile(h // 2)
            ac.wait_ge(s_pa, 8)
            ac.wait_ge(s_seg, H_SSM)
            for t in range(TT):
                S.activation(scr[:, t, :], z[:, t, :], ACT.Sigmoid).then_inc(s_zs, 1)

            def mixed(r):
                ac.wait_ge(s_mxp, r + 1)
                for c in (2 * r, 2 * r + 1):
                    ins = S.activation(mix_hi[:, c % KT, :], B[6 + r % 2][:, (c % 2) * T:(c % 2 + 1) * T], ACT.Copy,
                                       scale=vecT[:, OFF_SN + c:OFF_SN + c + 1])
                ins.then_inc(s_mxh, 1)

            def w_out_high(u):
                ac.wait_ge(full[slot_of(N_IN + u // 2)], fills(N_IN + u // 2))
                if u < 4:
                    ac.wait_ge(s_pj, NQK + min(10 + u, 12))
                else:
                    ac.wait_ge(s_ou, u - 3)
                S.activation(halves[u % 4], out_unit(ring, u), ACT.Copy).then_inc(s_woh, 1)

            ac.wait_ge(s_y, H_SSM)
            for h in range(H_LSTM):
                ac.wait_ge(s_gb, h + 1)
                if h >= 3:
                    ac.wait_ge(s_num, h - 2)
                S.activation(dec[:, h % 3, 0:2 * P], B[2 + h % 2][:, 0:2 * P], ACT.Exp, bias=agT[:, 0, 0, h:h + 1])
                S.activation(dec[:, h % 3, 2 * P:3 * P], B[2 + h % 2][:, 2 * P:3 * P], ACT.Exp,
                             bias=agT[:, 0, 1, h:h + 1]).then_inc(s_ld, 1)
                if h == H_LSTM - 1:
                    w_out_high(0)
                    mixed(0)
                if h % 2:
                    by_token_tile(8 + h // 2)
                    for hh in (h - 1, h):
                        ac.wait_ge(s_hl, hh + 1)
                        if hh >= 2:
                            ac.wait_ge(s_nsq, hh - 1)
                        for t in range(TT):
                            ins = S.activation(junk[:, hh % 2, t, :], hl[:, t, hh, :], ACT.Square,
                                               accum_out=ls[:, 1, t, hh:hh + 1])
                        ins.then_inc(s_nsq, 1)
                if h == 3:
                    ac.wait_ge(s_yg, 1)
                    for t in range(TT):
                        S.activation(scr[:, t, :], yssm[:, t, :], ACT.Square, accum_out=st[:, YS + t:YS + t + 1])
            w_out_high(1)
            mixed(1)
            w_out_high(2)
            mixed(2)
            ac.wait_ge(s_pa, 12)
            for t in range(TT):
                ins = S.activation(og[:, t, :], og[:, t, :], ACT.Sigmoid)
            ins.then_inc(s_osg, 1)
            rms(st[:, YS + 2:YS + 4], st[:, YS:YS + 2]).then_inc(s_yr, 1)
            ac.wait_ge(s_lr, 1)
            S.activation(ls[:, 3, :, :], ls[:, 5, :, :], ACT.Sqrt, scale=1.0 / HD_LSTM, bias=epst[:, :]).then_inc(s_lm, 1)
            w_out_high(3)
            mixed(3)
            w_out_high(4)
            for u in range(5, UO):
                w_out_high(u)
                mixed(u - 1)
            mixed(UO - 1)
            for t in range(TT):
                ac.wait_ge(s_hTp, 2 * t + 2)
                for j in range(4, KT):
                    S.activation(hT[:, j, t * P:(t + 1) * P], hT_banks[t][1][:, (j - 4) * P:(j - 3) * P], ACT.Copy,
                                 scale=nfw[:, j:j + 1]).then_inc(s_hTa, 1)
                link(S.activation(scr[:, t, :], x[:, t, :], ACT.Square, accum_out=st[:, HS + t:HS + t + 1]))
                rms(st[:, HS + 2 + t:HS + 3 + t], st[:, HS + t:HS + t + 1]).then_inc(s_rm3, 1)
            for t in range(TT):
                ac.wait_ge(s_tp, t + 1)
                S.activation(sm[:, t, 0:4], top[:, t, 0:4], ACT.Exp, bias=sm[:, t, 4:5],
                             accum_out=sm[:, t, 5:6]).then_inc(s_se, 1)

            def expert(m):
                ac.wait_ge(s_g, m + 1)
                S.activation(sig, gmin, ACT.Sigmoid, scale=ALPHA).then_inc(s_sig, 1)
                ac.wait_ge(s_pt, m + 1)
                S.activation(PTg.rearrange("p t n -> p (t n)"), outb[:, 0:T], ACT.Copy).then_inc(s_ptg, 1)
                ac.wait_ge(s_atp, m + 1)
                S.activation(actT, hg[:, :], ACT.Copy).then_inc(s_aT, 1)
                ac.wait_ge(s_dn, m + 1)
                S.activation(outS, outb[:, :], ACT.Copy).then_inc(s_os, 1)

            with ac.Fori(0, NE) as n:
                expert(n)
            ac.wait_ge(s_tab, 1)
            over = ac.value_load(tab[0:1, 2 * MAXOVER:2 * MAXOVER + 1], min_val=0, max_val=MAXOVER - 1)
            with ac.If(over > 0):
                with ac.Fori(0, over) as i:
                    expert(i + NE)
            S.activation(st[:, 31:32], epst[:, :], ACT.Sqrt)
            ac.wait_ge(s_Pg, over + NE)
            for t in range(TT):
                ac.wait_ge((s_sca0, s_sca)[t], over + NE)
                for hf in range(2):
                    ins = S.activation(scr[:, t, hf * 512:(hf + 1) * 512], ybank[t][hf][:, :], ACT.Square,
                                       accum_out=st[:, FS + 2 * t + hf:FS + 1 + 2 * t + hf])
                ins.then_inc(s_fsq, 1)
                ac.wait_ge(s_frm, t + 1)
                rms(st[:, FS + 6 + t:FS + 7 + t], st[:, FS + 4 + t:FS + 5 + t]).then_inc(s_fr, 1)

        @block.vector
        def _(ve):
            link = chain(ve, c_dve)

            def transposed(dst, bank, t, wgt, done):
                V.tensor_tensor(dst[:, 0:4, t * P:(t + 1) * P], bank[:, :].rearrange("p (j t) -> p j t", j=4),
                                wgt[:, 0:4].unsqueeze(2).broadcast_to([P, 4, P]), ALU.mult).then_inc(done, 1)
            for t in range(TT):
                ve.wait_ge(s_rms, t + 1)
                V.reciprocal(st[:, XS + 4 + t:XS + 5 + t], st[:, XS + 2 + t:XS + 3 + t]).then_inc(s_rx, 1)
                ve.wait_ge(s_rx, t + 1)
                ve.wait_ge(s_nmp, 1)
                for half in range(2):
                    cols = slice(half * 512, (half + 1) * 512)
                    V.scalar_tensor_tensor(scr[:, t, cols], x[:, t, cols], st[:, XS + 4 + t:XS + 5 + t],
                                           B[4 + half][:, :], ALU.mult, ALU.mult).then_inc(s_xs, 1)
            def xT_low(t):
                rows = slice(t * P, (t + 1) * P)
                for b in range(2):
                    ve.wait_ge(s_xh, 2 * t + b + 1)
                    js = slice(4 * b, 4 * b + 4)
                    V.tensor_tensor(xl[:, js, rows], B[2 * t + b][:, :].rearrange("p (j t) -> p j t", j=4),
                                    xh[:, js, rows], ALU.subtract).then_inc(s_xl, 1)

            def w_low(u):
                ve.wait_ge(s_wh, u + 2)
                V.tensor_tensor(unit(ringr, u), unit(ring, u), w_hi[u % NHB], ALU.subtract).then_inc(s_wl, 1)
            for t, cols in enumerate(tile_cols):
                xT_low(t)
                ve.wait_ge(s_wh, t + 1)
                V.tensor_tensor(unit(ringr, 0)[:, :, cols], unit(ring, 0)[:, :, cols], w_hi[0][:, :, cols],
                                ALU.subtract).then_inc(s_wl, 1)
            ve.wait_ge(s_vps, 1)
            V.tensor_copy(vecT[:, :], B[4][:, 0:NVEC]).then_inc(s_vecT, 1)
            ve.wait_ge(s_vecT, 1)
            ve.wait_ge(s_smh, 1)
            V.tensor_tensor(small_lo[:, :, :], small[:, :, :], small_hi[:, :, :], ALU.subtract).then_inc(s_sml2, 1)
            w_low(1)

            by_t = "p (t n) -> p t n"

            def softplus_inputs():
                ve.wait_ge(s_sml, 1)
                ve.wait_ge(s_par, 112)
                u = dsp[:, 0, :].rearrange(by_t, t=TT)
                V.tensor_tensor(u, B[5][:, 0:TT * NS].rearrange(by_t, t=TT),
                                smb[:, :].unsqueeze(1).broadcast_to([P, TT, NS]), ALU.add).then_inc(s_dt, 1)
                ve.wait_ge(s_dt, 1)
                f = u[:, :, H_SSM + H_LSTM:]
                V.tensor_scalar(f, f, -1.0, None, ALU.mult).then_inc(s_dt, 1)
                ve.wait_ge(s_dt, 2)
                V.scalar_tensor_tensor(dsp[:, 1, :], dsp[:, 0, :], -1.0, dsp[:, 0, :], ALU.mult,
                                       ALU.max).then_inc(s_spin, 1)

            def softplus():
                ve.wait_ge(s_spln, 1)
                link(V.tensor_scalar(dsp[:, 4, :], dsp[:, 2, :], 1.0, -1.0, ALU.add, ALU.add))
                link(V.tensor_scalar(dsp[:, 5, :], dsp[:, 4, :], 0.0, None, ALU.is_equal))
                V.tensor_tensor(dsp[:, 3, :], dsp[:, 3, :], dsp[:, 5, :], ALU.add)
                link(V.tensor_tensor(dsp[:, 4, :], dsp[:, 4, :], dsp[:, 5, :], ALU.add))
                link(V.reciprocal(dsp[:, 6, :], dsp[:, 4, :]))
                link(V.tensor_tensor(dsp[:, 3, :], dsp[:, 3, :], dsp[:, 2, :], ALU.mult))
                link(V.tensor_tensor(dsp[:, 3, :], dsp[:, 3, :], dsp[:, 6, :], ALU.mult))
                V.scalar_tensor_tensor(dsp[:, 6, :], dsp[:, 0, :], 0.0, dsp[:, 3, :], ALU.max, ALU.add).then_inc(s_spd, 1)

            def ssd_gates():
                ve.wait_ge(s_spd, 1)
                dt = dsp[:, 6, :].rearrange(by_t, t=TT)[:, :, 0:H_SSM]
                V.tensor_copy(dtt[:, :, :], dt)
                ve.wait_ge(s_expa, 1)
                V.scalar_tensor_tensor(at[:, :, :], dt, -1.0, alog[:, :].unsqueeze(1).broadcast_to([P, TT, H_SSM]),
                                       ALU.mult, ALU.mult).then_inc(s_at, 1)

            def lstm_gates():
                ve.wait_ge(s_ift, 1)
                link(V.tensor_copy(gates[:, 0, :], B[4][0:H_LSTM, T:2 * T]))
                link(V.tensor_tensor_scan(gates[:, 1, :], gates[:, 5, :], gates[:, 0, :], 0.0, ALU.mult, ALU.add))
                link(V.tensor_tensor(gates[:, 2, :], B[4][0:H_LSTM, 0:T], gates[:, 1, :], ALU.add))
                link(V.tensor_tensor_scan(gates[:, 3, :], gates[:, 2, :], gates[:, 2, :], 0.0, ALU.max, ALU.max))
                V.tensor_scalar(negG[:, :], gates[:, 3, :], -1.0, None, ALU.mult)
                V.tensor_tensor(gates[:, 4, :], gates[:, 3, :], gates[:, 1, :], ALU.subtract).then_inc(s_gh, 1)

            def conv_finish(c):
                ve.wait_ge(s_cs, c + 1)
                V.tensor_tensor(conv[:, c, :], conv[:, c, :], csig[:, c % 2, :], ALU.mult).then_inc(s_cd, 1)
            for c in range(NCH):
                if c % 2 == 0 and c // 2 + 2 not in POOL_IN_UNITS:
                    w_low(c // 2 + 2)
                ve.wait_ge(s_raw, c + 1)
                for w in range(1, CONV_W):
                    ins = V.scalar_tensor_tensor(conv[:, c, :], raw[:, c % 3, w:w + T],
                                                 vecT[:, w * NCH + c:w * NCH + c + 1], conv[:, c, :], ALU.mult, ALU.add)
                    if w < CONV_W - 1:
                        link(ins)
                ins.then_inc(s_cv, 1)
                if c:
                    conv_finish(c - 1)
                if c == 3:
                    ve.wait_ge(s_smp, 1)
                    V.tensor_copy(smT, B[4][0:NS, 0:T]).then_inc(s_smc, 1)

            def gates_by_token():
                ve.wait_ge(s_gtp, 1)
                V.tensor_copy(agT[:, :, :, :].rearrange("p a t h -> p (a t h)"), B[5][:, 80:112])
                V.tensor_copy(r0[:, :], B[5][:, 64:80]).then_inc(s_gte, 1)

            def xs_by_token(b):
                t, half = b // 2, b % 2
                ve.wait_ge(s_xsp, b + 1)
                src = B[b][:, :].rearrange("p (h d) -> p h d", h=8)
                for dst, wgt in ((xd, dtt[:, t, 8 * half:8 * half + 8]), (yssm, dsk[:, 8 * half:8 * half + 8])):
                    ins = V.tensor_tensor(dst[:, t, half * 512:(half + 1) * 512].rearrange("p (h d) -> p h d", h=8),
                                          src, wgt.unsqueeze(2).broadcast_to([P, 8, HD_SSM]), ALU.mult)
                ins.then_inc(s_xse, 1)

            def cb_masked(g):
                ve.wait_ge(s_cbp, g + 1)
                V.tensor_tensor(cbm[:, g, 0:2 * P].rearrange("p (b n) -> p b n", b=2),
                                B[4 + g][:, 0:2 * P].rearrange("p (b n) -> p b n", b=2),
                                tri_le[:, :].unsqueeze(1).broadcast_to([P, 2, P]), ALU.mult)
                V.tensor_copy(cbm[:, g, 2 * P:3 * P], B[4 + g][:, 2 * P:3 * P]).then_inc(s_cbe, 1)

            for i in range(NCH, NQK):
                if i % 2 == 0 and i // 2 + 2 not in POOL_IN_UNITS:
                    w_low(i // 2 + 2)
                if i == NCH + 11:
                    ve.wait_ge(s_ngh, 1)
                    V.tensor_tensor(negG_lo[:, :], negG[:, :], negG_hi[:, :], ALU.subtract).then_inc(s_ngl, 1)
                if i == NCH:
                    conv_finish(NCH - 1)
                    softplus_inputs()
                if i == NCH + 2:
                    softplus()
                    ssd_gates()
                if i == I_TR + 1:
                    lstm_gates()
                if i == I_GT:
                    gates_by_token()
                if i == I_XS:
                    for b in range(4):
                        xs_by_token(b)
                if i == I_CB:
                    cb_masked(0)
                    cb_masked(1)
            ve.wait_ge(s_cbe, 2)
            ve.wait_ge(s_xse, 4)
            for h in range(H_SSM):
                ve.wait_ge(s_dec, h + 1)
                V.tensor_tensor(dec[:, h % 3, :], dec[:, h % 3, :], cbm[:, h // 8, :], ALU.mult).then_inc(s_m, 1)
                if h % 2:
                    w_low(NQK // 2 + h // 2 + 2)
                if h % 8 == 7:
                    half = h // 8
                    ve.wait_ge(s_y, h + 1)
                    for t in range(TT):
                        part = yssm[:, t, half * 512:(half + 1) * 512]
                        V.tensor_tensor(part, B[2 + t][:, :], part, ALU.add).then_inc(s_yev, 1)

            def weights(h):
                ve.wait_ge(s_sp, h + 1)
                ve.wait_ge(s_ld, h + 1)
                V.scalar_tensor_tensor(dec[:, h % 3, :], B[h % 2][:, 0:3 * P], QK_SCALE, dec[:, h % 3, :],
                                       ALU.mult, ALU.mult).then_inc(s_sc, 1)

            def mixed_low(r):
                ve.wait_ge(s_mxh, r + 1)
                for c in (2 * r, 2 * r + 1):
                    ins = V.scalar_tensor_tensor(mix_lo[:, c % KT, :], B[6 + r % 2][:, (c % 2) * T:(c % 2 + 1) * T],
                                                 vecT[:, OFF_SN + c:OFF_SN + c + 1], mix_hi[:, c % KT, :],
                                                 ALU.mult, ALU.subtract)
                ins.then_inc(s_mxe, 1)

            def w_out_low(u):
                ve.wait_ge(s_woh, u + 1)
                V.tensor_tensor(out_unit(ringr, u), out_unit(ring, u), halves[u % 4], ALU.subtract).then_inc(s_wol, 1)

            for h in range(0, H_LSTM, 2):
                weights(h)
                weights(h + 1)
                if NQK // 2 + 8 + h // 2 + 2 < 2 * N_IN:
                    w_low(NQK // 2 + 8 + h // 2 + 2)
                if h == H_LSTM - 2:
                    w_out_low(0)
                    mixed_low(0)
                if h == 0:
                    for t in range(TT):
                        ve.wait_ge(s_zs, t + 1)
                        link(V.tensor_tensor(z[:, t, :], z[:, t, :], scr[:, t, :], ALU.mult))
                    ve.wait_ge(s_yev, 4)
                    V.tensor_tensor(yssm[:, 0, :], yssm[:, 0, :], z[:, 0, :], ALU.mult)
                    V.tensor_tensor(yssm[:, 1, :], yssm[:, 1, :], z[:, 1, :], ALU.mult).then_inc(s_yg, 1)
                for hh in (h, h + 1):
                    ve.wait_ge(s_num, hh + 1)
                    nb = B[4 + hh % 2][:, :].rearrange("p (t n) -> p t n", t=TT)
                    V.tensor_copy(hl[:, :, hh, :], nb[:, :, 0:HD_LSTM])
                    V.tensor_copy(ls[:, 0, :, hh:hh + 1], nb[:, :, HD_LSTM:HD_LSTM + 1]).then_inc(s_hl, 1)
            w_out_low(1)
            mixed_low(1)
            ve.wait_ge(s_hl, H_LSTM)
            ve.wait_ge(s_nsq, H_LSTM)
            link(V.scalar_tensor_tensor(ls[:, 5, :, :], ls[:, 0, :, :], -1.0, ls[:, 0, :, :], ALU.mult, ALU.max))
            link(V.tensor_tensor(ls[:, 5, :, :], ls[:, 5, :, :], agT[:, 1, :, :], ALU.max))
            link(V.reciprocal(ls[:, 2, :, :], ls[:, 5, :, :]))
            link(V.tensor_tensor(ls[:, 4, :, :], ls[:, 2, :, :], ls[:, 1, :, :], ALU.mult))
            V.tensor_tensor(ls[:, 5, :, :], ls[:, 4, :, :], ls[:, 2, :, :], ALU.mult).then_inc(s_lr, 1)
            w_out_low(2)
            mixed_low(2)
            ve.wait_ge(s_lm, 1)
            link(V.reciprocal(ls[:, 4, :, :], ls[:, 3, :, :]))
            link(V.tensor_tensor(ls[:, 4, :, :], ls[:, 4, :, :], ls[:, 2, :, :], ALU.mult))
            w_out_low(3)
            mixed_low(3)
            ve.wait_ge(s_osg, 1)

            def gated(r):
                for h in (2 * r, 2 * r + 1):
                    for t in range(TT):
                        ins = V.scalar_tensor_tensor(hl[:, t, h, :], hl[:, t, h, :], ls[:, 4, t, h:h + 1],
                                                     og[:, t, h * HD_LSTM:(h + 1) * HD_LSTM], ALU.mult, ALU.mult)
                ins.then_inc(s_hln, 1)
            gated(0)
            gated(1)
            w_out_low(4)
            mixed_low(4)
            gated(2)
            gated(3)
            mixed_low(5)
            ve.wait_ge(s_yr, 1)
            link(V.reciprocal(st[:, YS + 4:YS + 6], st[:, YS + 2:YS + 4]))
            ve.wait_ge(s_ou, 4)
            for t in range(TT):
                for half in range(2):
                    part = x[:, t, half * 512:(half + 1) * 512]
                    ins = V.scalar_tensor_tensor(part, B[2 * t + half][:, :], st[:, YS + 4 + t:YS + 5 + t], part,
                                                 ALU.mult, ALU.add)
                ins.then_inc(s_ha, 1)
                if t == 0:
                    w_out_low(6)
                mixed_low(6 + t)

            def choose(t):
                ve.wait_ge(s_op, t + 1)
                ve.wait_ge(s_ha, t + 1)
                for half in range(2):
                    part = x[:, t, half * 512:(half + 1) * 512]
                    ins = V.tensor_tensor(part, B[(4, 0)[t] + half][:, :], part, ALU.add)
                ins.then_inc(s_h, 1)
                ve.wait_ge(s_hTp, 2 * t + 1)
                transposed(hT, hT_banks[t][0], t, nfw, s_hTv)
                ve.wait_ge(s_rm3, t + 1)
                link(V.reciprocal(st[:, HS + 4 + t:HS + 5 + t], st[:, HS + 2 + t:HS + 3 + t]))
                ve.wait_ge(s_lgp, t + 1)
                V.scalar_tensor_tensor(lg[:, t, :], B[6 + t][:, 0:NE], st[:, HS + 4 + t:HS + 5 + t], br[:, :],
                                       ALU.mult, ALU.add).then_inc(s_lge, 1)
                ve.wait_ge(s_lge, t + 1)
                link(V.max(top[:, t, :], lg[:, t, :]))
                link(V.max_index(tidx[:, t, :], top[:, t, :], lg[:, t, :]))
                link(V.tensor_copy(tidf[:, t, :], tidx[:, t, :]))
                link(V.tensor_tensor(eq[:, t, :, :], ie[:, :].unsqueeze(1).broadcast_to([P, TOPK, NE]),
                                     tidf[:, t, 0:TOPK].unsqueeze(2).broadcast_to([P, TOPK, NE]), ALU.is_equal))
                V.tensor_reduce(mall[:, t, 0:NE], eq[:, t, :, :].rearrange("p k e -> p e k"), AX.X,
                                ALU.add).then_inc(s_M, 1)
                V.tensor_scalar(sm[:, t, 4:5], top[:, t, 0:1], -1.0, None, ALU.mult).then_inc(s_tp, 1)

            def position_tables():
                ve.wait_ge(s_pos, 1)
                link(V.scalar_tensor_tensor(posm[:, :, 0:NE], xb[:, 64:64 + TT * NE].rearrange("p (t e) -> p t e", t=TT),
                                            1.0, mall[:, :, 0:NE], ALU.add, ALU.mult))

            def block_tables():
                for b in range(NBLK - 1, 0, -1):
                    V.tensor_scalar(posm[:, :, b * NE:(b + 1) * NE], posm[:, :, 0:NE], -1.0 * b * SL, None, ALU.add)
                    V.tensor_copy(mall[:, :, b * NE:(b + 1) * NE], mall[:, :, 0:NE])
                for t in range(TT):
                    ve.wait_ge(s_se, t + 1)
                    link(V.reciprocal(sm[:, t, 6:7], sm[:, t, 5:6]))
                    link(V.tensor_scalar(sm[:, t, 0:4], sm[:, t, 0:4], sm[:, t, 6:7], None, ALU.mult))
                    link(V.tensor_tensor(eqg, eq[:, t, :, :], sm[:, t, 0:TOPK].unsqueeze(2).broadcast_to([P, TOPK, NE]),
                                         ALU.mult))
                    link(V.tensor_reduce(gall[:, t, 0:NE], eqg.rearrange("p k e -> p e k"), AX.X, ALU.add))
                for b in range(1, NBLK):
                    ins = V.tensor_copy(gall[:, :, b * NE:(b + 1) * NE], gall[:, :, 0:NE])
                ins.then_inc(s_tabs, 1)
                ve.wait_ge(s_tabs, 1)

            choose(0)
            choose(1)
            position_tables()

            def pick(v):
                for t in range(TT):
                    ins = V.tensor_scalar(Pm[:, t, :], islot[:, 0, :], posm[:, t, bass.ds(v, 1)],
                                          st[:, HS + 4 + t:HS + 5 + t], ALU.is_equal, ALU.mult)
                ins.then_inc(s_P, 1)

            def pick_gated(v):
                for t in range(TT):
                    V.tensor_scalar(Pg[:, t, :], islot[:, :, :].rearrange("p a s -> p (a s)"), posm[:, t, bass.ds(v, 1)],
                                    gall[:, t, bass.ds(v, 1)], ALU.is_equal, ALU.mult)
                V.tensor_copy(sel, selall[:, :, :].rearrange("p b e -> p (b e)")[:, bass.ds(v, 1)]
                              .broadcast_to([P, SL])).then_inc(s_Pg, 1)

            def gathered():
                V.tensor_tensor(XT.rearrange("p (j s) -> p j s", j=KT), xb[:, :].rearrange("p (j s) -> p j s", j=KT),
                                nfw[:, :].unsqueeze(2).broadcast_to([P, KT, SL]), ALU.mult).then_inc(s_XT, 1)

            def swiglu(m):
                ve.wait_ge(s_gu, m + 1)
                V.tensor_scalar(gmin, hg[:, :], LIMIT, None, ALU.min).then_inc(s_g, 1)
                V.tensor_scalar(ucl, hu[:, :], -LIMIT, LIMIT, ALU.max, ALU.min)
                ve.wait_ge(s_sig, m + 1)
                V.tensor_tensor(gsg, gmin, sig, ALU.mult).then_inc(s_gs, 1)
                ve.wait_ge(s_gs, m + 1)
                V.scalar_tensor_tensor(act, ucl, 1.0, gsg, ALU.add, ALU.mult).then_inc(s_act, 1)

            pick(0)
            block_tables()
            ve.wait_ge(s_xg, 1)
            gathered()
            pick_gated(0)
            pick(1)
            ve.wait_ge(s_cnt, 1)
            V.tensor_tensor(flag[:, 0:1], outb[:, 0:1], thr[:, :], ALU.is_gt).then_inc(s_fl, 1)
            ve.wait_ge(s_pi, 1)
            link(V.tensor_copy(flag[:, 1:2], outb[:, 1:2]))
            V.tensor_scalar(oh[:, :], iover[:, :], flag[:, 1:2], flag[:, 0:1], ALU.is_equal,
                            ALU.mult).then_inc(s_oh, 1)
            ve.wait_ge(s_tb, 1)
            link(V.tensor_copy(tabf[:, :], outb[0:1, 2:2 + 2 * MAXOVER + 1]))
            V.tensor_copy(tab[:, :], tabf[:, :]).then_inc(s_tab, 1)

            def main_item(n):
                swiglu(n)
                ve.wait_ge(s_xg, n + 2)
                gathered()
                pick(n + 2)
                ve.wait_ge(s_dnb, n + 1)
                pick_gated(n + 1)
            with ve.Fori(0, NE - 1) as n:
                main_item(n)
            swiglu(NE - 1)
            ve.wait_ge(s_tab, 1)
            over = ve.value_load(tab[0:1, 2 * MAXOVER:2 * MAXOVER + 1], min_val=0, max_val=MAXOVER - 1)
            with ve.If(over > 0):
                with ve.Fori(0, over) as i:
                    v = ve.value_load(tab[0:1, bass.ds(i, 1)], min_val=0, max_val=NV - 1)
                    ve.wait_ge(s_sca, i + NE)
                    ve.wait_ge(s_P, i + NE + 1)
                    ve.wait_ge(s_Pg, i + NE)
                    pick(v)
                    pick_gated(v)
                    ve.wait_ge(s_xg, i + NE + 1)
                    gathered()
                    swiglu(i + NE)
            ve.wait_ge(s_wfin, 16)
            for t in range(TT):
                ve.wait_ge(s_fsq, t + 1)
                a = FS + 2 * t
                V.tensor_tensor(st[:, FS + 4 + t:FS + 5 + t], st[:, a:a + 1], st[:, a + 1:a + 2], ALU.add).then_inc(s_frm, 1)
                ve.wait_ge(s_fr, t + 1)
                link(V.reciprocal(st[:, FS + 8 + t:FS + 9 + t], st[:, FS + 6 + t:FS + 7 + t]))
                for hf in range(2):
                    V.scalar_tensor_tensor(fin[:, t, hf * 512:(hf + 1) * 512], ybank[t][hf][:, :],
                                           st[:, FS + 8 + t:FS + 9 + t], wfin[:, hf * 512:(hf + 1) * 512],
                                           ALU.mult, ALU.mult).then_inc(s_fin, 1)

        @block.tensor
        def _(pe):
            mm = E.matmul
            pe.wait_ge(c_ones, 1)
            pe.wait_ge(s_nm, 16)
            for half in range(2):
                ins = mm(B[4 + half][:, :], ones[0:1, :], nmr[:, half * 512:(half + 1) * 512], start=True, stop=True)
            ins.then_inc(s_nmp, 1)
            pe.wait_ge(c_id, 1)

            def transpose_x(src, t, banks, done):
                for j in range(KT):
                    if src is scr and j % 4 == 0:
                        pe.wait_ge(s_xs, 2 * t + j // 4 + 1)
                    ins = E.transpose(banks[j // 4][:, (j % 4) * P:(j % 4 + 1) * P],
                                      src[:, t, j * P:(j + 1) * P], ident[:, :])
                    if j % 4 == 3:
                        ins.then_inc(done, 1)
            for t in range(TT):
                transpose_x(scr, t, B[2 * t:2 * t + 2], s_xT)
            pe.wait_ge(s_vec, 80)
            E.transpose(B[4][:, 0:NVEC], vecs[:, :], ident[0:NVEC, 0:NVEC]).then_inc(s_vps, 1)
            pe.wait_ge(s_xl, 4)

            def split_product(out, lhs_hi, lhs_lo, rhs_hi, rhs_lo, start, stop):
                mm(out, lhs_hi, rhs_hi, start=start, stop=False)
                mm(out, lhs_hi, rhs_lo, start=False, stop=False)
                return mm(out, lhs_lo, rhs_hi, start=False, stop=stop)

            def small_projections():
                pe.wait_ge(s_sml2, 1)
                pe.wait_ge(s_vecT, 1)
                for j in range(KT):
                    ins = split_product(B[4][0:NS, 0:T], small_hi[:, j, :], small_lo[:, j, :], xh[:, j, :], xl[:, j, :],
                                        j == 0, j == KT - 1)
                ins.then_inc(s_smp, 1)

            def small_by_token():
                pe.wait_ge(s_smc, 1)
                for t in range(TT):
                    ins = E.transpose(B[5][:, t * NS:(t + 1) * NS], smT[:, t * P:(t + 1) * P], ident[0:NS, 0:NS])
                ins.then_inc(s_sml, 1)

            def if_by_head():
                pe.wait_ge(s_spd, 1)
                for k, row in ((0, 0), (1, 6)):
                    for t in range(TT):
                        o = t * NS + H_SSM + k * H_LSTM
                        ins = E.transpose(B[4][0:H_LSTM, k * T + t * P:k * T + (t + 1) * P],
                                          dsp[:, row, o:o + H_LSTM], ident[:, :])
                ins.then_inc(s_ift, 1)

            def bank_free(i):
                if i < N4:
                    if i >= 4:
                        pe.wait_ge(s_pe, i - 3)
                elif NQK <= i - 2:
                    pe.wait_ge(s_pa, i - 1 - NQK)
                elif i >= 2:
                    pe.wait_ge(s_pe, i - 1)

            def unit_split(u):
                if u in POOL_IN_UNITS:
                    pe.wait_ge(s_wlp, POOL_IN_UNITS.index(u) + 1)
                else:
                    pe.wait_ge(s_wl, 1 + sum(v not in POOL_IN_UNITS for v in range(u + 1)))

            def by_channel(i):
                u = i // 2
                if i:
                    unit_split(u)
                else:
                    pe.wait_ge(s_wl, 1)
                bank_free(i)
                cols = slice((i % 2) * P, (i % 2 + 1) * P)
                for j in range(KT):
                    ins = split_product(channel_bank(i)[:, 0:T], w_hi[u % NHB][:, j, cols], unit(ringr, u)[:, j, cols],
                                        xh[:, j, :], xl[:, j, :], j == 0, j == KT - 1)
                ins.then_inc(s_pj, 1)

            def by_token(n):
                i, u = NQK + n, NQK // 2 + n
                unit_split(u)
                bank_free(i)
                for t in range(TT):
                    rows = slice(t * P, (t + 1) * P)
                    for j in range(KT):
                        ins = split_product(B[6 + i % 2][:, t * UW:(t + 1) * UW], xh[:, j, rows], xl[:, j, rows],
                                            w_hi[u % NHB][:, j, :], unit(ringr, u)[:, j, :], j == 0, j == KT - 1)
                ins.then_inc(s_pj, 1)

            for i in range(NCH):
                by_channel(i)
                if i == 2:
                    small_projections()
                if i == 6:
                    small_by_token()
            def gates_by_token():
                pe.wait_ge(s_at, 1)
                pe.wait_ge(s_em, 1)
                pe.wait_ge(c_consts, 1)
                mm(B[5][:, 64:80], tri_gt[:, :], at[:, 0, :], start=True, stop=True)
                for a, row in ((0, 2), (1, 6)):
                    for t in range(TT):
                        ins = E.transpose(B[5][:, 80 + 16 * a + 8 * t:88 + 16 * a + 8 * t],
                                          gates[:, row, t * P:(t + 1) * P], ident[0:H_LSTM, 0:H_LSTM])
                ins.then_inc(s_gtp, 1)

            def xs_by_token():
                pe.wait_ge(s_cd, XT_TILES)
                for t in range(TT):
                    for c in range(XT_TILES):
                        ins = E.transpose(B[2 * t + c // 4][:, (c % 4) * P:(c % 4 + 1) * P],
                                          conv[:, c, t * P:(t + 1) * P], ident[:, :])
                        if c % 4 == 3:
                            ins.then_inc(s_xsp, 1)

            def c_dot_b():
                pe.wait_ge(s_cd, NCH)
                pe.wait_ge(s_gte, 1)
                for g in range(2):
                    bT, cT = conv[:, XT_TILES + g, :], conv[:, XT_TILES + 2 + g, :]
                    mm(B[4 + g][:, 0:P], bT[:, 0:P], cT[:, 0:P], start=True, stop=True)
                    mm(B[4 + g][:, 2 * P:3 * P], bT[:, 0:P], cT[:, P:T], start=True, stop=True)
                    mm(B[4 + g][:, P:2 * P], bT[:, P:T], cT[:, P:T], start=True, stop=True).then_inc(s_cbp, 1)
            for i in range(NCH, NQK):
                if i == I_TR:
                    if_by_head()
                if i == I_GT:
                    gates_by_token()
                if i == I_XS:
                    xs_by_token()
                if i == I_CB:
                    c_dot_b()
                by_channel(i)
            pe.wait_ge(s_xse, 4)

            def seg(h):
                pe.wait_ge(s_au, 2 * (h // 4) + 2)
                if h >= 2:
                    pe.wait_ge(s_dec, h - 1)
                bank, a = B[h % 2], au[:, (h // 4) % 2, h % 4, :, :]
                mm(bank[:, 0:P], a[:, 0, :], tri_le[:, :], start=True, stop=True)
                mm(bank[:, P:2 * P], a[:, 1, :], tri_le[:, :], start=True, stop=True)
                mm(bank[:, 2 * P:3 * P], at[:, 1, h:h + 1].broadcast_to([P, P]), tri_le[:, :],
                   start=True, stop=True).then_inc(s_seg, 1)

            def ssd_product(h):
                pe.wait_ge(s_m, h + 1)
                if h == 8:
                    pe.wait_ge(s_yev, 2)
                w, c = dec[:, h % 3, :], (h % 8) * HD_SSM
                xd0, xd1 = (xd[:, t, h * HD_SSM:(h + 1) * HD_SSM] for t in range(TT))
                mm(B[2][:, c:c + HD_SSM], w[:, 0:P], xd0, start=True, stop=True)
                mm(B[3][:, c:c + HD_SSM], w[:, 2 * P:3 * P], xd0, start=True, stop=False)
                mm(B[3][:, c:c + HD_SSM], w[:, P:2 * P], xd1, start=False, stop=True).then_inc(s_y, 1)

            for n in range(H_SSM // 2):
                seg(2 * n)
                seg(2 * n + 1)
                by_token(n)
                ssd_product(2 * n)
                ssd_product(2 * n + 1)
            def mix_transposes(r):
                if r == 0:
                    pe.wait_ge(s_yg, 1)
                if r >= KT // 2:
                    pe.wait_ge(s_hln, r - KT // 2 + 1)
                if r < 2:
                    pe.wait_ge(s_pa, 11 + r)
                else:
                    pe.wait_ge(s_mxe, r - 1)
                for c in (2 * r, 2 * r + 1):
                    for t in range(TT):
                        src = yssm[:, t, c * P:(c + 1) * P] if c < 8 else hl[:, t, c - 8, :]
                        o = (c % 2) * T + t * P
                        ins = E.transpose(B[6 + r % 2][:, o:o + P], src, ident[:, :])
                ins.then_inc(s_mxp, 1)

            def scores(h):
                if h < 2:
                    pe.wait_ge(s_dec, H_SSM)
                else:
                    pe.wait_ge(s_sc, h - 1)
                q = qT[:, h, :]
                mm(B[h % 2][:, 0:T], kT[:, h, 0:P], q, start=True, stop=True)
                mm(B[h % 2][:, T:T + P], kT[:, h, P:T], q[:, P:T], start=True, stop=True).then_inc(s_sp, 1)
                if h >= 2:
                    pe.wait_ge(s_ld, h - 1)
                gb = B[2 + h % 2]
                if h == 0:
                    pe.wait_ge(s_yev, 4)
                    pe.wait_ge(s_ngl, 1)
                selh = identr[:, h:h + 1].broadcast_to([H_LSTM, P])
                mm(gb[:, 0:T], selh, negG_hi[:, :], start=True, stop=False)
                mm(gb[:, 0:T], selh, negG_lo[:, :], start=False, stop=False)
                mm(gb[:, 0:P], identb[:, :], negm[:, :], start=False, stop=True)
                mm(gb[:, T:T + P], selh, negG_hi[:, P:T], start=True, stop=False)
                mm(gb[:, T:T + P], selh, negG_lo[:, P:T], start=False, stop=False)
                mm(gb[:, T:T + P], identb[:, :], negm[:, :], start=False, stop=True).then_inc(s_gb, 1)

            def lstm_product(h):
                pe.wait_ge(s_sc, h + 1)
                if h < 2:
                    pe.wait_ge(s_pa, 4)
                else:
                    pe.wait_ge(s_hl, h - 1)
                w, nb = dec[:, h % 3, :], B[4 + h % 2]
                mm(nb[:, 0:VW], w[:, 0:P], v1[:, 0, h, :], start=True, stop=True)
                mm(nb[:, T:T + VW], w[:, P:2 * P], v1[:, 0, h, :], start=True, stop=False)
                mm(nb[:, T:T + VW], w[:, 2 * P:3 * P], v1[:, 1, h, :], start=False, stop=True).then_inc(s_num, 1)

            for n in range(H_LSTM // 2):
                scores(2 * n)
                scores(2 * n + 1)
                if n == H_LSTM // 2 - 1:
                    mix_transposes(0)
                by_token(8 + n)
                lstm_product(2 * n)
                lstm_product(2 * n + 1)
            def router_logits(t):
                pe.wait_ge(s_hTv, t + 1)
                pe.wait_ge(s_hTa, 4 * t + 4)
                for j in range(KT):
                    ins = mm(B[6 + t][:, 0:NE], hT[:, j, t * P:(t + 1) * P], wr[:, j, :],
                             start=j == 0, stop=j == KT - 1)
                ins.then_inc(s_lgp, 1)

            def out_products(u, t):
                if t == 0:
                    if u in POOL_UNITS:
                        pe.wait_ge(s_wop, POOL_UNITS.index(u) + 1)
                    else:
                        pe.wait_ge(s_wol, sum(v not in POOL_UNITS for v in range(u + 1)))
                    pe.wait_ge(s_mxe, u + 1)
                for c in (2 * u, 2 * u + 1):
                    tokens = slice(t * P, (t + 1) * P)
                    for half in range(2):
                        bank = B[2 * t + half] if c < 8 else B[(4, 0)[t] + half]
                        o = (c % 2) * D + half * 512
                        ins = split_product(bank[:, :], mix_hi[:, c % KT, tokens], mix_lo[:, c % KT, tokens],
                                            halves[u % 4][:, o:o + 512], out_unit(ringr, u)[:, o:o + 512],
                                            c % 8 == 0, c % 8 == 7)
                return ins
            mix_transposes(1)
            pe.wait_ge(s_sc, H_LSTM)
            for u in range(4):
                if u in (1, 2):
                    mix_transposes(u + 1)
                out_products(u, 0)
                if u == 3:
                    mix_transposes(u + 1)
                out_products(u, 1).then_inc(s_ou, 1)
            for u in range(4, UO):
                if u < UO - 1:
                    mix_transposes(u + 1)
                ins = out_products(u, 0)
            ins.then_inc(s_op, 1)
            pe.wait_ge(s_ha, 1)
            for u in range(4, UO):
                ins = out_products(u, 1)
                if u == 5:
                    ins.then_inc(s_ou, 1)
                    pe.wait_ge(s_h, 1)
                    pe.wait_ge(s_ha, 2)
                    transpose_x(x, 0, hT_banks[0], s_hTp)
                if u == 6:
                    router_logits(0)
            ins.then_inc(s_op, 1)
            def residual(t, half):
                mm(ybank[t][half][:, :], ident[:, :], x[:, t, half * 512:(half + 1) * 512], start=True, stop=False)
            residual(0, 0)
            pe.wait_ge(s_h, 2)
            transpose_x(x, 1, hT_banks[1], s_hTp)
            residual(0, 1)
            router_logits(1)
            residual(1, 0)
            pe.wait_ge(s_M, 2)
            mm(xb[:, 64:96], tri_lt[:, :], mall[:, 0, 0:NE], start=True, stop=True)
            mm(xb[:, 96:128], ones[:, :], mall[:, 0, 0:NE], start=True, stop=False)
            mm(xb[:, 96:128], tri_lt[:, :], mall[:, 1, 0:NE], start=False, stop=True).then_inc(s_pos, 1)
            residual(1, 1)

            def gather(p):
                pe.wait_ge(s_P, p)
                for j in range(KT):
                    for t in range(TT):
                        ins = mm(xb[:, j * SL:(j + 1) * SL], x[:, t, j * P:(j + 1) * P], Pm[:, t, :], start=t == 0, stop=t == TT - 1)
                ins.then_inc(s_xg, 1)

            def column_tiles(bank, lhsT, rhs, start, stop):
                for hf in range(2):
                    ins = mm(bank[hf * SL:(hf + 1) * SL, :], lhsT[hf], rhs[hf], start=start, stop=stop)
                return ins

            def gate_up(m, ready):
                pe.wait_ge(s_XT, ready)
                for j in range(KT):
                    c = j // 2
                    if j % 2 == 0 and in_annex(m, c):
                        pe.wait_ge(s_annex[c], 16)
                    elif j % 2 == 0:
                        pe.wait_ge(full[expert_slot(m, c)], expert_fills(m, c))
                    w = expert_chunk(m, c)
                    lhsT = XT[:, j * SL:(j + 1) * SL]
                    for bank, o in ((hg, 0), (hu, FF)):
                        o += (j % 2) * 2 * FF
                        ins = column_tiles(bank, [lhsT] * 2, [w[:, o:o + 512], w[:, o + 512:o + 1024]],
                                           j == 0, j == KT - 1)
                    if j % 2:
                        ins.then_inc(used if j < KT - 1 else s_gu, 1)
                    if j == 1:
                        pe.wait_ge(s_Pg, ready)
                        for bank, o in ((hg, 0), (hu, FF)):
                            column_tiles(bank, [sel] * 2, [biases[:, o:o + 512], biases[:, o + 512:o + 1024]],
                                         False, False)
                    if j % 2 and is_item(m, FIRST) and c < 3:
                        item_table(c)

            def item_table(step):
                if step == 0:
                    for t in range(TT):
                        ins = mm(outb[:, 0:1], mall[:, t, :], ones[:, 0:1], start=t == 0, stop=t == TT - 1)
                    ins.then_inc(s_cnt, 1)
                elif step == 1:
                    pe.wait_ge(s_fl, 1)
                    mm(outb[:, 1:2], tri_lt[:, :], flag[:, 0:1], start=True, stop=True).then_inc(s_pi, 1)
                else:
                    pe.wait_ge(s_oh, 1)
                    mm(outb[0:1, 2:2 + MAXOVER], ipart[:, :], oh[:, :], start=True, stop=True)
                    mm(outb[0:1, 2 + MAXOVER:2 + 2 * MAXOVER], vmod[:, :], oh[:, :], start=True, stop=True)
                    mm(outb[0:1, 2 + 2 * MAXOVER:3 + 2 * MAXOVER], flag[:, 0:1], ones[:, 0:1], start=True,
                       stop=True).then_inc(s_tb, 1)

            def transpose_gates():
                for t in range(TT):
                    ins = E.transpose(outb[:, t * P:(t + 1) * P], Pg[:, t, :], ident[:, :])
                ins.then_inc(s_pt, 1)

            def down(m):
                pe.wait_ge(s_act, m + 1)
                for q in range(4):
                    ins = E.transpose(hg[:, q * P:(q + 1) * P], act[:, q * P:(q + 1) * P], ident[:, :])
                ins.then_inc(s_atp, 1)
                pe.wait_ge(s_ptg, m + 1)
                column_tiles(outb, [sel] * 2, [biases[:, 2 * FF:2 * FF + 512], biases[:, 2 * FF + 512:3 * FF]],
                             True, False).then_inc(s_dnb, 1)
                pe.wait_ge(s_aT, m + 1)
                for f in range(8):
                    c = 4 + f // 4
                    if is_item(m, NE - 1) and 4 <= f < 7:
                        pe.wait_ge(s_piece[f - 4], 16)
                    elif f % 4 == 0 or is_item(m, NE - 1) and f == 7:
                        pe.wait_ge(full[expert_slot(m, c)], expert_fills(m, c))
                    w = expert_chunk(m, c)
                    q, half = f % 4, f // 4
                    lhsT = actT[:, q * P + half * SL:q * P + (half + 1) * SL]
                    o = q * D
                    ins = column_tiles(outb, [lhsT] * 2, [w[:, o:o + 512], w[:, o + 512:o + 1024]],
                                       False, f == 7)
                    if f % 4 == 3:
                        ins.then_inc(used if f < 7 else s_dn, 1)

            def scatter(m, last=False, again=False):
                pe.wait_ge(s_os, m + 1)
                for t in range(TT):
                    for hf in range(2):
                        rows = slice(hf * SL, (hf + 1) * SL)
                        ins = mm(ybank[t][hf][:, :], PTg[rows, t, :], outS[rows, :], start=False, stop=last,
                                 skip_group_check=again)
                    ins.then_inc((s_sca0, s_sca)[t], 1)

            gather(1)
            pe.wait_ge(s_bias, 32)

            def main_item(m):
                gate_up(m, m + 1)
                if is_item(m, FIRST):
                    pe.wait_ge(s_tab, 1)
                else:
                    scatter(m - 1)
                transpose_gates()
                if not is_item(m, NE - 1):
                    gather(m + 2)
                down(m)

            main_item(FIRST)
            main_item(SECOND)
            with pe.Fori(2, NE - 1) as n:
                main_item(n)
            main_item(NE - 1)
            scatter(NE - 1, last=True)
            over = pe.value_load(tab[0:1, 2 * MAXOVER:2 * MAXOVER + 1], min_val=0, max_val=MAXOVER - 1)
            with pe.If(over > 0):
                with pe.Fori(0, over) as i:
                    gather(i + NE + 2)
                    gate_up(i + NE, i + NE + 1)
                    transpose_gates()
                    down(i + NE)
                    scatter(i + NE, last=True, again=True)


_INS = ['x', 'norm_mix_w', 'w_in', 'conv_w', 'conv_b', 'dt_bias', 'a_log', 'd_skip', 'ssm_norm_w', 'lstm_i_bias',
        'lstm_f_bias', 'lstm_norm_w', 'w_out', 'norm_ffn_w', 'w_router', 'b_router', 'w_gate_up', 'b_gate_up',
        'w_down', 'b_down', 'norm_final_w']


def kernel(**inputs):
    import numpy as _np
    import concourse.bacc as _bacc
    from concourse import mybir as _mybir
    from concourse.bass_utils import run_bass_kernel_spmd as _run

    nc = _bacc.Bacc("TRN2", target_bir_lowering=False, num_devices=1)
    arrays, args = {}, []
    for name in _INS:
        a = _np.ascontiguousarray(inputs[name])
        arrays[f"in_{name}_dram"] = a
        args.append(nc.dram_tensor(f"in_{name}_dram", a.shape, _mybir.dt.from_np(a.dtype), kind="ExternalInput").ap())
    args.append(nc.dram_tensor("out_0_dram", (1, T, D), _mybir.dt.float32, kind="ExternalOutput").ap())
    hybrid_block(nc, *args)
    r = _run(nc, [arrays], core_ids=[0])
    return r.results[0]["out_0_dram"]
```
